# Optimizing a Trainium2 kernel written in Bass

```python
import math
import jax, jax.numpy as jnp
from jax import lax
import numpy as np

D_MODEL = 2048
BATCH = 1
SEQ = 256
DEPTH = 1

HEAD_DIM = 128
N_HEADS = D_MODEL // HEAD_DIM
MIX_W = N_HEADS * HEAD_DIM
A_HEADS = 3 * N_HEADS // 8
C_HEADS = N_HEADS // 4
B_HEADS = N_HEADS - A_HEADS - C_HEADS
A_W = A_HEADS * HEAD_DIM
B_W = B_HEADS * HEAD_DIM
C_W = C_HEADS * HEAD_DIM
DIL_PATTERNS = ((128, 1), (512, 4), (2048, 16))
BAND_BLK = 128
NSA_KV = 2
NSA_GROUP = B_HEADS // NSA_KV
KV_W = NSA_KV * HEAD_DIM
CMP_LEN = 32
CMP_STRIDE = 16
SLC_LEN = 64
SLC_TOPN = 8
NSA_WINDOW = 512
FORCE = 1e4
MOBA_BLK = 256
MOBA_TOPK = 3
GATHER_QBLK = 16
REL_BUCKETS = 32
REL_MAX_DIST = 1024
PEER_HEADS = 8
PEER_NKEYS = 128
PEER_EXPERTS = PEER_NKEYS * PEER_NKEYS
PEER_DQ = 256
PEER_TOPK = 16
PEER_TOKBLK = 128
PLE_DIM = 256
EPS = 1e-6
PROJ_SPLITS = (A_W, A_W, A_W, B_W, KV_W, KV_W, KV_W, KV_W, KV_W, KV_W, 3 * B_HEADS, C_W, C_W, C_W)
PROJ_COLS = sum(PROJ_SPLITS)
PROJ_BOUNDS = tuple(int(c) for c in np.cumsum(PROJ_SPLITS)[:-1])

kernel_name = 'hybrid_dilated_nsa_moba_peer'

def rmsnorm(x, g):
    x32 = x.astype(jnp.float32)
    y = x32 * lax.rsqrt(jnp.mean(x32 * x32, axis=-1, keepdims=True) + EPS)
    return (y * g.astype(jnp.float32)).astype(x.dtype)

def rel_bucket(dist):
    exact = REL_BUCKETS // 2
    d = jnp.maximum(dist, 0)
    logd = jnp.log(jnp.maximum(d, 1).astype(jnp.float32) / exact)
    large = exact + (logd / math.log(REL_MAX_DIST / exact) * (REL_BUCKETS - exact)).astype(jnp.int32)
    large = jnp.clip(large, exact, REL_BUCKETS - 1)
    return jnp.where(d < exact, d, large)

def masked_softmax(s, mask):
    s = jnp.where(mask, s.astype(jnp.float32), -jnp.inf)
    m = jnp.max(s, axis=-1, keepdims=True)
    m = jnp.where(jnp.isfinite(m), m, 0.0)
    e = jnp.exp(s - m)
    z = jnp.sum(e, axis=-1, keepdims=True)
    zs = jnp.where(z > 0, z, 1.0)
    p = e / zs
    lse = jnp.where(z > 0, m + jnp.log(zs), -jnp.inf)
    return p, lse[..., 0]

def merge_partials(outs, lses):
    w = jax.nn.softmax(jnp.stack(lses, axis=0), axis=0)
    o = jnp.sum(w[..., None] * jnp.stack(outs, axis=0).astype(jnp.float32), axis=0)
    return o.astype(outs[0].dtype)

def banded_attention(q, k, v, n_back, dist_scale, bias_tab):
    n, l, h, hd = q.shape
    blk = BAND_BLK
    nb = l // blk
    npv = -(-n_back // blk)
    w = (npv + 1) * blk
    pad = ((0, 0), (npv * blk, 0), (0, 0), (0, 0))
    kb = jnp.pad(k, pad).reshape(n, nb + npv, blk, h, hd)
    vb = jnp.pad(v, pad).reshape(n, nb + npv, blk, h, hd)
    kwin = jnp.concatenate([kb[:, j:j + nb] for j in range(npv + 1)], axis=2)
    vwin = jnp.concatenate([vb[:, j:j + nb] for j in range(npv + 1)], axis=2)
    qb = q.reshape(n, nb, blk, h, hd)
    s = jnp.einsum('nbqhd,nbkhd->nbhqk', qb, kwin).astype(jnp.float32) * (hd ** -0.5)
    dist = jnp.arange(blk)[:, None] - jnp.arange(w)[None, :] + npv * blk
    bias = bias_tab[rel_bucket(dist * dist_scale)].astype(jnp.float32)
    s = s + jnp.transpose(bias, (2, 0, 1))
    kpos = jnp.arange(nb)[:, None] * blk + jnp.arange(w)[None, :] - npv * blk
    mask = ((dist >= 0) & (dist <= n_back))[None, :, :] & (kpos >= 0)[:, None, :]
    p, lse = masked_softmax(s, mask[None, :, None])
    o = jnp.einsum('nbhqk,nbkhd->nbqhd', p.astype(v.dtype), vwin)
    return o.reshape(n, l, h, hd), jnp.transpose(lse, (0, 1, 3, 2)).reshape(n, l, h)

def dilated_attention(q, k, v, bias_tab):
    b, s, h, hd = q.shape
    outs, lses = [], []
    for window, dil in DIL_PATTERNS:
        l = s // dil
        lp = -(-l // BAND_BLK) * BAND_BLK

        def to_res(t):
            t = t.reshape(b, l, dil, h, hd).transpose(0, 2, 1, 3, 4).reshape(b * dil, l, h, hd)
            return jnp.pad(t, ((0, 0), (0, lp - l), (0, 0), (0, 0)))

        o, lse = banded_attention(to_res(q), to_res(k), to_res(v), window // dil, dil, bias_tab)
        outs.append(o[:, :l].reshape(b, dil, l, h, hd).transpose(0, 2, 1, 3, 4).reshape(b, s, h, hd))
        lses.append(lse[:, :l].reshape(b, dil, l, h).transpose(0, 2, 1, 3).reshape(b, s, h))
    return merge_partials(outs, lses)

def nsa_attention(q, kc, vc, ks, vs, kw, vw, gates, cmp_wk, cmp_wv, cmp_pos, bias_tab):
    b, s, h, hd = q.shape
    f32 = jnp.float32
    scale = hd ** -0.5
    pos = jnp.arange(s)
    qg = q.reshape(b, s, NSA_KV, NSA_GROUP, hd)
    ncmp = (s - CMP_LEN) // CMP_STRIDE + 1
    cidx = jnp.arange(ncmp)[:, None] * CMP_STRIDE + jnp.arange(CMP_LEN)[None, :]
    k_cmp = jnp.einsum('bnlgd,lde->bnge', kc[:, cidx] + cmp_pos[:, None, :], cmp_wk)
    v_cmp = jnp.einsum('bnlgd,lde->bnge', vc[:, cidx] + cmp_pos[:, None, :], cmp_wv)
    s_c = jnp.einsum('bqgrd,bngd->bgrqn', qg, k_cmp).astype(f32) * scale
    cend = jnp.arange(ncmp) * CMP_STRIDE + CMP_LEN - 1
    dist_c = pos[:, None] - cend[None, :]
    bias_c = bias_tab[rel_bucket(dist_c)].astype(f32).reshape(s, ncmp, NSA_KV, NSA_GROUP)
    s_c = s_c + bias_c.transpose(2, 3, 0, 1)
    p_c, _ = masked_softmax(s_c, dist_c >= 0)
    o_cmp = jnp.einsum('bgrqn,bngd->bqgrd', p_c.astype(vc.dtype), v_cmp).reshape(b, s, h, hd)
    nslc = s // SLC_LEN
    cstart = jnp.arange(ncmp) * CMP_STRIDE
    sstart = jnp.arange(nslc) * SLC_LEN
    cover = ((cstart[:, None] < sstart[None, :] + SLC_LEN)
             & (cstart[:, None] + CMP_LEN > sstart[None, :])).astype(f32)
    imp = jnp.einsum('bgrqn,nj->bgqj', p_c, cover)
    qblk = pos // SLC_LEN
    jb = jnp.arange(nslc)
    forced = (jb[None, :] == 0) | (jb[None, :] == qblk[:, None]) | (jb[None, :] == qblk[:, None] - 1)
    future = jb[None, :] > qblk[:, None]
    imp = jnp.where(forced, FORCE, jnp.where(future, -FORCE, imp))
    topn = min(SLC_TOPN, nslc)
    _, sel = lax.top_k(imp, topn)
    ksb = ks.transpose(0, 2, 1, 3).reshape(b, NSA_KV, nslc, SLC_LEN * hd)
    vsb = vs.transpose(0, 2, 1, 3).reshape(b, NSA_KV, nslc, SLC_LEN * hd)
    nq = s // GATHER_QBLK
    q_ch = qg.reshape(b, nq, GATHER_QBLK, NSA_KV, NSA_GROUP, hd).transpose(1, 0, 2, 3, 4, 5)
    sel_ch = sel.reshape(b, NSA_KV, nq, GATHER_QBLK, topn).transpose(2, 0, 1, 3, 4)
    tab = bias_tab.reshape(REL_BUCKETS, NSA_KV, NSA_GROUP)
    bi = jnp.arange(b)[:, None, None]
    gi = jnp.arange(NSA_KV)[None, :, None]
    kk_len = topn * SLC_LEN

    def sel_block(args):
        ci, qc, ic = args
        flat = ic.reshape(b, NSA_KV, GATHER_QBLK * topn)
        kk = ksb[bi, gi, flat].reshape(b, NSA_KV, GATHER_QBLK, kk_len, hd)
        vv = vsb[bi, gi, flat].reshape(b, NSA_KV, GATHER_QBLK, kk_len, hd)
        sc = jnp.einsum('bqgrd,bgqkd->bgrqk', qc, kk).astype(f32) * scale
        qpos = ci * GATHER_QBLK + jnp.arange(GATHER_QBLK)
        kpos = (ic[..., None] * SLC_LEN + jnp.arange(SLC_LEN)).reshape(b, NSA_KV, GATHER_QBLK, kk_len)
        dist = qpos[None, None, :, None] - kpos
        bias = tab[rel_bucket(dist), jnp.arange(NSA_KV)[None, :, None, None]].astype(f32)
        sc = sc + jnp.moveaxis(bias, -1, 2)
        p, _ = masked_softmax(sc, (dist >= 0)[:, :, None])
        return jnp.einsum('bgrqk,bgqkd->bqgrd', p.astype(vv.dtype), vv)

    o_sel = lax.map(sel_block, (jnp.arange(nq), q_ch, sel_ch))
    o_sel = o_sel.transpose(1, 0, 2, 3, 4, 5).reshape(b, s, h, hd)
    o_win, _ = banded_attention(q, jnp.repeat(kw, NSA_GROUP, axis=2), jnp.repeat(vw, NSA_GROUP, axis=2),
                                NSA_WINDOW - 1, 1, bias_tab)
    return gates[..., 0:1] * o_cmp + gates[..., 1:2] * o_sel + gates[..., 2:3] * o_win

def moba_attention(q, k, v, bias_tab):
    b, s, h, hd = q.shape
    f32 = jnp.float32
    scale = hd ** -0.5
    sp = -(-s // MOBA_BLK) * MOBA_BLK
    pad = ((0, 0), (0, sp - s), (0, 0), (0, 0))
    q, k, v = jnp.pad(q, pad), jnp.pad(k, pad), jnp.pad(v, pad)
    nblk = sp // MOBA_BLK
    qb = q.reshape(b, nblk, MOBA_BLK, h, hd)
    kb = k.reshape(b, nblk, MOBA_BLK, h, hd)
    vb = v.reshape(b, nblk, MOBA_BLK, h, hd)
    s_o = jnp.einsum('bnqhd,bnkhd->bnhqk', qb, kb).astype(f32) * scale
    dist_o = jnp.arange(MOBA_BLK)[:, None] - jnp.arange(MOBA_BLK)[None, :]
    s_o = s_o + jnp.transpose(bias_tab[rel_bucket(dist_o)].astype(f32), (2, 0, 1))
    p_o, lse_o = masked_softmax(s_o, dist_o >= 0)
    o_own = jnp.einsum('bnhqk,bnkhd->bnqhd', p_o.astype(v.dtype), vb).reshape(b, sp, h, hd)
    lse_own = jnp.transpose(lse_o, (0, 1, 3, 2)).reshape(b, sp, h)
    ntop = min(MOBA_TOPK, nblk - 1)
    if ntop == 0:
        return o_own[:, :s]
    kmean = jnp.mean(kb.astype(f32), axis=2)
    gate = jnp.einsum('bshd,bnhd->bhsn', q.astype(f32), kmean)
    qblk_all = jnp.arange(sp) // MOBA_BLK
    past = jnp.arange(nblk)[None, :] < qblk_all[:, None]
    gate = jnp.where(past, gate, -jnp.inf)
    _, sel = lax.top_k(gate, ntop)
    kbf = kb.transpose(0, 3, 1, 2, 4).reshape(b, h, nblk, MOBA_BLK * hd)
    vbf = vb.transpose(0, 3, 1, 2, 4).reshape(b, h, nblk, MOBA_BLK * hd)
    nq = sp // GATHER_QBLK
    q_ch = q.reshape(b, nq, GATHER_QBLK, h, hd).transpose(1, 0, 2, 3, 4)
    sel_ch = sel.reshape(b, h, nq, GATHER_QBLK, ntop).transpose(2, 0, 1, 3, 4)
    bi = jnp.arange(b)[:, None, None]
    hi = jnp.arange(h)[None, :, None]
    kk_len = ntop * MOBA_BLK

    def blk_fn(args):
        ci, qc, ic = args
        flat = ic.reshape(b, h, GATHER_QBLK * ntop)
        kk = kbf[bi, hi, flat].reshape(b, h, GATHER_QBLK, kk_len, hd)
        vv = vbf[bi, hi, flat].reshape(b, h, GATHER_QBLK, kk_len, hd)
        sc = jnp.einsum('bqhd,bhqkd->bhqk', qc, kk).astype(f32) * scale
        qpos = ci * GATHER_QBLK + jnp.arange(GATHER_QBLK)
        kpos = (ic[..., None] * MOBA_BLK + jnp.arange(MOBA_BLK)).reshape(b, h, GATHER_QBLK, kk_len)
        dist = qpos[None, None, :, None] - kpos
        sc = sc + bias_tab[rel_bucket(dist), jnp.arange(h)[None, :, None, None]].astype(f32)
        valid = ic < (qpos // MOBA_BLK)[None, None, :, None]
        p, lse = masked_softmax(sc, jnp.repeat(valid, MOBA_BLK, axis=-1))
        o = jnp.einsum('bhqk,bhqkd->bqhd', p.astype(vv.dtype), vv)
        return o, jnp.transpose(lse, (0, 2, 1))

    o_g, lse_g = lax.map(blk_fn, (jnp.arange(nq), q_ch, sel_ch))
    o_g = o_g.transpose(1, 0, 2, 3, 4).reshape(b, sp, h, hd)
    lse_g = lse_g.transpose(1, 0, 2, 3).reshape(b, sp, h)
    return merge_partials([o_own, o_g], [lse_own, lse_g])[:, :s]

def hybrid_mixer(a, w_in, cmp_wk, cmp_wv, cmp_pos, out_norm, w_out, rel_bias):
    b, s, _ = a.shape
    (qa, ka, va, qb, kc, vc, ks, vs, kw, vw, gt, qc, kc_c, vc_c) = jnp.split(a @ w_in, PROJ_BOUNDS, axis=-1)

    def hs(t):
        return t.reshape(b, s, -1, HEAD_DIM)

    tab_a = rel_bias[:, :A_HEADS]
    tab_b = rel_bias[:, A_HEADS:A_HEADS + B_HEADS]
    tab_c = rel_bias[:, A_HEADS + B_HEADS:]
    oa = dilated_attention(hs(qa), hs(ka), hs(va), tab_a)
    gates = jax.nn.sigmoid(gt.astype(jnp.float32)).astype(a.dtype).reshape(b, s, B_HEADS, 3)
    ob = nsa_attention(hs(qb), hs(kc), hs(vc), hs(ks), hs(vs), hs(kw), hs(vw), gates,
                       cmp_wk, cmp_wv, cmp_pos, tab_b)
    oc = moba_attention(hs(qc), hs(kc_c), hs(vc_c), tab_c)
    g_a, g_b, g_c = jnp.split(out_norm, [A_W, A_W + B_W])
    y = jnp.concatenate([rmsnorm(oa.reshape(b, s, A_W), g_a),
                         rmsnorm(ob.reshape(b, s, B_W), g_b),
                         rmsnorm(oc.reshape(b, s, C_W), g_c)], axis=-1)
    return y @ w_out

def peer_ffn(x, wq, subkeys, u, v):
    b, s, d = x.shape
    q = (x @ wq).reshape(b, s, PEER_HEADS, 2, PEER_DQ // 2)
    sc = jnp.einsum('bshcd,hckd->bshck', q, subkeys).astype(jnp.float32)
    top_s, top_i = lax.top_k(sc, PEER_TOPK)
    cand = top_s[..., 0, :, None] + top_s[..., 1, None, :]
    cand_i = top_i[..., 0, :, None] * PEER_NKEYS + top_i[..., 1, None, :]
    best_s, best_j = lax.top_k(cand.reshape(b, s, PEER_HEADS, PEER_TOPK * PEER_TOPK), PEER_TOPK)
    expert = jnp.take_along_axis(cand_i.reshape(b, s, PEER_HEADS, PEER_TOPK * PEER_TOPK), best_j, axis=-1)
    g = jax.nn.softmax(best_s, axis=-1)
    nt = (b * s) // PEER_TOKBLK
    hk = PEER_HEADS * PEER_TOPK
    xs = x.reshape(nt, PEER_TOKBLK, d)
    es = expert.reshape(nt, PEER_TOKBLK, hk)
    gs = g.reshape(nt, PEER_TOKBLK, hk).astype(x.dtype)

    def tok_fn(args):
        xc, ec, gc = args
        act = jax.nn.gelu(jnp.einsum('td,tkd->tk', xc, u[ec]), approximate=False)
        return jnp.einsum('tk,tkd->td', gc * act, v[ec])

    return lax.map(tok_fn, (xs, es, gs)).reshape(b, s, d)

def setup_inputs(seed: int = 0) -> dict:
    key = jax.random.key(seed)
    k = jax.random.split(key, 20)
    f32 = jnp.float32

    def nrm(kk, shape, scale):
        return jax.random.normal(kk, shape, f32) * scale

    return {
        'x': nrm(k[0], (BATCH, SEQ, D_MODEL), 1.0),
        'p': nrm(k[1], (DEPTH, BATCH, SEQ, PLE_DIM), 1.0),
        'ln_mix': 1.0 + nrm(k[2], (DEPTH, D_MODEL), 0.02),
        'w_in': nrm(k[3], (DEPTH, D_MODEL, PROJ_COLS), D_MODEL ** -0.5),
        'cmp_wk': nrm(k[4], (DEPTH, CMP_LEN, HEAD_DIM, HEAD_DIM), (CMP_LEN * HEAD_DIM) ** -0.5),
        'cmp_wv': nrm(k[5], (DEPTH, CMP_LEN, HEAD_DIM, HEAD_DIM), (CMP_LEN * HEAD_DIM) ** -0.5),
        'cmp_pos': nrm(k[6], (DEPTH, CMP_LEN, HEAD_DIM), 0.1),
        'out_norm': 1.0 + nrm(k[7], (DEPTH, MIX_W), 0.02),
        'w_out': nrm(k[8], (DEPTH, MIX_W, D_MODEL), MIX_W ** -0.5),
        'rel_bias': nrm(k[9], (REL_BUCKETS, N_HEADS), 0.5),
        'ln_ffn': 1.0 + nrm(k[10], (DEPTH, D_MODEL), 0.02),
        'peer_wq': nrm(k[11], (DEPTH, D_MODEL, PEER_HEADS * PEER_DQ), D_MODEL ** -0.5),
        'peer_keys': nrm(k[12], (DEPTH, PEER_HEADS, 2, PEER_NKEYS, PEER_DQ // 2), (PEER_DQ // 2) ** -0.5),
        'peer_u': nrm(k[13], (DEPTH, PEER_EXPERTS, D_MODEL), D_MODEL ** -0.5),
        'peer_v': nrm(k[14], (DEPTH, PEER_EXPERTS, D_MODEL), PEER_HEADS ** -0.5),
        'ln_ple': 1.0 + nrm(k[15], (DEPTH, D_MODEL), 0.02),
        'ple_gate': nrm(k[16], (DEPTH, D_MODEL, D_MODEL), D_MODEL ** -0.5),
        'ple_proj': nrm(k[17], (DEPTH, PLE_DIM, D_MODEL), PLE_DIM ** -0.5),
        'ln_final': 1.0 + nrm(k[18], (D_MODEL,), 0.02),
    }

def reference(x, p, ln_mix, w_in, cmp_wk, cmp_wv, cmp_pos, out_norm, w_out, rel_bias, ln_ffn,
              peer_wq, peer_keys, peer_u, peer_v, ln_ple, ple_gate, ple_proj, ln_final):
    h = x
    for i in range(DEPTH):
        h = h + hybrid_mixer(rmsnorm(h, ln_mix[i]), w_in[i], cmp_wk[i], cmp_wv[i], cmp_pos[i],
                             out_norm[i], w_out[i], rel_bias)
        h = h + peer_ffn(rmsnorm(h, ln_ffn[i]), peer_wq[i], peer_keys[i], peer_u[i], peer_v[i])
        gate = jax.nn.sigmoid((rmsnorm(h, ln_ple[i]) @ ple_gate[i]).astype(jnp.float32)).astype(h.dtype)
        h = h + gate * (p[i] @ ple_proj[i])
    return rmsnorm(h, ln_final)


_drawn_inputs = setup_inputs


def setup_inputs(seed=0):
    import zlib

    import numpy as np

    out = dict(_drawn_inputs(seed))
    spreads = {}
    factors = {'out_norm': 2.83, 'ln_ffn': 8.617, 'ln_ple': 64.0, 'ln_final': 8.126}
    for name, (base, spread) in spreads.items():
        noise = np.random.default_rng([zlib.crc32(name.encode()), seed]).standard_normal(out[name].shape)
        drawn = base * np.exp(spread * noise) if base else spread * noise
        out[name] = __import__('jax').numpy.asarray(drawn.astype(out[name].dtype))
    for name, factor in factors.items():
        out[name] = (out[name] * factor).astype(out[name].dtype)
    return out
```

```python
import math

import numpy as np

import concourse.bass as bass
from concourse import mybir

SEQ, D, HD = 256, 2048, 128
P = 128
TT = SEQ // P
KT = D // P
A_H, B_H, C_H, KV = 6, 6, 4, 2
NH = A_H + B_H + C_H
GROUP = B_H // KV
GATES = 3 * B_H
CMP_LEN, CMP_STRIDE = 32, 16
NCMP = (SEQ - CMP_LEN) // CMP_STRIDE + 1
NCMP0 = (P - CMP_LEN) // CMP_STRIDE + 1
PEER_H, NKEYS, TOPK = 8, 128, 16
PLE = 256
BUCKETS, MAX_DIST = 32, 1024
EPS = 1e-6
SCALE = HD ** -0.5
NEG = -1e30
TAKEN = -3e38

QA, KA, VA = 0, A_H, 2 * A_H
QB = 3 * A_H
KC, VC = QB + B_H, QB + B_H + KV
KS, VS, KW, VW = VC + KV, VC + 2 * KV, VC + 3 * KV, VC + 4 * KV
QC = VW + KV
KCC, VCC = QC + C_H, QC + 2 * C_H
UNITS = VCC + C_H
GATE_COL = QC * P
V_UNITS = [*range(VA, VA + A_H), *range(VS, VS + KV), *range(VW, VW + KV), *range(VCC, VCC + C_H)]

CHUNK_K, CHUNK_C = 8, 256
RING = 4
GRING = 8
RLEN = 384


def bias_table():
    dist = 255 - np.arange(RLEN)
    d = np.maximum(dist, 0)
    exact = BUCKETS // 2
    logd = np.log(np.maximum(d, 1).astype(np.float32) / np.float32(exact))
    large = exact + (logd / np.float32(math.log(MAX_DIST / exact)) * np.float32(BUCKETS - exact)).astype(np.int32)
    bucket = np.where(d < exact, d, np.clip(large, exact, BUCKETS - 1))
    out = np.zeros((BUCKETS + 2, NH + RLEN), np.float32)
    out[BUCKETS, :A_H] = 1.0
    out[BUCKETS + 1, A_H:NH] = 1.0
    out[bucket, NH + np.arange(RLEN)] = 1.0
    count = (dist <= 128).astype(int) + (dist % 4 == 0) + (dist % 16 == 0)
    dilated = np.where((dist >= 0) & (count > 0), np.log(np.maximum(count, 1)), NEG)
    out[BUCKETS, NH:] = dilated
    out[BUCKETS + 1, NH:] = np.where(dist >= 0, 0.0, NEG)
    return out


def calls():
    out = []
    for h in range(A_H):
        out.append((QA + h, KA + h, VA + h, h, h, "full", None, True, True))
    for h in range(C_H):
        out.append((QC + h, KCC + h, VCC + h, A_H + B_H + h, A_H + B_H + h, "full", None, True, True))
    for h in range(B_H):
        g = h // GROUP
        out.append((QB + h, KS + g, VS + g, A_H + h, A_H + h, "full", 3 * h + 1, True, False))
        out.append((QB + h, KW + g, VW + g, A_H + h, A_H + h, "full", 3 * h + 2, False, False))
        out.append((QB + h, g, g, A_H + h, A_H + h, "cmp", 3 * h, False, True))
    return out


class Steps:

    def __init__(self, eng, sem):
        self.eng, self.sem, self.n, self.base = eng, sem, 0, 0

    def did(self, ins):
        ins.then_inc(self.sem, 1)
        self.n += 1

    def wait(self):
        self.eng.wait_ge(self.sem, self.base + self.n)

    def wait_apart(self):
        self.wait()
        self.eng.nop(nofuse=True)

    def enter(self, turn, per_turn):
        self.before, self.per_turn = self.n, per_turn
        self.base, self.n = self.before + turn * per_turn, 0

    def leave(self, turns):
        assert self.n == self.per_turn, (self.n, self.per_turn)
        self.base, self.n = 0, self.before + turns * self.per_turn


def build(nc, x, p, ln_mix, w_in, cmp_wk, cmp_wv, cmp_pos, out_norm, w_out, rel_bias, ln_ffn, peer_wq,
          peer_keys, peer_u, peer_v, ln_ple, ple_gate, ple_proj, ln_final, table, out):
    fp32, f32r, i32, u32 = mybir.dt.float32, mybir.dt.float32r, mybir.dt.int32, mybir.dt.uint32
    ALU, ACT, AX = mybir.AluOpType, mybir.ActivationFunctionType, mybir.AxisListType

    base = -(-nc.sbuf_base // 64) * 64
    size = {fp32: 4, f32r: 4, i32: 4, u32: 4}

    def at(name, offset, shape, dt=fp32):
        return nc.alloc_sbuf_tensor_at(name, shape, dt, offset=base + offset)

    cursor = [0]

    def place(name, shape, dt=fp32):
        o = cursor[0]
        cursor[0] += -(-int(np.prod(shape[1:])) * size[dt] // 32) * 32
        return at(name, o, shape, dt)

    def mark():
        return cursor[0]

    KB = 1024
    hres = place("hres", [P, TT, D])
    o_xn = mark()
    xn = place("xn", [P, TT, D])
    gain = place("gain", [P, D])
    bias = at("bias", o_xn, [P, NH, RLEN])
    ident = place("ident", [P, P])
    ones = place("ones", [P, P])
    o_raw = mark()
    raw = [place(f"raw{r}", [P, CHUNK_K, CHUNK_C]) for r in range(RING)]
    o_split = mark()
    whi = [place(f"whi{b}", [P, CHUNK_K, CHUNK_C], f32r) for b in range(2)]
    wlo = [place(f"wlo{b}", [P, CHUNK_K, CHUNK_C], f32r) for b in range(2)]
    o_xt = mark()
    xthi = place("xthi", [P, KT, SEQ], f32r)
    xtlo = place("xtlo", [P, KT, SEQ], f32r)
    o_pr = mark()
    pr = place("pr", [P, UNITS, SEQ])

    ot = at("ot", o_split, [P, NH, SEQ])
    o_att = o_split + 16 * KB
    sc = [at(f"sc{b}", o_att + b * 1536, [P, RLEN]) for b in range(2)]
    pb = [at(f"pb{b}", o_att + 3072 + b * 1536, [P, RLEN]) for b in range(3)]
    pts = [at(f"pts{b}", o_att + 7680 + b * 1536, [P, RLEN]) for b in range(2)]
    diag = [at(f"diag{b}", o_att + 10752 + b * 1024, [P, TT, P]) for b in range(2)]
    wcmp = [at("wk_cmp", o_xt, [P, CMP_LEN, HD]), at("wv_cmp", o_xt + 16 * KB, [P, CMP_LEN, HD])]
    osq = at("osq", o_pr, [P, NH, SEQ])
    orms = at("orms", o_pr + 16 * KB, [P, 3, SEQ])
    ysc = at("ysc", o_pr + 20 * KB, [P, NH, SEQ])
    qt = at("qt", o_pr, [P, 2 * PEER_H, SEQ])
    scores = at("scores", o_pr + 16 * KB, [P, TT * PEER_H, 2, NKEYS])
    keys = at("keys", o_pr + 32 * KB, [P, 2 * PEER_H, HD])
    keyst = at("keyst", o_pr + 40 * KB, [P, 2 * PEER_H, NKEYS])
    rows = [at(f"rows{r}", o_split + r * 8 * KB, [P, D]) for r in range(GRING)]
    pproj = at("pproj", o_pr + 32 * KB, [P, PLE // P, D])
    pp = at("pp", o_pr, [P, TT, D])
    sig = [at(f"sig{b}", o_pr + 16 * KB + b * 2 * KB, [P, TT * CHUNK_C]) for b in range(2)]

    o_xcmp = mark()
    xcmp = place("xcmp", [P, 2, CMP_LEN, KV, NCMP])
    kct = place("kct", [P, KV, NCMP])
    vcm = place("vcm", [P, KV, HD])
    wg = place("wg", [P, KT, GATES])
    wghi = place("wghi", [P, KT, GATES], f32r)
    wglo = place("wglo", [P, KT, GATES], f32r)
    gates = place("gates", [P, TT, GATES])
    ptile = place("ptile", [P, TT, PLE])
    ptt = place("ptt", [P, PLE // P, SEQ])
    posn = place("posn", [CMP_LEN, HD])
    post = place("post", [P, CMP_LEN])
    ongn = place("ongn", [NH, HD])
    ongt = place("ongt", [P, NH])
    tabl = place("tabl", [BUCKETS + 2, NH + RLEN])
    rvec = place("rvec", [NH, RLEN])
    valid = place("valid", [P, 1])
    ssq = place("ssq", [P, TT])
    rstd = place("rstd", [P, TT])
    negmax = [place(f"negmax{b}", [P, TT]) for b in range(2)]
    zsum = [place(f"zsum{b}", [P, TT]) for b in range(2)]
    rz = [place(f"rz{b}", [P, TT]) for b in range(2)]
    s1 = at("s1", o_xcmp + 0 * KB, [P, 2, NKEYS])
    s2 = at("s2", o_xcmp + 1 * KB, [P, 2, NKEYS])
    top = place("top", [P, 2, TOPK])
    topi = place("topi", [P, 2, TOPK], u32)
    topf = place("topf", [P, 2, TOPK])
    cand = at("cand", o_xcmp + 2 * KB, [P, TOPK, TOPK])
    cand2 = at("cand2", o_xcmp + 3 * KB, [P, TOPK, TOPK])
    best = place("best", [P, TOPK])
    bestj = place("bestj", [P, TOPK], u32)
    bidx = place("bidx", [P, 2, TOPK], u32)
    pick = at("pick", o_xcmp + 4 * KB, [P, TOPK, TOPK])
    pair = place("pair", [P, 2, TOPK])
    iota = place("iota", [P, TOPK])
    nbest = place("nbest", [P, 1])
    expert = [place(f"expert{b}", [P, TOPK], i32) for b in range(2)]
    gsum = [place(f"gsum{b}", [P, 1]) for b in range(2)]
    gexp = [place(f"gexp{b}", [P, TOPK]) for b in range(2)]
    dots = [place(f"dots{b}", [P, TOPK]) for b in range(2)]
    gel = [place(f"gel{b}", [P, TOPK]) for b in range(2)]
    coef = [place(f"coef{b}", [P, TOPK]) for b in range(2)]
    assert base + cursor[0] <= nc.sbuf_usable_end, (base + cursor[0], nc.sbuf_usable_end)

    bank = [nc.alloc_psum_tensor(f"bank{b}", [P, 512], fp32) for b in range(8)]
    rdram = nc.dram_tensor("bias_by_distance", (NH, P, RLEN), fp32, kind="Internal").ap()

    def sem(name):
        return nc.alloc_semaphore(name)

    dve_step, pool_step = sem("dve_step"), sem("pool_step")
    const_ready = sem("const_ready")
    x_in, small_in, keys_in = sem("x_in"), sem("small_in"), sem("keys_in")
    wg_in, wcmp_in, pproj_in = sem("wg_in"), sem("wcmp_in"), sem("pproj_in")
    gain_in = sem("gain_in")
    norms = ["mix", "ffn", "ple", "fin"]
    norm_sq = {n: sem(f"{n}_squared") for n in norms}
    norm_root = {n: sem(f"{n}_root") for n in norms}
    norm_done = {n: sem(f"{n}_normed") for n in norms}
    tr_done = {n: sem(f"{n}_transposed") for n in norms[:3]}
    tr_hi = {n: sem(f"{n}_xthi") for n in norms[:3]}
    tr_lo = {n: sem(f"{n}_xtlo") for n in norms[:3]}
    stages = ["in", "out", "wq", "gate"]
    landed = {s: [sem(f"{s}_landed{r}") for r in range(RING)] for s in stages}
    hi_ready = {s: sem(f"{s}_whi") for s in stages}
    lo_ready = {s: sem(f"{s}_wlo") for s in stages}
    mm_done = {s: sem(f"{s}_products") for s in stages}
    evac = {s: sem(f"{s}_evacuated") for s in stages}
    NG = {"in": UNITS * P // CHUNK_C, "out": D // CHUNK_C, "wq": D // CHUNK_C, "gate": D // CHUNK_C}
    small_tr, small_sb = sem("small_transposed"), sem("small_copied")
    r_mm, r_sb, r_out, bias_in = sem("r_mm"), sem("r_sb"), sem("r_out"), sem("bias_in")
    gate_hi, gate_lo, gate_mm, gate_sig = sem("gate_hi"), sem("gate_lo"), sem("gate_mm"), sem("gate_sig")
    xcmp_ready, cmp_mm, cmp_sb = sem("xcmp_ready"), sem("cmp_mm"), sem("cmp_sb")
    vt_mm, vt_sb = sem("vt_mm"), sem("vt_sb")
    s_score, s_biased, s_prob, s_diag = sem("scores_ready"), sem("biased"), sem("probs"), sem("diag_ready")
    s_pt, s_pts, s_pv, s_ot = sem("probs_transposed"), sem("probs_t_copied"), sem("pv_done"), sem("head_out")
    g_sq, g_sum, g_root, g_rstd = sem("group_squares"), sem("group_sums"), sem("group_root"), sem("group_rstd")
    y_ready, y_hi, y_lo = sem("y_ready"), sem("y_hi"), sem("y_lo")
    kt_mm, kt_sb, sc_mm, sc_sb = sem("keys_transposed"), sem("keys_copied"), sem("key_scores"), sem("key_scores_copied")
    routed, gate_exp = sem("experts_chosen"), sem("gate_exp")
    fetched = [sem(f"rows_fetched{r}") for r in range(GRING)]
    eaten = sem("rows_used")
    dots_ready, gelu_ready, peer_done = sem("dots_ready"), sem("gelu_ready"), sem("peer_done")
    pt2_mm, pt2_sb, pp_mm, pp_sb = sem("p_transposed"), sem("p_copied"), sem("pp_mm"), sem("pp_sb")
    ple_added, out_sem = sem("ple_added"), sem("out_written")

    CALLS = calls()
    NC_ = len(CALLS)
    HEAD_ORD = {}
    for c, call in enumerate(CALLS):
        if call[7]:
            HEAD_ORD[call[4]] = len(HEAD_ORD)
    LAST = {c: call[4] for c, call in enumerate(CALLS) if call[8]}
    GROUPS = [(0, A_H), (A_H, A_H + B_H), (A_H + B_H, NH)]
    PEER_STEPS = TT * PEER_H
    PAIRS = PEER_STEPS // 2
    GET = 2 * TOPK

    def weights_of(stage):
        return {"in": w_in, "out": w_out, "wq": peer_wq, "gate": ple_gate}[stage]

    block = nc.Block()
    with block:
        @block.sync
        def _(sp):
            for tt in range(TT):
                sp.dma_start(hres[:, tt, :], x[0, tt * P:(tt + 1) * P, :]).then_inc(x_in, 16)
            sp.dma_start(gain[:, :], ln_mix[0:1, :].partition_broadcast(P)).then_inc(gain_in, 16)

            def stream(stage, ngroups, first_group, gap):
                w = weights_of(stage)
                cols = ngroups * CHUNK_C
                c0 = first_group * CHUNK_C + gap
                view = w[0, :, c0:c0 + cols].rearrange("(h k q) c -> q h k c", q=P, k=CHUNK_K)

                def turn(i, peeled):
                    for r in range(RING):
                        if not peeled:
                            sp.wait_ge(lo_ready[stage], (first_group // 2 + i) * RING + r - RING + 1)
                        col = (2 * i + r // 2) * CHUNK_C
                        sp.dma_start(raw[r][:, :, :], view[:, r % 2, :, bass.ds(col, CHUNK_C)])\
                            .then_inc(landed[stage][r], 16)

                start = 0
                if first_group == 0:
                    turn(0, True)
                    start = 1
                with sp.Fori(start, ngroups // 2) as i:
                    turn(i, False)

            stream("in", QC // 2, 0, 0)
            sp.dma_start(wg[:, :, :], w_in[0, :, GATE_COL:GATE_COL + GATES].rearrange("(k q) c -> q k c", q=P))\
                .then_inc(wg_in, 16)
            stream("in", (UNITS - QC) // 2, QC // 2, GATES)
            sp.wait_ge(mm_done["in"], 2 * NG["in"])
            sp.wait_ge(gate_mm, 1)
            for w, sb in ((cmp_wk, wcmp[0]), (cmp_wv, wcmp[1])):
                sp.dma_start(sb[:, :, :], w[0].rearrange("l d e -> d l e")).then_inc(wcmp_in, 16)
            sp.wait_ge(lo_ready["in"], 2 * NG["in"])
            stream("out", NG["out"], 0, 0)
            sp.wait_ge(s_biased, 2 * NC_)
            sp.dma_start(gain[:, :], ln_ffn[0:1, :].partition_broadcast(P)).then_inc(gain_in, 16)
            sp.wait_ge(y_lo, 3)
            sp.dma_start(keys[:, :, :], peer_keys[0].rearrange("h c k d -> k (h c) d")).then_inc(keys_in, 16)
            sp.wait_ge(lo_ready["out"], 2 * NG["out"])
            stream("wq", NG["wq"], 0, 0)
            sp.wait_ge(norm_done["ffn"], TT)
            sp.dma_start(gain[:, :], ln_ple[0:1, :].partition_broadcast(P)).then_inc(gain_in, 16)
            sp.wait_ge(sc_mm, PEER_STEPS // 2)
            sp.dma_start(pproj[:, :, :], ple_proj[0].rearrange("(k q) c -> q k c", q=P)).then_inc(pproj_in, 16)
            sp.wait_ge(lo_ready["wq"], 2 * NG["wq"])
            stream("gate", NG["gate"], 0, 0)
            sp.wait_ge(norm_done["ple"], TT)
            sp.dma_start(gain[:, :], ln_final[None, :].partition_broadcast(P)).then_inc(gain_in, 16)
            for tt in range(TT):
                sp.wait_ge(norm_done["fin"], tt + 1)
                sp.dma_start(out[0, tt * P:(tt + 1) * P, :], xn[:, tt, :]).then_inc(out_sem, 16)
            sp.wait_ge(out_sem, 16 * TT)

        @block.gpsimd
        def _(pool):
            pool.memset(ident[:, :], 0.0).then_inc(pool_step, 1)
            pool.memset(valid[:, :], 1.0).then_inc(pool_step, 1)
            pool.memset(ones[:, :], 1.0).then_inc(const_ready, 1)
            pool.iota(iota[:, :], [[1, TOPK]], base=0, channel_multiplier=0,
                      allow_small_or_imprecise_dtypes=True).then_inc(const_ready, 1)
            pool.wait_ge(pool_step, 2)
            pool.affine_select(out=ident[:, :], in_=ident[:, :], compare_op=ALU.not_equal, fill=1.0, base=0,
                               pattern=[[-1, P]], channel_multiplier=1).then_inc(const_ready, 1)
            pool.affine_select(out=valid[:, :], in_=valid[:, :], compare_op=ALU.is_ge, fill=0.0,
                               base=-(CMP_LEN - 1), pattern=[[0, 1]], channel_multiplier=1).then_inc(const_ready, 1)
            pool.dma_start(tabl[:, NH:], table[:, NH:]).then_inc(small_in, 16)
            pool.dma_start(tabl[BUCKETS:, 0:NH], table[BUCKETS:, 0:NH]).then_inc(small_in, 16)
            pool.dma_start(tabl[0:BUCKETS, 0:NH], rel_bias).then_inc(small_in, 16)
            pool.dma_start(posn[:, :], cmp_pos[0]).then_inc(small_in, 16)
            pool.dma_start(ongn[:, :], out_norm[0].rearrange("(h d) -> h d", d=HD)).then_inc(small_in, 16)
            pool.dma_start(ptile[:, :, :], p[0, 0].rearrange("(t q) c -> q t c", q=P)).then_inc(small_in, 16)
            pool.wait_ge(r_sb, 1)
            pool.dma_start(rdram, rvec[:, None, :].broadcast_to([NH, P, RLEN])).then_inc(r_out, 16)
            pool.wait_ge(r_out, 16)
            pool.wait_ge(tr_lo["mix"], 8)
            pool.wait_ge(tr_hi["mix"], 8)
            shift, heads = [RLEN - 1, P], [P * RLEN, NH]
            tile1 = bass.AP(tensor=rdram.tensor, offset=P - 1, ap=[shift, heads, [1, SEQ]])
            tile0 = bass.AP(tensor=rdram.tensor, offset=SEQ - 1, ap=[shift, heads, [1, P]])
            pool.dma_start(bias[:, :, P:RLEN], tile1).then_inc(bias_in, 16)
            pool.dma_start(bias[:, :, 0:P], tile0).then_inc(bias_in, 16)

            pool.wait_ge(evac["in"], VC // 2 + 1)
            pool.wait_ge(small_sb, 2)
            for kv, unit in ((0, KC), (1, VC)):
                for g in range(KV):
                    a = pr[:, unit + g, :]
                    win = bass.AP(tensor=a.tensor, offset=a.offset, ap=[a.ap[0], [1, CMP_LEN], [CMP_STRIDE, NCMP]])
                    pool.tensor_tensor(xcmp[:, kv, :, g, :], win, post[:, :, None].broadcast_to([P, CMP_LEN, NCMP]),
                                       ALU.add).then_inc(xcmp_ready, 1)

            def fetch(pairs, peeled):
                for b in range(2):
                    pool.wait_ge(routed, pairs * 2 + b + 1)
                    for n in range(GET):
                        slot = n % GRING
                        if not (peeled and b == 0 and n < GRING):
                            pool.wait_ge(eaten, (pairs * 2 + b) * GET + n - GRING + 1)
                        pool.nop(nofuse=True)
                        src = peer_u if n < TOPK else peer_v
                        k = n % TOPK
                        pool.indirect_dma_start(rows[slot][:, :], None, src[0],
                                                bass.IndirectOffsetOnAxis(ap=expert[b][:, k:k + 1], axis=0))\
                            .then_inc(fetched[slot], 16)

            pool.wait_ge(mm_done["wq"], 2 * NG["wq"])
            fetch(0, True)
            with pool.Fori(1, PAIRS) as i:
                fetch(i, False)

        @block.scalar
        def _(act):
            def norm_sums(name):
                for tt in range(TT):
                    act.activation(xn[:, tt, :], hres[:, tt, :], ACT.Square, accum_out=ssq[:, tt:tt + 1])\
                        .then_inc(norm_sq[name], 1)
                act.wait_ge(norm_root[name], 1)
                act.activation(rstd[:, :], ssq[:, :], ACT.Sqrt).then_inc(norm_root[name], 1)

            def take_hi(name):
                for b in range(8):
                    tt, kb = b // 4, b % 4
                    act.wait_ge(tr_done[name], b + 1)
                    act.copy(xthi[:, 4 * kb:4 * kb + 4, tt * P:(tt + 1) * P],
                             bank[2 + b % 4][:, :].rearrange("p (a t) -> p a t", a=4)).then_inc(tr_hi[name], 1)

            def split_hi(stage, turn, r, peeled):
                act.wait_ge(landed[stage][r], 16 * (turn + 1))
                if not (peeled and r < 2):
                    act.wait_ge(mm_done[stage], RING * turn + r - 1)
                act.copy(whi[r % 2][:, :, :], raw[r][:, :, :]).then_inc(hi_ready[stage], 1)

            def run(stage, take):
                def turn(i, peeled):
                    split_hi(stage, i, 0, peeled)
                    if not peeled and take:
                        take(2 * i - 1, 1)
                    split_hi(stage, i, 1, peeled)
                    split_hi(stage, i, 2, peeled)
                    if take:
                        take(2 * i, 0)
                    split_hi(stage, i, 3, peeled)

                turns = NG[stage] // 2
                turn(0, True)
                with act.Fori(1, turns) as i:
                    turn(i, False)
                if take:
                    take(2 * turns - 1, 1)

            def copy_to(dst, stage):
                def take(group, parity):
                    act.wait_ge(mm_done[stage], 2 * group + 2)
                    act.copy(dst[:, bass.ds(2 * group, 2), :],
                             bank[parity][:, :].rearrange("p (u t) -> p u t", u=2)).then_inc(evac[stage], 1)
                return take

            act.wait_ge(x_in, 32)
            norm_sums("mix")
            take_hi("mix")
            run("in", copy_to(pr, "in"))

            act.wait_ge(wg_in, 16)
            act.copy(wghi[:, :, :], wg[:, :, :]).then_inc(gate_hi, 1)
            act.wait_ge(gate_mm, 1)
            act.activation(gates[:, :, :], bank[7][:, 0:TT * GATES].rearrange("p (t g) -> p t g", t=TT),
                           ACT.Sigmoid).then_inc(gate_sig, 1)
            for n in range(len(V_UNITS) // 2):
                act.wait_ge(vt_mm, n + 1)
                u = V_UNITS[2 * n]
                act.copy(pr[:, u:u + 2, :], bank[2 + n % 2][:, :].rearrange("p (u t) -> p u t", u=2))\
                    .then_inc(vt_sb, 1)

            def exps(c):
                w = RLEN if CALLS[c][5] == "full" else NCMP0 + NCMP
                w0 = P if CALLS[c][5] == "full" else NCMP0
                act.wait_ge(s_biased, 2 * c + 2)
                if c >= 3:
                    act.wait_ge(s_pt, c - 2)
                for tt, cols in ((0, slice(0, w0)), (1, slice(w0, w))):
                    act.activation(pb[c % 3][:, cols], sc[c % 2][:, cols], ACT.Exp, bias=negmax[c % 2][:, tt:tt + 1],
                                   accum_out=zsum[c % 2][:, tt:tt + 1]).then_inc(s_prob, 1)

            def copy_pt(c):
                act.wait_ge(s_pt, c + 1)
                if c >= 2:
                    act.wait_ge(s_pv, c - 1)
                rows_, w = (P, RLEN) if CALLS[c][5] == "full" else (NCMP, SEQ)
                act.copy(pts[c % 2][0:rows_, 0:w], bank[4 + c % 2][0:rows_, 0:w]).then_inc(s_pts, 1)

            def head_out(c):
                h = LAST[c]
                act.wait_ge(s_pv, c + 1)
                act.copy(ot[:, h, :], bank[6 + HEAD_ORD[h] % 2][:, 0:SEQ]).then_inc(s_ot, 1)

            for s in range(NC_ + 4):
                if s < NC_:
                    exps(s)
                if 0 <= s - 2 < NC_:
                    copy_pt(s - 2)
                if s - 4 in LAST:
                    head_out(s - 4)
            act.wait_ge(s_ot, NH)
            for n, (a, b) in enumerate(GROUPS):
                act.activation(osq[:, a:b, :], ot[:, a:b, :], ACT.Square).then_inc(g_sq, 1)
            act.wait_ge(g_root, 3)
            act.activation(orms[:, :, :], orms[:, :, :], ACT.Sqrt).then_inc(g_rstd, 1)
            for n, (a, b) in enumerate(GROUPS):
                act.wait_ge(y_ready, b)
                act.copy(xthi[:, a:b, :], ysc[:, a:b, :]).then_inc(y_hi, 1)
            run("out", None)
            act.wait_ge(evac["out"], NG["out"])
            norm_sums("ffn")
            take_hi("ffn")
            run("wq", copy_to(qt, "wq"))
            for n in range(4):
                act.wait_ge(kt_mm, n + 1)
                act.copy(keyst[:, 4 * n:4 * n + 4, :], bank[2 + n % 2][:, :].rearrange("p (a k) -> p a k", a=4))\
                    .then_inc(kt_sb, 1)
            for n in range(8):
                act.wait_ge(sc_mm, n + 1)
                act.copy(scores[:, 2 * n:2 * n + 2, :, :],
                         bank[4 + n % 2][:, :].rearrange("p (s c k) -> p s c k", s=2, c=2)).then_inc(sc_sb, 1)

            def route_exp(turn, b, peeled):
                s = 2 * turn + b
                act.wait_ge(routed, s + 1)
                act.activation(gexp[b][:, :], best[:, :], ACT.Exp, bias=nbest[:, :], accum_out=gsum[b][:, :])\
                    .then_inc(gate_exp, 1)

            def gelu(turn, b):
                act.wait_ge(dots_ready, 2 * turn + b + 1)
                act.activation(gel[b][:, :], dots[b][:, :], ACT.Gelu).then_inc(gelu_ready, 1)

            route_exp(0, 0, True)

            for k in range(PLE // P):
                act.wait_ge(pt2_mm, k + 1)
                act.copy(ptt[:, k, :], bank[6 + k][:, 0:SEQ]).then_inc(pt2_sb, 1)
            for n in range(8):
                act.wait_ge(pp_mm, n + 1)
                tt, cb = n // 4, n % 4
                act.copy(pp[:, tt, cb * 512:(cb + 1) * 512], bank[2 + n % 2][:, :]).then_inc(pp_sb, 1)

            def peer(i, last):
                gelu_first(i)
                if not last:
                    route_exp(i + 1, 0, False)
                gelu(i, 1)

            def gelu_first(i):
                route_exp(i, 1, False)
                gelu(i, 0)

            with act.Fori(0, PAIRS - 1) as i:
                peer(i, False)
            peer(PAIRS - 1, True)

            act.wait_ge(peer_done, TT)
            norm_sums("ple")
            take_hi("ple")

            def sigmoid_out(group, parity):
                act.wait_ge(mm_done["gate"], 2 * group + 2)
                if not (isinstance(group, int) and group == 0):
                    act.wait_ge(ple_added, group)
                act.activation(sig[parity][:, :], bank[parity][:, :], ACT.Sigmoid).then_inc(evac["gate"], 1)

            run("gate", sigmoid_out)
            act.wait_ge(ple_added, NG["gate"])
            norm_sums("fin")

        @block.vector
        def _(dve):
            st = Steps(dve, dve_step)

            def normed(name, turn):
                dve.wait_ge(norm_sq[name], TT)
                dve.tensor_scalar(ssq[:, :], ssq[:, :], 1.0 / D, EPS, ALU.mult, ALU.add)\
                    .then_inc(norm_root[name], 1)
                dve.wait_ge(norm_root[name], 2)
                st.did(dve.reciprocal(rstd[:, :], rstd[:, :]))
                dve.wait_ge(gain_in, 16 * (turn + 1))
                st.wait()
                for tt in range(TT):
                    dve.scalar_tensor_tensor(out=xn[:, tt, :], in0=hres[:, tt, :], scalar=rstd[:, tt:tt + 1],
                                             in1=gain[:, :], op0=ALU.mult, op1=ALU.mult).then_inc(norm_done[name], 1)

            def take_lo(name):
                for b in range(8):
                    tt, kb = b // 4, b % 4
                    dve.wait_ge(tr_hi[name], b + 1)
                    dst = (slice(None), slice(4 * kb, 4 * kb + 4), slice(tt * P, (tt + 1) * P))
                    dve.tensor_tensor(xtlo[dst], bank[2 + b % 4][:, :].rearrange("p (a t) -> p a t", a=4),
                                      xthi[dst].bitcast(fp32), ALU.subtract).then_inc(tr_lo[name], 1)

            def run(stage, take):
                def split_lo(i, r):
                    dve.wait_ge(hi_ready[stage], RING * i + r + 1)
                    dve.tensor_tensor(wlo[r % 2][:, :, :], raw[r][:, :, :], whi[r % 2][:, :, :].bitcast(fp32),
                                      ALU.subtract).then_inc(lo_ready[stage], 1)

                def turn(i, peeled):
                    split_lo(i, 0)
                    if not peeled and take:
                        take(2 * i - 1, 1)
                    split_lo(i, 1)
                    split_lo(i, 2)
                    if take:
                        take(2 * i, 0)
                    split_lo(i, 3)

                turns = NG[stage] // 2
                turn(0, True)
                with dve.Fori(1, turns) as i:
                    turn(i, False)
                if take:
                    take(2 * turns - 1, 1)

            normed("mix", 0)
            take_lo("mix")
            dve.wait_ge(small_tr, 2)
            dve.tensor_copy(post[:, :], bank[6][:, 0:CMP_LEN]).then_inc(small_sb, 1)
            dve.tensor_copy(ongt[:, :], bank[6][:, CMP_LEN:CMP_LEN + NH]).then_inc(small_sb, 1)
            dve.wait_ge(r_mm, 1)
            dve.tensor_copy(rvec[:, :], bank[7][0:NH, 0:RLEN]).then_inc(r_sb, 1)
            run("in", None)
            dve.wait_ge(gate_hi, 1)
            dve.tensor_tensor(wglo[:, :, :], wg[:, :, :], wghi[:, :, :].bitcast(fp32), ALU.subtract)\
                .then_inc(gate_lo, 1)

            def biased(c):
                _, _, _, bh, _, kind, _, _, _ = CALLS[c]
                dve.wait_ge(s_score, c + 1)
                if c >= 2:
                    dve.wait_ge(s_prob, 2 * (c - 1))
                if kind == "full":
                    w, w0 = RLEN, P
                    spans = [(slice(0, RLEN), bias[:, bh, :])]
                else:
                    w, w0 = NCMP0 + NCMP, NCMP0
                    spans = [(slice(0, w0), bias[:, bh, CMP_LEN - 1:P:CMP_STRIDE]),
                             (slice(w0, w), bias[:, bh, P + CMP_LEN - 1:RLEN:CMP_STRIDE])]
                for cols, b in spans:
                    st.did(dve.scalar_tensor_tensor(out=sc[c % 2][:, cols], in0=bank[2 + c % 2][:, cols], scalar=SCALE,
                                                    in1=b, op0=ALU.mult, op1=ALU.add))
                st.wait()
                for tt, cols in ((0, slice(0, w0)), (1, slice(w0, w))):
                    dve.tensor_reduce(negmax[c % 2][:, tt:tt + 1], sc[c % 2][:, cols], AX.X, ALU.max, negate=True)\
                        .then_inc(s_biased, 1)

            def scaled_identity(c):
                _, _, _, _, _, kind, gate, _, _ = CALLS[c]
                dve.wait_ge(s_prob, 2 * c + 2)
                r = rz[c % 2]
                st.did(dve.reciprocal(r[:, :], zsum[c % 2][:, :]))
                st.wait()
                if gate is not None:
                    st.did(dve.tensor_tensor(r[:, :], r[:, :], gates[:, :, gate], ALU.mult))
                    st.wait()
                if kind == "cmp":
                    st.did(dve.tensor_tensor(r[:, 0:1], r[:, 0:1], valid[:, :], ALU.mult))
                    st.wait()
                if c >= 2:
                    dve.wait_ge(s_pt, c - 1)
                for tt in range(TT):
                    dve.tensor_scalar(diag[c % 2][:, tt, :], ident[:, :], r[:, tt:tt + 1], None, ALU.mult)\
                        .then_inc(s_diag, 1)

            dve.wait_ge(bias_in, 32)
            dve.wait_ge(const_ready, 4)
            dve.wait_ge(gate_sig, 1)
            for s in range(NC_ + 1):
                if s < NC_:
                    biased(s)
                if s >= 1:
                    scaled_identity(s - 1)
                if s == A_H:
                    dve.wait_ge(cmp_mm, 1)
                    dve.tensor_copy(kct[:, :, :], bank[0][:, 0:KV * NCMP].rearrange("p (g n) -> p g n", g=KV))\
                        .then_inc(cmp_sb, 1)
                    dve.tensor_copy(vcm[0:NCMP, :, :],
                                    bank[1][0:NCMP, 0:KV * HD].rearrange("p (g d) -> p g d", g=KV)).then_inc(cmp_sb, 1)
            for n, (a, b) in enumerate(GROUPS):
                dve.wait_ge(g_sum, n + 1)
                dve.tensor_scalar(orms[:, n, :], bank[2 + n][:, 0:SEQ], 1.0 / ((b - a) * HD), EPS, ALU.mult, ALU.add)\
                    .then_inc(g_root, 1)
            dve.wait_ge(g_rstd, 1)
            st.did(dve.reciprocal(orms[:, :, :], orms[:, :, :]))
            st.wait()
            for n, (a, b) in enumerate(GROUPS):
                for h in range(a, b):
                    dve.scalar_tensor_tensor(out=ysc[:, h, :], in0=ot[:, h, :], scalar=ongt[:, h:h + 1],
                                             in1=orms[:, n, :], op0=ALU.mult, op1=ALU.mult).then_inc(y_ready, 1)
                dve.wait_ge(y_hi, n + 1)
                dve.tensor_tensor(xtlo[:, a:b, :], ysc[:, a:b, :], xthi[:, a:b, :].bitcast(fp32), ALU.subtract)\
                    .then_inc(y_lo, 1)

            def add_mixer(group, parity):
                dve.wait_ge(mm_done["out"], 2 * group + 2)
                cols = bass.ds(group * CHUNK_C, CHUNK_C)
                dve.tensor_tensor(hres[:, :, cols], hres[:, :, cols],
                                  bank[parity][:, :].rearrange("p (t c) -> p t c", t=TT), ALU.add)\
                    .then_inc(evac["out"], 1)

            run("out", add_mixer)
            dve.wait_ge(evac["out"], NG["out"])
            normed("ffn", 1)
            take_lo("ffn")
            run("wq", None)

            def route(s, b, peeled):
                if not peeled:
                    dve.wait_ge(gate_exp, s)
                st.did(dve.tensor_copy(s1[:, :, :], scores[:, bass.ds(s, 1), :, :].rearrange("p o c k -> p (o c) k")))
                st.wait_apart()
                for c in range(2):
                    st.did(dve.max(top[:, c, 0:8], s1[:, c, :]))
                st.wait_apart()
                for c in range(2):
                    st.did(dve.max_index(topi[:, c, 0:8], top[:, c, 0:8], s1[:, c, :]))
                    st.did(dve.match_replace(s2[:, c, :], top[:, c, 0:8], s1[:, c, :], TAKEN))
                st.wait_apart()
                for c in range(2):
                    st.did(dve.max(top[:, c, 8:16], s2[:, c, :]))
                st.wait_apart()
                for c in range(2):
                    st.did(dve.max_index(topi[:, c, 8:16], top[:, c, 8:16], s2[:, c, :]))
                st.did(dve.tensor_tensor(cand[:, :, :], top[:, 0, :, None].broadcast_to([P, TOPK, TOPK]),
                                         top[:, 1, None, :].broadcast_to([P, TOPK, TOPK]), ALU.add))
                st.wait()
                st.did(dve.tensor_copy(topf[:, :, :], topi[:, :, :]))
                c1 = cand[:, :, :].rearrange("p a b -> p (a b)")
                c2 = cand2[:, :, :].rearrange("p a b -> p (a b)")
                st.did(dve.max(best[:, 0:8], c1))
                st.wait_apart()
                st.did(dve.max_index(bestj[:, 0:8], best[:, 0:8], c1))
                st.did(dve.match_replace(c2, best[:, 0:8], c1, TAKEN))
                st.did(dve.tensor_scalar(nbest[:, :], best[:, 0:1], -1.0, None, ALU.mult))
                st.wait_apart()
                st.did(dve.max(best[:, 8:16], c2))
                st.wait_apart()
                st.did(dve.max_index(bestj[:, 8:16], best[:, 8:16], c2))
                st.wait()
                st.did(dve.tensor_scalar(bidx[:, 0, :], bestj[:, :], 4, None, ALU.logical_shift_right))
                st.did(dve.tensor_scalar(bidx[:, 1, :], bestj[:, :], TOPK - 1, None, ALU.bitwise_and))
                st.wait()
                for c in range(2):
                    st.did(dve.tensor_tensor(pick[:, :, :], bidx[:, c, :, None].broadcast_to([P, TOPK, TOPK]),
                                             iota[:, None, :].broadcast_to([P, TOPK, TOPK]), ALU.is_equal))
                    st.wait()
                    st.did(dve.tensor_tensor(pick[:, :, :], pick[:, :, :],
                                             topf[:, c, None, :].broadcast_to([P, TOPK, TOPK]), ALU.mult))
                    st.wait()
                    st.did(dve.tensor_reduce(pair[:, c, :], pick[:, :, :], AX.X, ALU.add))
                    st.wait()
                dve.scalar_tensor_tensor(out=expert[b][:, :], in0=pair[:, 0, :], scalar=float(NKEYS),
                                         in1=pair[:, 1, :], op0=ALU.mult, op1=ALU.add).then_inc(routed, 1)

            ROUTE_STEPS = 1 + 2 + 4 + 2 + 3 + 2 + 3 + 1 + 1 + 2 + 6

            def use_rows(turn, b, tt):
                s = 2 * turn + b

                def row(n):
                    dve.wait_ge(fetched[n % GRING], (s * (GET // GRING) + n // GRING + 1) * 16)
                    return rows[n % GRING]

                for k in range(TOPK):
                    r = row(k)
                    dve.scalar_tensor_tensor(out=r[:, :], in0=r[:, :], scalar=1.0, in1=xn[:, tt, :], op0=ALU.mult,
                                             op1=ALU.mult, accum_out=dots[b][:, k:k + 1]).then_inc(eaten, 1)
                dve.wait_ge(eaten, s * GET + TOPK)
                dve.wait_ge(gate_exp, s + 1)
                dve.reciprocal(gsum[b][:, :], gsum[b][:, :]).then_inc(dots_ready, 1)
                dve.wait_ge(gelu_ready, s + 1)
                st.did(dve.scalar_tensor_tensor(out=coef[b][:, :], in0=gel[b][:, :], scalar=gsum[b][:, :],
                                                in1=gexp[b][:, :], op0=ALU.mult, op1=ALU.mult))
                st.wait()
                for k in range(TOPK):
                    r = row(TOPK + k)
                    dve.scalar_tensor_tensor(out=hres[:, tt, :], in0=r[:, :], scalar=coef[b][:, k:k + 1],
                                             in1=hres[:, tt, :], op0=ALU.mult, op1=ALU.add).then_inc(eaten, 1)
                    dve.wait_ge(eaten, s * GET + TOPK + k + 1)

            def peer_pair(i, tt, last):
                route(2 * i + 1, 1, False)
                use_rows(i, 0, tt)
                if not last:
                    route(2 * i + 2, 0, False)
                use_rows(i, 1, tt)

            dve.wait_ge(sc_sb, 8)
            route(0, 0, True)
            half = PAIRS // TT
            for tt in range(TT):
                end = (tt + 1) * half - (1 if tt == TT - 1 else 0)
                with dve.Fori(tt * half, end) as i:
                    st.enter(i - tt * half, 2 * (ROUTE_STEPS + 1))
                    peer_pair(i, tt, False)
                st.leave(end - tt * half)
            peer_pair(PAIRS - 1, TT - 1, True)
            dve.nop().then_inc(peer_done, TT)

            normed("ple", 2)
            take_lo("ple")

            def add_ple(group, parity):
                dve.wait_ge(evac["gate"], group + 1)
                cols = bass.ds(group * CHUNK_C, CHUNK_C)
                g = sig[parity][:, :].rearrange("p (t c) -> p t c", t=TT)
                st.did(dve.tensor_tensor(g, g, pp[:, :, cols], ALU.mult))
                st.wait()
                dve.tensor_tensor(hres[:, :, cols], hres[:, :, cols], g, ALU.add).then_inc(ple_added, 1)

            def run_gate():
                stage = "gate"

                def split_lo(i, r):
                    dve.wait_ge(hi_ready[stage], RING * i + r + 1)
                    dve.tensor_tensor(wlo[r % 2][:, :, :], raw[r][:, :, :], whi[r % 2][:, :, :].bitcast(fp32),
                                      ALU.subtract).then_inc(lo_ready[stage], 1)

                split_lo(0, 0)
                split_lo(0, 1)
                split_lo(0, 2)
                add_ple(0, 0)
                split_lo(0, 3)
                with dve.Fori(1, NG[stage] // 2) as i:
                    st.enter(i - 1, 2)
                    split_lo(i, 0)
                    add_ple(2 * i - 1, 1)
                    split_lo(i, 1)
                    split_lo(i, 2)
                    add_ple(2 * i, 0)
                    split_lo(i, 3)
                st.leave(NG[stage] // 2 - 1)
                add_ple(NG[stage] - 1, 1)

            dve.wait_ge(pp_sb, 8)
            run_gate()
            normed("fin", 3)

        @block.tensor
        def _(pe):
            def transposes(name):
                pe.wait_ge(norm_done[name], TT)
                for b in range(8):
                    tt, kb = b // 4, b % 4
                    if b >= 4:
                        pe.wait_ge(tr_lo[name], b - 3)
                    for a in range(4):
                        k = 4 * kb + a
                        last = pe.transpose(bank[2 + b % 4][:, a * P:(a + 1) * P], xn[:, tt, k * P:(k + 1) * P],
                                            ident[:, :])
                    last.then_inc(tr_done[name], 1)

            def chunk(stage, i, r, peeled):
                feature_major = stage in ("in", "wq")
                acc = bank[r // 2]
                pe.wait_ge(lo_ready[stage], RING * i + r + 1)
                if r % 2 == 0 and not peeled:
                    pe.wait_ge(evac[stage], 2 * i + r // 2 - 1)
                for k in range(CHUNK_K):
                    kk = (r % 2) * CHUNK_K + k
                    for u in range(2):
                        cols = slice(u * P, (u + 1) * P)
                        start = r % 2 == 0 and k == 0 and u == 0
                        stop = r % 2 == 1 and k == CHUNK_K - 1
                        hi, lo = whi[r % 2], wlo[r % 2]
                        dst = acc[:, u * SEQ:(u + 1) * SEQ]
                        if feature_major:
                            parts = [(hi[:, k, cols], xthi[:, kk, :]), (hi[:, k, cols], xtlo[:, kk, :]),
                                     (lo[:, k, cols], xthi[:, kk, :])]
                        else:
                            parts = [(xthi[:, kk, cols], hi[:, k, :]), (xthi[:, kk, cols], lo[:, k, :]),
                                     (xtlo[:, kk, cols], hi[:, k, :])]
                        for n, (a, b) in enumerate(parts):
                            last = pe.matmul(dst, a, b, start=start and n == 0, stop=stop and n == 2,
                                             skip_group_check=True)
                last.then_inc(mm_done[stage], 1)

            def run(stage):
                for r in range(RING):
                    chunk(stage, 0, r, True)
                with pe.Fori(1, NG[stage] // 2) as i:
                    for r in range(RING):
                        chunk(stage, i, r, False)

            pe.wait_ge(const_ready, 4)
            transposes("mix")
            pe.wait_ge(small_in, 96)
            pe.transpose(bank[6][:, 0:CMP_LEN], posn[:, :], ident[0:CMP_LEN, 0:CMP_LEN]).then_inc(small_tr, 1)
            pe.transpose(bank[6][:, CMP_LEN:CMP_LEN + NH], ongn[:, :], ident[0:NH, 0:NH]).then_inc(small_tr, 1)
            pe.matmul(bank[7][0:NH, 0:RLEN], tabl[:, 0:NH], tabl[:, NH:], start=True, stop=True).then_inc(r_mm, 1)
            pe.wait_ge(tr_lo["mix"], 8)
            run("in")
            pe.wait_ge(gate_lo, 1)
            pe.wait_ge(r_sb, 1)
            for tt in range(TT):
                cols = slice(tt * P, (tt + 1) * P)
                for k in range(KT):
                    parts = [(xthi, wghi), (xthi, wglo), (xtlo, wghi)]
                    for n, (a, b) in enumerate(parts):
                        last = pe.matmul(bank[7][:, tt * GATES:(tt + 1) * GATES], a[:, k, cols], b[:, k, :],
                                         start=tt == 0 and k == 0 and n == 0, stop=k == KT - 1 and n == 2,
                                         skip_group_check=True)
            last.then_inc(gate_mm, 1)
            pe.wait_ge(evac["in"], NG["in"])
            for n in range(len(V_UNITS) // 2):
                if n >= 2:
                    pe.wait_ge(vt_sb, n - 1)
                for a in range(4):
                    u, tt = V_UNITS[2 * n + a // 2], a % 2
                    last = pe.transpose(bank[2 + n % 2][:, a * P:(a + 1) * P], pr[:, u, tt * P:(tt + 1) * P],
                                        ident[:, :])
                last.then_inc(vt_mm, 1)

            def score(c):
                q, k, _, _, _, kind, _, _, _ = CALLS[c]
                if c >= 2:
                    pe.wait_ge(s_biased, 2 * (c - 1))
                dst = bank[2 + c % 2]
                if kind == "full":
                    pe.matmul(dst[:, 0:P], pr[:, q, 0:P], pr[:, k, 0:P], start=True, stop=True)
                    last = pe.matmul(dst[:, P:RLEN], pr[:, q, P:SEQ], pr[:, k, :], start=True, stop=True)
                else:
                    pe.matmul(dst[:, 0:NCMP0], pr[:, q, 0:P], kct[:, k, 0:NCMP0], start=True, stop=True)
                    last = pe.matmul(dst[:, NCMP0:NCMP0 + NCMP], pr[:, q, P:SEQ], kct[:, k, :], start=True, stop=True)
                last.then_inc(s_score, 1)

            def transpose_probs(c):
                kind = CALLS[c][5]
                pe.wait_ge(s_diag, 2 * c + 2)
                if c >= 2:
                    pe.wait_ge(s_pts, c - 1)
                dst, pr_, dg = bank[4 + c % 2], pb[c % 3], diag[c % 2]
                if kind == "full":
                    pe.matmul(dst[:, 0:P], pr_[:, 0:P], dg[:, 0, :], start=True, stop=True)
                    pe.matmul(dst[:, P:2 * P], pr_[:, P:2 * P], dg[:, 1, :], start=True, stop=True)
                    last = pe.matmul(dst[:, 2 * P:RLEN], pr_[:, 2 * P:RLEN], dg[:, 1, :], start=True, stop=True)
                else:
                    pe.matmul(dst[0:NCMP0, 0:P], pr_[:, 0:NCMP0], dg[:, 0, :], start=True, stop=True)
                    last = pe.matmul(dst[0:NCMP, P:SEQ], pr_[:, NCMP0:NCMP0 + NCMP], dg[:, 1, :], start=True, stop=True)
                last.then_inc(s_pt, 1)

            def values(c):
                _, _, v, _, h, kind, _, first, final = CALLS[c]
                pe.wait_ge(s_pts, c + 1)
                n = HEAD_ORD[h]
                if first and n >= 2:
                    pe.wait_ge(s_ot, n - 1)
                dst, pt = bank[6 + n % 2], pts[c % 2]
                if kind == "full":
                    pe.matmul(dst[:, 0:SEQ], pr[:, v, 0:P], pt[:, 0:SEQ], start=first, stop=False,
                              skip_group_check=True)
                    last = pe.matmul(dst[:, P:SEQ], pr[:, v, P:SEQ], pt[:, SEQ:RLEN], start=False, stop=final,
                                     skip_group_check=True)
                else:
                    pe.matmul(dst[:, 0:P], vcm[0:NCMP0, v, :], pt[0:NCMP0, 0:P], start=False, stop=False,
                              skip_group_check=True)
                    last = pe.matmul(dst[:, P:SEQ], vcm[0:NCMP, v, :], pt[0:NCMP, P:SEQ], start=False, stop=final,
                                     skip_group_check=True)
                last.then_inc(s_pv, 1)

            pe.wait_ge(vt_sb, len(V_UNITS) // 2)
            pe.wait_ge(gate_sig, 1)
            for s in range(NC_ + 3):
                if s < NC_:
                    if CALLS[s][5] == "cmp":
                        pe.wait_ge(cmp_sb, 2)
                    score(s)
                if 0 <= s - 2 < NC_:
                    transpose_probs(s - 2)
                if 0 <= s - 3 < NC_:
                    values(s - 3)
                if s == A_H - 1:
                    pe.wait_ge(wcmp_in, 32)
                    pe.wait_ge(xcmp_ready, 2 * KV)
                    for l in range(CMP_LEN):
                        pe.matmul(bank[0][:, 0:KV * NCMP], wcmp[0][:, l, :],
                                  xcmp[:, 0, l, :, :].rearrange("p g n -> p (g n)"), start=l == 0, stop=l == CMP_LEN - 1)
                        for g in range(KV):
                            last = pe.matmul(bank[1][0:NCMP, g * HD:(g + 1) * HD], xcmp[:, 1, l, g, :],
                                             wcmp[1][:, l, :], start=l == 0 and g == 0, stop=l == CMP_LEN - 1,
                                             skip_group_check=True)
                    last.then_inc(cmp_mm, 1)
            for n, (a, b) in enumerate(GROUPS):
                pe.wait_ge(g_sq, n + 1)
                for h in range(a, b):
                    last = pe.matmul(bank[2 + n][:, 0:SEQ], ones[:, :], osq[:, h, :], start=h == a, stop=h == b - 1)
                last.then_inc(g_sum, 1)
            pe.wait_ge(y_lo, 3)
            pe.wait_ge(cmp_sb, 2)
            run("out")
            transposes("ffn")
            pe.wait_ge(tr_lo["ffn"], 8)
            pe.wait_ge(evac["out"], NG["out"])
            run("wq")
            pe.wait_ge(keys_in, 16)
            for n in range(4):
                if n >= 2:
                    pe.wait_ge(kt_sb, n - 1)
                for a in range(4):
                    last = pe.transpose(bank[2 + n % 2][:, a * P:(a + 1) * P], keys[:, 4 * n + a, :], ident[:, :])
                last.then_inc(kt_mm, 1)
            pe.wait_ge(kt_sb, 4)
            pe.wait_ge(evac["wq"], NG["wq"])
            for n in range(8):
                tt, h0 = n // 4, 2 * (n % 4)
                if n >= 2:
                    pe.wait_ge(sc_sb, n - 1)
                for a in range(4):
                    hc = 2 * h0 + a
                    last = pe.matmul(bank[4 + n % 2][:, a * P:(a + 1) * P], qt[:, hc, tt * P:(tt + 1) * P],
                                     keyst[:, hc, :], start=True, stop=True)
                last.then_inc(sc_mm, 1)
            for k in range(PLE // P):
                for tt in range(TT):
                    last = pe.transpose(bank[6 + k][:, tt * P:(tt + 1) * P], ptile[:, tt, k * P:(k + 1) * P], ident[:, :])
                last.then_inc(pt2_mm, 1)
            pe.wait_ge(pt2_sb, PLE // P)
            pe.wait_ge(pproj_in, 16)
            for n in range(8):
                tt, cb = n // 4, n % 4
                if n >= 2:
                    pe.wait_ge(pp_sb, n - 1)
                for k in range(PLE // P):
                    last = pe.matmul(bank[2 + n % 2][:, :], ptt[:, k, tt * P:(tt + 1) * P],
                                     pproj[:, k, cb * 512:(cb + 1) * 512], start=k == 0, stop=k == PLE // P - 1)
                last.then_inc(pp_mm, 1)
            transposes("ple")
            pe.wait_ge(tr_lo["ple"], 8)
            run("gate")


NAMES = ["x", "p", "ln_mix", "w_in", "cmp_wk", "cmp_wv", "cmp_pos", "out_norm", "w_out", "rel_bias", "ln_ffn",
         "peer_wq", "peer_keys", "peer_u", "peer_v", "ln_ple", "ple_gate", "ple_proj", "ln_final"]


def kernel(**inputs):
    import concourse.bacc as bacc
    from concourse.bass_utils import run_bass_kernel_spmd as run

    nc = bacc.Bacc("TRN2", target_bir_lowering=False, num_devices=1)
    arrays, args = {}, []
    for name in NAMES:
        a = np.ascontiguousarray(inputs[name])
        arrays[f"{name}_dram"] = a
        args.append(nc.dram_tensor(f"{name}_dram", a.shape, mybir.dt.from_np(a.dtype), kind="ExternalInput").ap())
    arrays["table_dram"] = bias_table()
    args.append(nc.dram_tensor("table_dram", arrays["table_dram"].shape, mybir.dt.float32, kind="ExternalInput").ap())
    args.append(nc.dram_tensor("out_dram", (1, SEQ, D), mybir.dt.float32, kind="ExternalOutput").ap())
    build(nc, *args)
    r = run(nc, [arrays], core_ids=[0])
    return r.results[0]["out_dram"]
```

```python
import math

import numpy as np

import concourse.bass as bass
from concourse import mybir

SEQ, D, HD = 256, 2048, 128
P = 128
TT = SEQ // P
KT = D // P
A_H, B_H, C_H, KV = 6, 6, 4, 2
NH = A_H + B_H + C_H
GROUP = B_H // KV
GATES = 3 * B_H
CMP_LEN, CMP_STRIDE = 32, 16
NCMP = (SEQ - CMP_LEN) // CMP_STRIDE + 1
NCMP0 = (P - CMP_LEN) // CMP_STRIDE + 1
PEER_H, NKEYS, TOPK = 8, 128, 16
PLE = 256
BUCKETS, MAX_DIST = 32, 1024
EPS = 1e-6
SCALE = HD ** -0.5
NEG = -1e30
TAKEN = -3e38

QA, KA, VA = 0, A_H, 2 * A_H
QB = 3 * A_H
KC, VC = QB + B_H, QB + B_H + KV
KS, VS, KW, VW = VC + KV, VC + 2 * KV, VC + 3 * KV, VC + 4 * KV
QC = VW + KV
KCC, VCC = QC + C_H, QC + 2 * C_H
UNITS = VCC + C_H
GATE_COL = QC * P
V_UNITS = [*range(VA, VA + A_H), *range(VS, VS + KV), *range(VW, VW + KV), *range(VCC, VCC + C_H)]

CHUNK_K, CHUNK_C = 8, 256
RING = 4
GRING = 8
SLOTS = PEER_H * TOPK
QUARTERS = 4
VCOL = D // QUARTERS
VBLK = QUARTERS - 1
VRING = 4
VUNITS = 3
TOKB = 4
RLEN = 384


def bias_table():
    dist = 255 - np.arange(RLEN)
    d = np.maximum(dist, 0)
    exact = BUCKETS // 2
    logd = np.log(np.maximum(d, 1).astype(np.float32) / np.float32(exact))
    large = exact + (logd / np.float32(math.log(MAX_DIST / exact)) * np.float32(BUCKETS - exact)).astype(np.int32)
    bucket = np.where(d < exact, d, np.clip(large, exact, BUCKETS - 1))
    out = np.zeros((BUCKETS + 2, NH + RLEN), np.float32)
    out[BUCKETS, :A_H] = 1.0
    out[BUCKETS + 1, A_H:NH] = 1.0
    out[bucket, NH + np.arange(RLEN)] = 1.0
    count = (dist <= 128).astype(int) + (dist % 4 == 0) + (dist % 16 == 0)
    dilated = np.where((dist >= 0) & (count > 0), np.log(np.maximum(count, 1)), NEG)
    out[BUCKETS, NH:] = dilated
    out[BUCKETS + 1, NH:] = np.where(dist >= 0, 0.0, NEG)
    return out


def calls():
    out = []
    for h in range(A_H):
        out.append((QA + h, KA + h, VA + h, h, h, "full", None, True, True))
    for h in range(C_H):
        out.append((QC + h, KCC + h, VCC + h, A_H + B_H + h, A_H + B_H + h, "full", None, True, True))
    for h in range(B_H):
        g = h // GROUP
        out.append((QB + h, KS + g, VS + g, A_H + h, A_H + h, "full", 3 * h + 1, True, False))
        out.append((QB + h, KW + g, VW + g, A_H + h, A_H + h, "full", 3 * h + 2, False, False))
        out.append((QB + h, g, g, A_H + h, A_H + h, "cmp", 3 * h, False, True))
    return out


class Steps:

    def __init__(self, eng, sem):
        self.eng, self.sem, self.n, self.base = eng, sem, 0, 0

    def did(self, ins):
        ins.then_inc(self.sem, 1)
        self.n += 1

    def wait(self):
        self.eng.wait_ge(self.sem, self.base + self.n)

    def wait_apart(self):
        self.wait()
        self.eng.nop(nofuse=True)

    def enter(self, turn, per_turn):
        self.before, self.per_turn = self.n, per_turn
        self.base, self.n = self.before + turn * per_turn, 0

    def leave(self, turns):
        assert self.n == self.per_turn, (self.n, self.per_turn)
        self.base, self.n = 0, self.before + turns * self.per_turn


def build(nc, x, p, ln_mix, w_in, cmp_wk, cmp_wv, cmp_pos, out_norm, w_out, rel_bias, ln_ffn, peer_wq,
          peer_keys, peer_u, peer_v, ln_ple, ple_gate, ple_proj, ln_final, table, out):
    fp32, f32r, i32, u32 = mybir.dt.float32, mybir.dt.float32r, mybir.dt.int32, mybir.dt.uint32
    ALU, ACT, AX = mybir.AluOpType, mybir.ActivationFunctionType, mybir.AxisListType

    base = -(-nc.sbuf_base // 64) * 64
    size = {fp32: 4, f32r: 4, i32: 4, u32: 4}

    def at(name, offset, shape, dt=fp32):
        return nc.alloc_sbuf_tensor_at(name, shape, dt, offset=base + offset)

    def placer(start):
        cursor = [start]

        def place(name, shape, dt=fp32):
            o = cursor[0]
            cursor[0] += -(-int(np.prod(shape[1:])) * size[dt] // 32) * 32
            return at(name, o, shape, dt)
        return place, cursor

    KB = 1024
    hres = at("hres", 0, [P, TT, D])
    xn = at("xn", 16 * KB, [P, TT, D])
    gain = at("gain", 32 * KB, [P, D])
    bias = at("bias", 16 * KB, [P, NH, RLEN])
    raw = [at(f"raw{r}", (40 + 8 * r) * KB, [P, CHUNK_K, CHUNK_C]) for r in range(RING)]
    whi = [at(f"whi{b}", (72 + 8 * b) * KB, [P, CHUNK_K, CHUNK_C], f32r) for b in range(2)]
    wlo = [at(f"wlo{b}", (88 + 8 * b) * KB, [P, CHUNK_K, CHUNK_C], f32r) for b in range(2)]
    xthi = at("xthi", 104 * KB, [P, KT, SEQ], f32r)
    xtlo = at("xtlo", 120 * KB, [P, KT, SEQ], f32r)
    pr = at("pr", 136 * KB, [P, UNITS, SEQ])

    ot = at("ot", 72 * KB, [P, NH, SEQ])
    o_att = 88 * KB
    sc = [at(f"sc{b}", o_att + b * 1536, [P, RLEN]) for b in range(2)]
    pb = [at(f"pb{b}", o_att + 3072 + b * 1536, [P, RLEN]) for b in range(3)]
    gatest = at("gatest", o_att + 3072, [GATES, SEQ])
    pts = [at(f"pts{b}", o_att + 7680 + b * 1536, [P, RLEN]) for b in range(2)]
    diag = [at(f"diag{b}", o_att + 10752 + b * 1024, [P, TT, P]) for b in range(2)]
    wcmp = [at("wk_cmp", 104 * KB, [P, CMP_LEN, HD]), at("wv_cmp", 120 * KB, [P, CMP_LEN, HD])]
    osq = at("osq", 136 * KB, [P, NH, SEQ])
    orms = at("orms", 152 * KB, [P, 3, SEQ])
    ysc = at("ysc", 156 * KB, [P, NH, SEQ])
    qt = at("qt", 136 * KB, [P, 2 * PEER_H, SEQ])
    keyst = at("keyst", 152 * KB, [P, 2 * PEER_H, NKEYS])
    scores = at("scores", 160 * KB, [P, TT * PEER_H, 2, NKEYS])
    keys = at("keys", 176 * KB, [P, 2 * PEER_H, HD])
    pproj = at("pproj", 40 * KB, [P, PLE // P, D])
    pp_made = at("pp_made", 56 * KB, [P, TT, D])
    ptile = at("ptile", 72 * KB, [P, TT, PLE])
    ptt = at("ptt", 74 * KB, [P, PLE // P, SEQ])
    spread = at("spread", 32 * KB, [P, TT, NKEYS, P])
    rows = [at(f"rows{r}", (96 + 8 * r) * KB, [P, D]) for r in range(GRING)]
    HOTS = [2, 4]
    o_spread = [190 * KB, 160 * KB]
    tsl = [at("tsl0", 198 * KB, [P, 3, P]), at("tsl1", 201 * KB, [P, 3, P])]
    hot1 = [[at(f"hot1_{t}_{b}", o_spread[t] + 2 * b * KB, [P, TOKB, NKEYS]) for b in range(HOTS[t])]
            for t in range(TT)]
    hot2 = [[at(f"hot2_{t}_{b}", o_spread[t] + 2 * (HOTS[t] + b) * KB, [P, TOKB, NKEYS]) for b in range(HOTS[t])]
            for t in range(TT)]
    vraw = [at(f"vraw{r}", (176 + 6 * r) * KB, [P, VBLK * VCOL]) for r in range(VRING)]
    vhi = [at(f"vhi{b}", (160 + 2 * b) * KB, [P, VCOL], f32r) for b in range(VUNITS)]
    vlo = [at(f"vlo{b}", (166 + 2 * b) * KB, [P, VCOL], f32r) for b in range(VUNITS)]
    chi = [at(f"chi{b}", (172 + b) * KB, [P, TT, P], f32r) for b in range(2)]
    clo = [at(f"clo{b}", (174 + b) * KB, [P, TT, P], f32r) for b in range(2)]
    vrow = [at(f"vrow{r}", (16 + 2 * r) * KB, [P, VCOL]) for r in range(GRING)]
    pp = at("pp", 136 * KB, [P, TT, D])
    sig = [at(f"sig{b}", (152 + 2 * b) * KB, [P, TT * CHUNK_C]) for b in range(2)]

    place, cursor = placer(184 * KB)
    vct = place("vct", [P, KV, NCMP])
    xcmp = place("xcmp", [P, 2, CMP_LEN, KV, NCMP])
    kct = place("kct", [P, KV, NCMP])
    wg = place("wg", [P, KT, GATES])
    wghi = place("wghi", [P, KT, GATES], f32r)
    wglo = place("wglo", [P, KT, GATES], f32r)
    gates = place("gates", [P, TT, GATES])
    ksb = at("ksb", cursor[0], [KV * NCMP, 2, HD])
    rvec = place("rvec", [NH, RLEN])
    tabl = place("tabl", [BUCKETS + 2, NH + RLEN])
    vcm = place("vcm", [P, KV, HD])
    assert cursor[0] <= 200 * KB, cursor[0]
    place, cursor = placer(184 * KB)
    s1 = place("s1", [P, 2, NKEYS])
    s2 = place("s2", [P, 2, NKEYS])
    cand = place("cand", [P, TOPK, TOPK])
    cand2 = place("cand2", [P, TOPK, TOPK])
    pick = place("pick", [P, TOPK, TOPK])
    assert cursor[0] <= 190 * KB

    place, cursor = placer(200 * KB)
    ident = place("ident", [P, P])
    ones = place("ones", [P, P])
    posn = at("posn", 200 * KB + 1024, [CMP_LEN, HD])
    ongn = at("ongn", 200 * KB + 1536, [NH, HD])
    slot_idx = place("slot_idx", [P, 2, TT * SLOTS])
    slot_row = place("slot_row", [P, TT * SLOTS], i32)
    slot_coef = place("slot_coef", [P, TT * SLOTS])
    post = place("post", [P, CMP_LEN])
    ongt = place("ongt", [P, NH])
    valid = place("valid", [P, 1])
    ssq = place("ssq", [P, TT])
    rstd = place("rstd", [P, TT])
    negmax = [place(f"negmax{b}", [P, TT]) for b in range(2)]
    zsum = [place(f"zsum{b}", [P, TT]) for b in range(2)]
    rz = [place(f"rz{b}", [P, TT]) for b in range(2)]
    top = place("top", [P, 2, TOPK])
    topi = place("topi", [P, 2, TOPK], u32)
    topf = place("topf", [P, 2, TOPK])
    best = place("best", [P, TOPK])
    bestj = place("bestj", [P, TOPK], u32)
    bidx = place("bidx", [P, 2, TOPK], u32)
    nbest = place("nbest", [P, 1])
    iota = place("iota", [P, NKEYS])
    expert = [place(f"expert{b}", [P, TOPK], i32) for b in range(2)]
    gsum = [place(f"gsum{b}", [P, 1]) for b in range(2)]
    gexp = [place(f"gexp{b}", [P, TOPK]) for b in range(2)]
    dots = [place(f"dots{b}", [P, TOPK]) for b in range(2)]
    gel = [place(f"gel{b}", [P, TOPK]) for b in range(2)]
    idx4 = place("idx4", [P, TOKB])
    vidx = [place(f"vidx{r}", [P, 1], i32) for r in range(GRING)]
    assert base + cursor[0] <= nc.sbuf_usable_end, (base + cursor[0], nc.sbuf_usable_end)

    SPREAD_BANK = [6, 7, 0, 1]
    bank = [nc.alloc_psum_tensor(f"bank{b}", [P, 512], fp32) for b in range(8)]
    rdram = nc.dram_tensor("bias_by_distance", (NH, P, RLEN), fp32, kind="Internal").ap()

    ppdram = nc.dram_tensor("p_projected", (P, TT, D), fp32, kind="Internal").ap()

    def sem(name):
        return nc.alloc_semaphore(name)

    dve_step, pool_step = sem("dve_step"), sem("pool_step")
    const_ready = sem("const_ready")
    x_in, small_in, keys_in = sem("x_in"), sem("small_in"), sem("keys_in")
    wg_in, wcmp_in, pproj_in = sem("wg_in"), sem("wcmp_in"), sem("pproj_in")
    gain_in = sem("gain_in")
    norms = ["mix", "ffn", "ple", "fin"]
    norm_sq = {n: sem(f"{n}_squared") for n in norms}
    norm_root = {n: sem(f"{n}_root") for n in norms}
    norm_done = {n: sem(f"{n}_normed") for n in norms}
    tr_done = {n: sem(f"{n}_transposed") for n in norms[:3]}
    tr_hi = {n: sem(f"{n}_xthi") for n in norms[:3]}
    tr_lo = {n: sem(f"{n}_xtlo") for n in norms[:3]}
    stages = ["in", "out", "wq", "gate"]
    landed = {s: [sem(f"{s}_landed{r}") for r in range(RING)] for s in stages}
    hi_ready = {s: sem(f"{s}_whi") for s in stages}
    lo_ready = {s: sem(f"{s}_wlo") for s in stages}
    mm_done = {s: sem(f"{s}_products") for s in stages}
    evac = {s: sem(f"{s}_evacuated") for s in stages}
    NG = {"in": UNITS * P // CHUNK_C, "out": D // CHUNK_C, "wq": D // CHUNK_C, "gate": D // CHUNK_C}
    small_tr, small_sb = sem("small_transposed"), sem("small_copied")
    r_mm, r_sb, r_out, bias_in = sem("r_mm"), sem("r_sb"), sem("r_out"), sem("bias_in")
    gate_hi, gate_lo, gate_mm, gate_sig = sem("gate_hi"), sem("gate_lo"), sem("gate_mm"), sem("gate_sig")
    gate_tr, gate_sb, cmp_tr = sem("gates_transposed"), sem("gates_copied"), sem("cmp_values_transposed")
    xcmp_ready, cmp_mm, cmp_sb = sem("xcmp_ready"), sem("cmp_mm"), sem("cmp_sb")
    vt_mm, vt_sb = sem("vt_mm"), sem("vt_sb")
    s_score, s_biased, s_prob, s_diag = sem("scores_ready"), sem("biased"), sem("probs"), sem("diag_ready")
    s_pt, s_pts, s_pv, s_ot = sem("probs_transposed"), sem("probs_t_copied"), sem("pv_done"), sem("head_out")
    g_sq, g_sum, g_root, g_rstd = sem("group_squares"), sem("group_sums"), sem("group_root"), sem("group_rstd")
    y_ready, y_hi, y_lo = sem("y_ready"), sem("y_hi"), sem("y_lo")
    kt_mm, kt_sb, sc_mm, sc_sb = sem("keys_transposed"), sem("keys_copied"), sem("key_scores"), sem("key_scores_copied")
    routed, gate_exp = sem("experts_chosen"), sem("gate_exp")
    fetched = [sem(f"rows_fetched{r}") for r in range(GRING)]
    eaten = sem("rows_used")
    dots_ready, gelu_ready, peer_done = sem("dots_ready"), sem("gelu_ready"), sem("peer_done")
    tsl_mm, tsl_sb = [[sem(f"{n}{t}") for t in range(TT)] for n in ("slots_transposed", "slots_copied")]
    hot_dist, hot_unit = sem("hot_distances"), sem("hot_units")
    hot_ready, hot1_ready = sem("tile0_one_hots"), sem("tile1_even_first_one_hots")
    hot2_ready, idx4_ready = sem("tile1_one_hots"), sem("indices_of_four_tokens")
    spread_mm, spread_sb = [[sem(f"{n}{t}") for t in range(TT)] for n in ("spread_products", "spread_copied")]
    v_landed = [sem(f"v_landed{r}") for r in range(VRING)]
    chi_ready, clo_ready, vhi_ready, vlo_ready = sem("chi_ready"), sem("clo_ready"), sem("vhi_ready"), sem("vlo_ready")
    v_mm = sem("v_products")
    vidx_ready, v_used = sem("vidx_ready"), sem("v_rows_used")
    v_fetched = [sem(f"v_rows_fetched{r}") for r in range(GRING)]
    coef_ready, pp_out, pp_in, p_in = sem("coef_ready"), sem("pp_out"), sem("pp_in"), sem("p_in")
    pt2_mm, pt2_sb, pp_mm, pp_sb = sem("p_transposed"), sem("p_copied"), sem("pp_mm"), sem("pp_sb")
    ple_added, out_sem = sem("ple_added"), sem("out_written")

    CALLS = calls()
    NC_ = len(CALLS)
    CMP_STEP, CMP_PARTS = 4, 4
    HEAD_ORD = {}
    for c, call in enumerate(CALLS):
        if call[7]:
            HEAD_ORD[call[4]] = len(HEAD_ORD)
    LAST = {c: call[4] for c, call in enumerate(CALLS) if call[8]}
    GROUPS = [(0, A_H), (A_H, A_H + B_H), (A_H + B_H, NH)]
    PEER_STEPS = TT * PEER_H
    PAIRS = PEER_STEPS // 2
    HALF = PAIRS // TT
    SPREADS = P // TOKB
    PER_STEP = SPREADS // PEER_H
    TURNS = NKEYS // VRING

    def weights_of(stage):
        return {"in": w_in, "out": w_out, "wq": peer_wq, "gate": ple_gate}[stage]

    block = nc.Block()
    with block:
        @block.sync
        def _(sp):
            for tt in range(TT):
                sp.dma_start(hres[:, tt, :], x[0, tt * P:(tt + 1) * P, :]).then_inc(x_in, 16)
            sp.dma_start(gain[:, :], ln_mix[0:1, :].partition_broadcast(P)).then_inc(gain_in, 16)

            def stream(stage, ngroups, first_group, gap):
                w = weights_of(stage)
                cols = ngroups * CHUNK_C
                c0 = first_group * CHUNK_C + gap
                view = w[0, :, c0:c0 + cols].rearrange("(h k q) c -> q h k c", q=P, k=CHUNK_K)

                def turn(i, peeled):
                    for r in range(RING):
                        if not peeled:
                            sp.wait_ge(lo_ready[stage], (first_group // 2 + i) * RING + r - RING + 1)
                        col = (2 * i + r // 2) * CHUNK_C
                        sp.dma_start(raw[r][:, :, :], view[:, r % 2, :, bass.ds(col, CHUNK_C)])\
                            .then_inc(landed[stage][r], 16)

                start = 0
                if first_group == 0:
                    turn(0, True)
                    start = 1
                if stage == "gate":
                    sp.wait_ge(pp_out, 16)
                    sp.dma_start(pp[:, :, :], ppdram).then_inc(pp_in, 16)
                with sp.Fori(start, ngroups // 2) as i:
                    turn(i, False)

            sp.dma_start(wg[:, :, :], w_in[0, :, GATE_COL:GATE_COL + GATES].rearrange("(k q) c -> q k c", q=P))\
                .then_inc(wg_in, 16)
            stream("in", QC // 2, 0, 0)
            stream("in", (UNITS - QC) // 2, QC // 2, GATES)
            sp.wait_ge(mm_done["in"], 2 * NG["in"])
            sp.wait_ge(gate_mm, 1)
            for w, sb in ((cmp_wk, wcmp[0]), (cmp_wv, wcmp[1])):
                sp.dma_start(sb[:, :, :], w[0].rearrange("l d e -> d l e")).then_inc(wcmp_in, 16)
            sp.wait_ge(lo_ready["in"], 2 * NG["in"])
            stream("out", NG["out"], 0, 0)
            sp.wait_ge(s_biased, 2 * NC_)
            sp.dma_start(gain[:, :], ln_ffn[0:1, :].partition_broadcast(P)).then_inc(gain_in, 16)
            sp.wait_ge(y_lo, 3)
            sp.dma_start(keys[:, :, :], peer_keys[0].rearrange("h c k d -> k (h c) d")).then_inc(keys_in, 16)
            sp.wait_ge(lo_ready["out"], 2 * NG["out"])
            stream("wq", NG["wq"], 0, 0)
            sp.wait_ge(mm_done["wq"], 2 * NG["wq"])
            sp.dma_start(ptile[:, :, :], p[0, 0].rearrange("(t q) c -> q t c", q=P)).then_inc(p_in, 16)
            sp.dma_start(pproj[:, :, :], ple_proj[0].rearrange("(k q) c -> q k c", q=P)).then_inc(pproj_in, 16)
            sp.wait_ge(pp_sb, 8)
            sp.dma_start(ppdram, pp_made[:, :, :]).then_inc(pp_out, 16)
            sp.wait_ge(routed, PEER_STEPS)
            sp.wait_ge(spread_sb[0], SPREADS)
            vview = peer_v[0].rearrange("(c q) d -> q c d", q=P)

            def v_turn(i, peeled):
                for r in range(VRING):
                    if not peeled:
                        sp.wait_ge(vlo_ready, (VRING * i + r - VRING + 1) * VBLK)
                    sp.dma_start(vraw[r][:, :], vview[:, bass.ds(VRING * i + r, 1), 0:VBLK * VCOL]
                                 .rearrange("q o d -> q (o d)")).then_inc(v_landed[r], 16)

            v_turn(0, True)
            with sp.Fori(1, TURNS) as i:
                v_turn(i, False)
            sp.wait_ge(clo_ready, NKEYS)
            sp.dma_start(gain[:, :], ln_ple[0:1, :].partition_broadcast(P)).then_inc(gain_in, 16)
            stream("gate", NG["gate"], 0, 0)
            sp.wait_ge(norm_done["ple"], TT)
            sp.dma_start(gain[:, :], ln_final[None, :].partition_broadcast(P)).then_inc(gain_in, 16)
            for tt in range(TT):
                sp.wait_ge(norm_done["fin"], tt + 1)
                sp.dma_start(out[0, tt * P:(tt + 1) * P, :], xn[:, tt, :]).then_inc(out_sem, 16)
            sp.wait_ge(out_sem, 16 * TT)

        @block.gpsimd
        def _(pool):
            pool.memset(ident[:, :], 0.0).then_inc(pool_step, 1)
            pool.memset(valid[:, :], 1.0).then_inc(pool_step, 1)
            pool.memset(ones[:, :], 1.0).then_inc(const_ready, 1)
            pool.iota(iota[:, :], [[1, NKEYS]], base=0, channel_multiplier=0,
                      allow_small_or_imprecise_dtypes=True).then_inc(const_ready, 1)
            pool.wait_ge(pool_step, 2)
            pool.affine_select(out=ident[:, :], in_=ident[:, :], compare_op=ALU.not_equal, fill=1.0, base=0,
                               pattern=[[-1, P]], channel_multiplier=1).then_inc(const_ready, 1)
            pool.affine_select(out=valid[:, :], in_=valid[:, :], compare_op=ALU.is_ge, fill=0.0,
                               base=-(CMP_LEN - 1), pattern=[[0, 1]], channel_multiplier=1).then_inc(const_ready, 1)
            pool.dma_start(tabl[:, NH:], table[:, NH:]).then_inc(small_in, 16)
            pool.dma_start(tabl[BUCKETS:, 0:NH], table[BUCKETS:, 0:NH]).then_inc(small_in, 16)
            pool.dma_start(tabl[0:BUCKETS, 0:NH], rel_bias).then_inc(small_in, 16)
            pool.dma_start(posn[:, :], cmp_pos[0]).then_inc(small_in, 16)
            pool.dma_start(ongn[:, :], out_norm[0].rearrange("(h d) -> h d", d=HD)).then_inc(small_in, 16)
            pool.wait_ge(r_sb, 1)
            pool.dma_start(rdram, rvec[:, None, :].broadcast_to([NH, P, RLEN])).then_inc(r_out, 16)
            pool.wait_ge(r_out, 16)
            pool.wait_ge(tr_lo["mix"], 8)
            pool.wait_ge(tr_hi["mix"], 8)
            shift, heads = [RLEN - 1, P], [P * RLEN, NH]
            tile1 = bass.AP(tensor=rdram.tensor, offset=P - 1, ap=[shift, heads, [1, SEQ]])
            tile0 = bass.AP(tensor=rdram.tensor, offset=SEQ - 1, ap=[shift, heads, [1, P]])
            pool.dma_start(bias[:, :, P:RLEN], tile1).then_inc(bias_in, 16)
            pool.dma_start(bias[:, :, 0:P], tile0).then_inc(bias_in, 16)

            pool.wait_ge(evac["in"], VC // 2 + 1)
            pool.wait_ge(small_sb, 2)
            for kv, unit in ((0, KC), (1, VC)):
                for g in range(KV):
                    a = pr[:, unit + g, :]
                    win = bass.AP(tensor=a.tensor, offset=a.offset, ap=[a.ap[0], [1, CMP_LEN], [CMP_STRIDE, NCMP]])
                    pool.tensor_tensor(xcmp[:, kv, :, g, :], win, post[:, :, None].broadcast_to([P, CMP_LEN, NCMP]),
                                       ALU.add).then_inc(xcmp_ready, 1)

            def fetch(pairs, peeled):
                for b in range(2):
                    pool.wait_ge(routed, pairs * 2 + b + 1)
                    for k in range(TOPK):
                        slot = k % GRING
                        if not (peeled and b == 0 and k < GRING):
                            pool.wait_ge(eaten, (pairs * 2 + b) * TOPK + k - GRING + 1)
                        pool.nop(nofuse=True)
                        pool.indirect_dma_start(rows[slot][:, :], None, peer_u[0],
                                                bass.IndirectOffsetOnAxis(ap=expert[b][:, k:k + 1], axis=0))\
                            .then_inc(fetched[slot], 16)

            pool.wait_ge(sc_mm, PEER_STEPS // 2)
            fetch(0, True)
            with pool.Fori(1, PAIRS) as i:
                fetch(i, False)

            quarters = peer_v[0].rearrange("e (f c) -> (e f) c", f=QUARTERS)

            def v_fetch(i, peeled):
                for r in range(GRING):
                    if not peeled:
                        pool.wait_ge(v_used, GRING * i + r - GRING + 1)
                    pool.tensor_copy(vidx[r][:, :], slot_row[:, bass.ds(GRING * i + r, 1)]).then_inc(vidx_ready, 1)
                    pool.wait_ge(vidx_ready, GRING * i + r + 1)
                    pool.nop(nofuse=True)
                    pool.indirect_dma_start(vrow[r][:, :], None, quarters,
                                            bass.IndirectOffsetOnAxis(ap=vidx[r][:, :], axis=0))\
                        .then_inc(v_fetched[r], 16)

            pool.wait_ge(eaten, PEER_STEPS * TOPK)

            def even_first_hots(i, m, peeled):
                n = 2 * i + m // 2
                if not peeled:
                    pool.wait_ge(spread_mm[1], 4 * i + m - 3)
                if not (peeled and m == 0):
                    pool.wait_ge(hot1_ready, TOKB * n)
                pool.tensor_copy(idx4[:, :], tsl[1][:, 0, bass.ds((4 * i + m) * TOKB, TOKB)]).then_inc(idx4_ready, 1)
                pool.wait_ge(idx4_ready, n + 1)
                pool.nop(nofuse=True)
                for a in range(TOKB):
                    pool.tensor_scalar(hot1[1][m][:, a, :], iota[:, :], idx4[:, a:a + 1], None,
                                       ALU.is_equal).then_inc(hot1_ready, 1)

            pool.wait_ge(tsl_sb[1], 1)
            for m in (0, 2):
                even_first_hots(0, m, True)
            with pool.Fori(1, SPREADS // 4) as i:
                for m in (0, 2):
                    even_first_hots(i, m, False)
            v_fetch(0, True)
            with pool.Fori(1, TURNS) as i:
                v_fetch(i, False)

        @block.scalar
        def _(act):
            def norm_sums(name):
                for tt in range(TT):
                    act.activation(xn[:, tt, :], hres[:, tt, :], ACT.Square, accum_out=ssq[:, tt:tt + 1])\
                        .then_inc(norm_sq[name], 1)
                act.wait_ge(norm_root[name], 1)
                act.activation(rstd[:, :], ssq[:, :], ACT.Sqrt).then_inc(norm_root[name], 1)

            def take_hi(name):
                for b in range(8):
                    tt, kb = b // 4, b % 4
                    act.wait_ge(tr_done[name], b + 1)
                    act.copy(xthi[:, 4 * kb:4 * kb + 4, tt * P:(tt + 1) * P],
                             bank[2 + b % 4][:, :].rearrange("p (a t) -> p a t", a=4)).then_inc(tr_hi[name], 1)

            def split_hi(stage, turn, r, peeled):
                act.wait_ge(landed[stage][r], 16 * (turn + 1))
                if not (peeled and r < 2):
                    act.wait_ge(mm_done[stage], RING * turn + r - 1)
                act.copy(whi[r % 2][:, :, :], raw[r][:, :, :]).then_inc(hi_ready[stage], 1)

            def run(stage, take):
                def turn(i, peeled):
                    split_hi(stage, i, 0, peeled)
                    if not peeled and take:
                        take(2 * i - 1, 1)
                    split_hi(stage, i, 1, peeled)
                    split_hi(stage, i, 2, peeled)
                    if take:
                        take(2 * i, 0)
                    split_hi(stage, i, 3, peeled)

                turns = NG[stage] // 2
                turn(0, True)
                with act.Fori(1, turns) as i:
                    turn(i, False)
                if take:
                    take(2 * turns - 1, 1)

            def copy_to(dst, stage):
                def take(group, parity):
                    act.wait_ge(mm_done[stage], 2 * group + 2)
                    act.copy(dst[:, bass.ds(2 * group, 2), :],
                             bank[parity][:, :].rearrange("p (u t) -> p u t", u=2)).then_inc(evac[stage], 1)
                return take

            act.wait_ge(x_in, 32)
            norm_sums("mix")
            take_hi("mix")
            act.wait_ge(wg_in, 16)
            act.copy(wghi[:, :, :], wg[:, :, :]).then_inc(gate_hi, 1)
            run("in", copy_to(pr, "in"))
            act.wait_ge(gate_mm, 1)
            act.activation(gatest[:, :], bank[7][0:GATES, 0:SEQ], ACT.Sigmoid).then_inc(gate_sig, 1)

            def exps(c):
                w = RLEN if CALLS[c][5] == "full" else NCMP0 + NCMP
                w0 = P if CALLS[c][5] == "full" else NCMP0
                act.wait_ge(s_biased, 2 * c + 2)
                if c >= 3:
                    act.wait_ge(s_pt, c - 2)
                for tt, cols in ((0, slice(0, w0)), (1, slice(w0, w))):
                    act.activation(pb[c % 3][:, cols], sc[c % 2][:, cols], ACT.Exp, bias=negmax[c % 2][:, tt:tt + 1],
                                   accum_out=zsum[c % 2][:, tt:tt + 1]).then_inc(s_prob, 1)

            def copy_pt(c):
                act.wait_ge(s_pt, c + 1)
                if c >= 2:
                    act.wait_ge(s_pv, c - 1)
                rows_, w = (P, RLEN) if CALLS[c][5] == "full" else (NCMP, SEQ)
                act.copy(pts[c % 2][0:rows_, 0:w], bank[4 + c % 2][0:rows_, 0:w]).then_inc(s_pts, 1)

            def head_out(c):
                h = LAST[c]
                act.wait_ge(s_pv, c + 1)
                act.copy(ot[:, h, :], bank[6 + HEAD_ORD[h] % 2][:, 0:SEQ]).then_inc(s_ot, 1)

            for s in range(NC_ + 4):
                if s < NC_:
                    exps(s)
                if 0 <= s - 2 < NC_:
                    copy_pt(s - 2)
                if s - 4 in LAST:
                    head_out(s - 4)
            act.wait_ge(s_ot, NH)
            for n, (a, b) in enumerate(GROUPS):
                act.activation(osq[:, a:b, :], ot[:, a:b, :], ACT.Square).then_inc(g_sq, 1)
            act.wait_ge(g_root, 3)
            act.activation(orms[:, :, :], orms[:, :, :], ACT.Sqrt).then_inc(g_rstd, 1)
            for n, (a, b) in enumerate(GROUPS):
                act.wait_ge(y_ready, b)
                act.copy(xthi[:, a:b, :], ysc[:, a:b, :]).then_inc(y_hi, 1)
            run("out", None)
            act.wait_ge(evac["out"], NG["out"])
            norm_sums("ffn")
            take_hi("ffn")
            run("wq", copy_to(qt, "wq"))
            for n in range(4):
                act.wait_ge(kt_mm, n + 1)
                act.copy(keyst[:, 4 * n:4 * n + 4, :], bank[2 + n % 2][:, :].rearrange("p (a k) -> p a k", a=4))\
                    .then_inc(kt_sb, 1)
            for n in range(8):
                act.wait_ge(sc_mm, n + 1)
                act.copy(scores[:, 2 * n:2 * n + 2, :, :],
                         bank[4 + n % 2][:, :].rearrange("p (s c k) -> p s c k", s=2, c=2)).then_inc(sc_sb, 1)

            def route_exp(turn, b, peeled):
                s = 2 * turn + b
                act.wait_ge(routed, s + 1)
                act.activation(gexp[b][:, :], best[:, :], ACT.Exp, bias=nbest[:, :], accum_out=gsum[b][:, :])\
                    .then_inc(gate_exp, 1)

            def gelu(turn, b):
                act.wait_ge(dots_ready, 2 * turn + b + 1)
                act.activation(gel[b][:, :], dots[b][:, :], ACT.Gelu).then_inc(gelu_ready, 1)

            route_exp(0, 0, True)

            for k in range(PLE // P):
                act.wait_ge(pt2_mm, k + 1)
                act.copy(ptt[:, k, :], bank[6 + k][:, 0:SEQ]).then_inc(pt2_sb, 1)
            for n in range(8):
                act.wait_ge(pp_mm, n + 1)
                tt, cb = n // 4, n % 4
                act.copy(pp_made[:, tt, cb * 512:(cb + 1) * 512], bank[2 + n % 2][:, :]).then_inc(pp_sb, 1)

            def take_spread(tt, q, m):
                act.wait_ge(spread_mm[tt], q + 1)
                act.copy(spread[:, tt, :, bass.ds(TOKB * q, TOKB)].rearrange("p i t -> p t i"),
                         bank[SPREAD_BANK[m % HOTS[tt]]][:, :].rearrange("p (t i) -> p t i", t=TOKB)).then_inc(spread_sb[tt], 1)

            def tile0_hots(q, m, peeled):
                if not (peeled and m < 2):
                    act.wait_ge(spread_mm[0], q - 1)
                h = [hot1[0][m % 2], hot2[0][m % 2]]
                for c in range(2):
                    for a in range(TOKB):
                        act.activation(h[c][:, a, :], iota[:, :], ACT.Abs, scale=-1.0,
                                       bias=tsl[0][:, c, bass.ds(TOKB * q + a, 1)]).then_inc(hot_dist, 1)
                act.wait_ge(hot_dist, 2 * TOKB * (q + 1))
                act.activation(h[1][:, :, :], h[1][:, :, :], ACT.Relu, scale=-1.0, bias=ones[:, 0:1])\
                    .then_inc(hot_unit, 1)
                act.activation(h[0][:, :, :], h[0][:, :, :], ACT.Relu, scale=-1.0, bias=ones[:, 0:1])\
                    .then_inc(hot_ready, 1)
                act.wait_ge(hot_unit, q + 1)
                for a in range(TOKB):
                    act.activation(h[1][:, a, :], h[1][:, a, :], ACT.Copy,
                                   scale=tsl[0][:, 2, bass.ds(TOKB * q + a, 1)]).then_inc(hot_ready, 1)

            def peer(i, spreading, last, first=False):
                for b in range(2):
                    if b == 0 or not last:
                        route_exp(i + b, 1 - b, False)
                    if spreading:
                        q = (2 * (i - HALF) + b) * PER_STEP
                        for m in range(PER_STEP):
                            tile0_hots(q + m, m, first and b == 0)
                            if m >= 1:
                                take_spread(0, q + m - 1, m - 1)
                        take_spread(0, q + PER_STEP - 1, PER_STEP - 1)
                    gelu(i, b)

            with act.Fori(0, HALF) as i:
                peer(i, False, False)
            act.wait_ge(tsl_mm[0], 1)
            act.copy(tsl[0][:, :, :], bank[5][:, 0:3 * P].rearrange("p (a t) -> p a t", a=3)).then_inc(tsl_sb[0], 1)
            act.wait_ge(pp_out, 16)
            act.wait_ge(tsl_sb[0], 1)
            peer(HALF, True, False, first=True)
            with act.Fori(HALF + 1, PAIRS - 1) as i:
                peer(i, True, False)
            peer(PAIRS - 1, True, True)
            act.wait_ge(tsl_mm[1], 1)
            act.copy(tsl[1][:, :, :], bank[5][:, 0:3 * P].rearrange("p (a t) -> p a t", a=3)).then_inc(tsl_sb[1], 1)
            with act.Fori(0, SPREADS // 4) as i:
                for m in range(4):
                    take_spread(1, 4 * i + m, m)

            act.wait_ge(spread_sb[1], SPREADS)
            def v_halves(i, peeled):
                for r in range(VRING):
                    c = VRING * i + r
                    if not (peeled and r < 2):
                        act.wait_ge(v_mm, VBLK * (c - 1))
                    act.copy(chi[r % 2][:, :, :], spread[:, :, bass.ds(c, 1), :].rearrange("p a o t -> p a (o t)"))\
                        .then_inc(chi_ready, 1)
                    act.wait_ge(v_landed[r], 16 * (i + 1))
                    for b in range(VBLK):
                        if not (peeled and r == 0):
                            act.wait_ge(v_mm, VBLK * c + b - VUNITS + 1)
                        act.copy(vhi[b][:, :], vraw[r][:, b * VCOL:(b + 1) * VCOL]).then_inc(vhi_ready, 1)

            v_halves(0, True)
            with act.Fori(1, TURNS) as i:
                v_halves(i, False)

            act.wait_ge(peer_done, TT * VBLK)
            norm_sums("ple")
            take_hi("ple")

            def sigmoid_out(group, parity):
                act.wait_ge(mm_done["gate"], 2 * group + 2)
                if not (isinstance(group, int) and group == 0):
                    act.wait_ge(ple_added, group)
                act.activation(sig[parity][:, :], bank[parity][:, :], ACT.Sigmoid).then_inc(evac["gate"], 1)

            run("gate", sigmoid_out)
            act.wait_ge(ple_added, NG["gate"])
            norm_sums("fin")

        @block.vector
        def _(dve):
            st = Steps(dve, dve_step)

            def normed(name, turn):
                dve.wait_ge(norm_sq[name], TT)
                dve.tensor_scalar(ssq[:, :], ssq[:, :], 1.0 / D, EPS, ALU.mult, ALU.add)\
                    .then_inc(norm_root[name], 1)
                dve.wait_ge(norm_root[name], 2)
                st.did(dve.reciprocal(rstd[:, :], rstd[:, :]))
                dve.wait_ge(gain_in, 16 * (turn + 1))
                st.wait()
                for tt in range(TT):
                    dve.scalar_tensor_tensor(out=xn[:, tt, :], in0=hres[:, tt, :], scalar=rstd[:, tt:tt + 1],
                                             in1=gain[:, :], op0=ALU.mult, op1=ALU.mult).then_inc(norm_done[name], 1)

            def take_lo(name):
                for b in range(8):
                    tt, kb = b // 4, b % 4
                    dve.wait_ge(tr_hi[name], b + 1)
                    dst = (slice(None), slice(4 * kb, 4 * kb + 4), slice(tt * P, (tt + 1) * P))
                    dve.tensor_tensor(xtlo[dst], bank[2 + b % 4][:, :].rearrange("p (a t) -> p a t", a=4),
                                      xthi[dst].bitcast(fp32), ALU.subtract).then_inc(tr_lo[name], 1)

            def run(stage, take):
                def split_lo(i, r):
                    dve.wait_ge(hi_ready[stage], RING * i + r + 1)
                    dve.tensor_tensor(wlo[r % 2][:, :, :], raw[r][:, :, :], whi[r % 2][:, :, :].bitcast(fp32),
                                      ALU.subtract).then_inc(lo_ready[stage], 1)

                def turn(i, peeled):
                    split_lo(i, 0)
                    if not peeled and take:
                        take(2 * i - 1, 1)
                    split_lo(i, 1)
                    split_lo(i, 2)
                    if take:
                        take(2 * i, 0)
                    split_lo(i, 3)

                turns = NG[stage] // 2
                turn(0, True)
                with dve.Fori(1, turns) as i:
                    turn(i, False)
                if take:
                    take(2 * turns - 1, 1)

            normed("mix", 0)
            take_lo("mix")
            dve.wait_ge(small_tr, 2)
            dve.tensor_copy(post[:, :], bank[6][:, 0:CMP_LEN]).then_inc(small_sb, 1)
            dve.tensor_copy(ongt[:, :], bank[6][:, CMP_LEN:CMP_LEN + NH]).then_inc(small_sb, 1)
            dve.wait_ge(r_mm, 1)
            dve.tensor_copy(rvec[:, :], bank[7][0:NH, 0:RLEN]).then_inc(r_sb, 1)
            dve.wait_ge(gate_hi, 1)
            dve.tensor_tensor(wglo[:, :, :], wg[:, :, :], wghi[:, :, :].bitcast(fp32), ALU.subtract)\
                .then_inc(gate_lo, 1)
            run("in", None)
            for n in range(len(V_UNITS) // 2):
                dve.wait_ge(vt_mm, n + 1)
                u = V_UNITS[2 * n]
                dve.tensor_copy(pr[:, u:u + 2, :], bank[2 + n % 4][:, :].rearrange("p (u t) -> p u t", u=2))\
                    .then_inc(vt_sb, 1)
            dve.wait_ge(gate_tr, 1)
            dve.tensor_copy(gates[:, :, :], bank[7][:, SEQ:SEQ + TT * GATES].rearrange("p (t g) -> p t g", t=TT))\
                .then_inc(gate_sb, 1)

            def biased(c):
                _, _, _, bh, _, kind, _, _, _ = CALLS[c]
                dve.wait_ge(s_score, c + 1)
                if c >= 2:
                    dve.wait_ge(s_prob, 2 * (c - 1))
                if kind == "full":
                    w, w0 = RLEN, P
                    spans = [(slice(0, RLEN), bias[:, bh, :])]
                else:
                    w, w0 = NCMP0 + NCMP, NCMP0
                    spans = [(slice(0, w0), bias[:, bh, CMP_LEN - 1:P:CMP_STRIDE]),
                             (slice(w0, w), bias[:, bh, P + CMP_LEN - 1:RLEN:CMP_STRIDE])]
                for cols, b in spans:
                    st.did(dve.scalar_tensor_tensor(out=sc[c % 2][:, cols], in0=bank[2 + c % 2][:, cols], scalar=SCALE,
                                                    in1=b, op0=ALU.mult, op1=ALU.add))
                st.wait()
                for tt, cols in ((0, slice(0, w0)), (1, slice(w0, w))):
                    dve.tensor_reduce(negmax[c % 2][:, tt:tt + 1], sc[c % 2][:, cols], AX.X, ALU.max, negate=True)\
                        .then_inc(s_biased, 1)

            def scaled_identity(c):
                _, _, _, _, _, kind, gate, _, _ = CALLS[c]
                dve.wait_ge(s_prob, 2 * c + 2)
                r = rz[c % 2]
                st.did(dve.reciprocal(r[:, :], zsum[c % 2][:, :]))
                st.wait()
                if gate is not None:
                    st.did(dve.tensor_tensor(r[:, :], r[:, :], gates[:, :, gate], ALU.mult))
                    st.wait()
                if kind == "cmp":
                    st.did(dve.tensor_tensor(r[:, 0:1], r[:, 0:1], valid[:, :], ALU.mult))
                    st.wait()
                if c >= 2:
                    dve.wait_ge(s_pt, c - 1)
                for tt in range(TT):
                    dve.tensor_scalar(diag[c % 2][:, tt, :], ident[:, :], r[:, tt:tt + 1], None, ALU.mult)\
                        .then_inc(s_diag, 1)

            dve.wait_ge(bias_in, 32)
            dve.wait_ge(const_ready, 4)
            dve.wait_ge(gate_sb, 1)
            for s in range(NC_ + 1):
                if s < NC_:
                    biased(s)
                if s >= 1:
                    scaled_identity(s - 1)
                if s == CMP_STEP + CMP_PARTS:
                    dve.wait_ge(cmp_mm, 1)
                    dve.tensor_copy(ksb[:, 0, :], bank[0][0:KV * NCMP, 0:HD]).then_inc(cmp_sb, 1)
                    dve.tensor_copy(ksb[:, 1, :], bank[1][0:KV * NCMP, 0:HD]).then_inc(cmp_sb, 1)
                if s == CMP_STEP + CMP_PARTS + 2:
                    dve.wait_ge(cmp_tr, 1)
                    for kv, dst in enumerate((kct, vct)):
                        dve.tensor_copy(dst[:, :, :], bank[0][:, (kv + 1) * P:(kv + 1) * P + KV * NCMP]
                                        .rearrange("p (g n) -> p g n", g=KV)).then_inc(cmp_sb, 1)
                if s == CMP_STEP + CMP_PARTS + 4:
                    dve.wait_ge(cmp_tr, 2)
                    dve.tensor_copy(vcm[0:NCMP, :, :],
                                    bank[1][0:NCMP, P:P + KV * HD].rearrange("p (g d) -> p g d", g=KV)).then_inc(cmp_sb, 1)
            for n, (a, b) in enumerate(GROUPS):
                dve.wait_ge(g_sum, n + 1)
                dve.tensor_scalar(orms[:, n, :], bank[2 + n][:, 0:SEQ], 1.0 / ((b - a) * HD), EPS, ALU.mult, ALU.add)\
                    .then_inc(g_root, 1)
            dve.wait_ge(g_rstd, 1)
            st.did(dve.reciprocal(orms[:, :, :], orms[:, :, :]))
            st.wait()
            for n, (a, b) in enumerate(GROUPS):
                for h in range(a, b):
                    dve.scalar_tensor_tensor(out=ysc[:, h, :], in0=ot[:, h, :], scalar=ongt[:, h:h + 1],
                                             in1=orms[:, n, :], op0=ALU.mult, op1=ALU.mult).then_inc(y_ready, 1)
                dve.wait_ge(y_hi, n + 1)
                dve.tensor_tensor(xtlo[:, a:b, :], ysc[:, a:b, :], xthi[:, a:b, :].bitcast(fp32), ALU.subtract)\
                    .then_inc(y_lo, 1)

            def add_mixer(group, parity):
                dve.wait_ge(mm_done["out"], 2 * group + 2)
                cols = bass.ds(group * CHUNK_C, CHUNK_C)
                dve.tensor_tensor(hres[:, :, cols], hres[:, :, cols],
                                  bank[parity][:, :].rearrange("p (t c) -> p t c", t=TT), ALU.add)\
                    .then_inc(evac["out"], 1)

            run("out", add_mixer)
            dve.wait_ge(evac["out"], NG["out"])
            normed("ffn", 1)
            take_lo("ffn")
            run("wq", None)

            def route(s, b, peeled):
                if not peeled:
                    dve.wait_ge(gate_exp, s)
                st.did(dve.tensor_copy(s1[:, :, :], scores[:, bass.ds(s, 1), :, :].rearrange("p o c k -> p (o c) k")))
                st.wait_apart()
                for c in range(2):
                    st.did(dve.max(top[:, c, 0:8], s1[:, c, :]))
                st.wait_apart()
                for c in range(2):
                    st.did(dve.max_index(topi[:, c, 0:8], top[:, c, 0:8], s1[:, c, :]))
                    st.did(dve.match_replace(s2[:, c, :], top[:, c, 0:8], s1[:, c, :], TAKEN))
                st.wait_apart()
                for c in range(2):
                    st.did(dve.max(top[:, c, 8:16], s2[:, c, :]))
                st.wait_apart()
                for c in range(2):
                    st.did(dve.max_index(topi[:, c, 8:16], top[:, c, 8:16], s2[:, c, :]))
                st.did(dve.tensor_tensor(cand[:, :, :], top[:, 0, :, None].broadcast_to([P, TOPK, TOPK]),
                                         top[:, 1, None, :].broadcast_to([P, TOPK, TOPK]), ALU.add))
                st.wait()
                st.did(dve.tensor_copy(topf[:, :, :], topi[:, :, :]))
                c1 = cand[:, :, :].rearrange("p a b -> p (a b)")
                c2 = cand2[:, :, :].rearrange("p a b -> p (a b)")
                st.did(dve.max(best[:, 0:8], c1))
                st.wait_apart()
                st.did(dve.max_index(bestj[:, 0:8], best[:, 0:8], c1))
                st.did(dve.match_replace(c2, best[:, 0:8], c1, TAKEN))
                st.did(dve.tensor_scalar(nbest[:, :], best[:, 0:1], -1.0, None, ALU.mult))
                st.wait_apart()
                st.did(dve.max(best[:, 8:16], c2))
                st.wait_apart()
                st.did(dve.max_index(bestj[:, 8:16], best[:, 8:16], c2))
                st.wait()
                st.did(dve.tensor_scalar(bidx[:, 0, :], bestj[:, :], 4, None, ALU.logical_shift_right))
                st.did(dve.tensor_scalar(bidx[:, 1, :], bestj[:, :], TOPK - 1, None, ALU.bitwise_and))
                st.wait()
                slots = bass.ds(s * TOPK, TOPK)
                for c in range(2):
                    st.did(dve.tensor_tensor(pick[:, :, :], bidx[:, c, :, None].broadcast_to([P, TOPK, TOPK]),
                                             iota[:, None, 0:TOPK].broadcast_to([P, TOPK, TOPK]), ALU.is_equal))
                    st.wait()
                    st.did(dve.tensor_tensor(pick[:, :, :], pick[:, :, :],
                                             topf[:, c, None, :].broadcast_to([P, TOPK, TOPK]), ALU.mult))
                    st.wait()
                    st.did(dve.tensor_reduce(slot_idx[:, c, slots], pick[:, :, :], AX.X, ALU.add))
                    st.wait()
                dve.scalar_tensor_tensor(out=expert[b][:, :], in0=slot_idx[:, 0, slots], scalar=float(NKEYS),
                                         in1=slot_idx[:, 1, slots], op0=ALU.mult, op1=ALU.add).then_inc(routed, 1)
                dve.wait_ge(routed, s + 1)
                st.did(dve.tensor_scalar(slot_row[:, slots], expert[b][:, :], float(QUARTERS), float(QUARTERS - 1),
                                         ALU.mult, ALU.add))

            ROUTE_STEPS = 1 + 2 + 4 + 2 + 3 + 2 + 3 + 1 + 1 + 2 + 6 + 1

            def tile1_hots(i, m, peeled):
                q = 4 * i + m
                if not peeled:
                    dve.wait_ge(spread_mm[1], q - 3)
                if m % 2:
                    dve.tensor_tensor(hot1[1][m][:, :, :], iota[:, None, :].broadcast_to([P, TOKB, NKEYS]),
                                      tsl[1][:, 0, bass.ds(TOKB * q, TOKB)][:, :, None]
                                      .broadcast_to([P, TOKB, NKEYS]), ALU.is_equal).then_inc(hot2_ready, 1)
                for a in range(TOKB):
                    t = TOKB * q + a
                    dve.tensor_scalar(hot2[1][m][:, a, :], iota[:, :], tsl[1][:, 1, bass.ds(t, 1)],
                                      tsl[1][:, 2, bass.ds(t, 1)], ALU.is_equal, ALU.mult).then_inc(hot2_ready, 1)

            def use_rows(turn, b, tt):
                s = 2 * turn + b
                for k in range(TOPK):
                    dve.wait_ge(fetched[k % GRING], (s * (TOPK // GRING) + k // GRING + 1) * 16)
                    r = rows[k % GRING]
                    dve.scalar_tensor_tensor(out=r[:, :], in0=r[:, :], scalar=1.0, in1=xn[:, tt, :], op0=ALU.mult,
                                             op1=ALU.mult, accum_out=dots[b][:, k:k + 1]).then_inc(eaten, 1)
                dve.wait_ge(eaten, (s + 1) * TOPK)
                dve.wait_ge(gate_exp, s + 1)
                dve.reciprocal(gsum[b][:, :], gsum[b][:, :]).then_inc(dots_ready, 1)
                dve.wait_ge(gelu_ready, s + 1)
                dve.scalar_tensor_tensor(out=slot_coef[:, bass.ds(s * TOPK, TOPK)], in0=gel[b][:, :],
                                         scalar=gsum[b][:, :], in1=gexp[b][:, :], op0=ALU.mult, op1=ALU.mult)\
                    .then_inc(coef_ready, 1)

            def peer_pair(i, tt, last=False):
                for b in range(2):
                    if b == 0 or not last:
                        route(2 * i + 1 + b, 1 - b, False)
                    use_rows(i, b, tt)

            dve.wait_ge(sc_sb, 8)
            route(0, 0, True)
            with dve.Fori(0, HALF) as i:
                st.enter(i, 2 * ROUTE_STEPS)
                peer_pair(i, 0)
            st.leave(HALF)
            with dve.Fori(HALF, PAIRS - 1) as i:
                st.enter(i - HALF, 2 * ROUTE_STEPS)
                peer_pair(i, 1)
            st.leave(PAIRS - 1 - HALF)
            peer_pair(PAIRS - 1, 1, last=True)
            dve.wait_ge(tsl_sb[1], 1)
            for m in range(4):
                tile1_hots(0, m, True)
            with dve.Fori(1, SPREADS // 4) as i:
                for m in range(4):
                    tile1_hots(i, m, False)

            def v_turn(i, tt, peeled):
                for r in range(VRING):
                    c = VRING * i + r
                    dve.wait_ge(chi_ready, c + 1)
                    dve.tensor_tensor(clo[r % 2][:, :, :], spread[:, :, bass.ds(c, 1), :].rearrange("p a o t -> p a (o t)"),
                                      chi[r % 2][:, :, :].bitcast(fp32), ALU.subtract).then_inc(clo_ready, 1)
                    for b in range(VBLK):
                        dve.wait_ge(vhi_ready, VBLK * c + b + 1)
                        dve.tensor_tensor(vlo[b][:, :], vraw[r][:, b * VCOL:(b + 1) * VCOL],
                                          vhi[b][:, :].bitcast(fp32), ALU.subtract).then_inc(vlo_ready, 1)
                    for n in (2 * r, 2 * r + 1):
                        dve.wait_ge(v_fetched[n], 16 * (i + 1))
                        if not (peeled and n == 0):
                            dve.wait_ge(v_used, GRING * i + n)
                        cols = hres[:, tt, VBLK * VCOL:D]
                        dve.scalar_tensor_tensor(out=cols, in0=vrow[n][:, :], scalar=slot_coef[:, bass.ds(GRING * i + n, 1)],
                                                 in1=cols, op0=ALU.mult, op1=ALU.add).then_inc(v_used, 1)

            v_turn(0, 0, True)
            with dve.Fori(1, TURNS // TT) as i:
                v_turn(i, 0, False)
            with dve.Fori(TURNS // TT, TURNS) as i:
                v_turn(i, 1, False)
            dve.wait_ge(v_used, TT * SLOTS)
            dve.wait_ge(v_mm, NKEYS * VBLK)
            for tt in range(TT):
                for b in range(VBLK):
                    cols = hres[:, tt, b * VCOL:(b + 1) * VCOL]
                    dve.tensor_tensor(cols, cols, bank[tt * VBLK + b][:, :], ALU.add).then_inc(peer_done, 1)
            dve.wait_ge(peer_done, TT * VBLK)

            normed("ple", 2)
            take_lo("ple")

            def add_ple(group, parity):
                dve.wait_ge(evac["gate"], group + 1)
                cols = bass.ds(group * CHUNK_C, CHUNK_C)
                g = sig[parity][:, :].rearrange("p (t c) -> p t c", t=TT)
                st.did(dve.tensor_tensor(g, g, pp[:, :, cols], ALU.mult))
                st.wait()
                dve.tensor_tensor(hres[:, :, cols], hres[:, :, cols], g, ALU.add).then_inc(ple_added, 1)

            def run_gate():
                stage = "gate"

                def split_lo(i, r):
                    dve.wait_ge(hi_ready[stage], RING * i + r + 1)
                    dve.tensor_tensor(wlo[r % 2][:, :, :], raw[r][:, :, :], whi[r % 2][:, :, :].bitcast(fp32),
                                      ALU.subtract).then_inc(lo_ready[stage], 1)

                split_lo(0, 0)
                split_lo(0, 1)
                split_lo(0, 2)
                add_ple(0, 0)
                split_lo(0, 3)
                with dve.Fori(1, NG[stage] // 2) as i:
                    st.enter(i - 1, 2)
                    split_lo(i, 0)
                    add_ple(2 * i - 1, 1)
                    split_lo(i, 1)
                    split_lo(i, 2)
                    add_ple(2 * i, 0)
                    split_lo(i, 3)
                st.leave(NG[stage] // 2 - 1)
                add_ple(NG[stage] - 1, 1)

            dve.wait_ge(pp_in, 16)
            run_gate()
            normed("fin", 3)

        @block.tensor
        def _(pe):
            def transposes(name):
                pe.wait_ge(norm_done[name], TT)
                for b in range(8):
                    tt, kb = b // 4, b % 4
                    if b >= 4:
                        pe.wait_ge(tr_lo[name], b - 3)
                    for a in range(4):
                        k = 4 * kb + a
                        last = pe.transpose(bank[2 + b % 4][:, a * P:(a + 1) * P], xn[:, tt, k * P:(k + 1) * P],
                                            ident[:, :])
                    last.then_inc(tr_done[name], 1)

            def chunk(stage, i, r, peeled):
                feature_major = stage in ("in", "wq")
                acc = bank[r // 2]
                pe.wait_ge(lo_ready[stage], RING * i + r + 1)
                if r % 2 == 0 and not peeled:
                    pe.wait_ge(evac[stage], 2 * i + r // 2 - 1)
                for k in range(CHUNK_K):
                    kk = (r % 2) * CHUNK_K + k
                    for u in range(2):
                        cols = slice(u * P, (u + 1) * P)
                        start = r % 2 == 0 and k == 0 and u == 0
                        stop = r % 2 == 1 and k == CHUNK_K - 1
                        hi, lo = whi[r % 2], wlo[r % 2]
                        dst = acc[:, u * SEQ:(u + 1) * SEQ]
                        if feature_major:
                            parts = [(hi[:, k, cols], xthi[:, kk, :]), (hi[:, k, cols], xtlo[:, kk, :]),
                                     (lo[:, k, cols], xthi[:, kk, :])]
                        else:
                            parts = [(xthi[:, kk, cols], hi[:, k, :]), (xthi[:, kk, cols], lo[:, k, :]),
                                     (xtlo[:, kk, cols], hi[:, k, :])]
                        for n, (a, b) in enumerate(parts):
                            last = pe.matmul(dst, a, b, start=start and n == 0, stop=stop and n == 2,
                                             skip_group_check=True)
                last.then_inc(mm_done[stage], 1)

            def run(stage):
                for r in range(RING):
                    chunk(stage, 0, r, True)
                with pe.Fori(1, NG[stage] // 2) as i:
                    for r in range(RING):
                        chunk(stage, i, r, False)

            pe.wait_ge(const_ready, 4)
            transposes("mix")
            pe.wait_ge(small_in, 80)
            pe.transpose(bank[6][:, 0:CMP_LEN], posn[:, :], ident[0:CMP_LEN, 0:CMP_LEN]).then_inc(small_tr, 1)
            pe.transpose(bank[6][:, CMP_LEN:CMP_LEN + NH], ongn[:, :], ident[0:NH, 0:NH]).then_inc(small_tr, 1)
            pe.matmul(bank[7][0:NH, 0:RLEN], tabl[:, 0:NH], tabl[:, NH:], start=True, stop=True).then_inc(r_mm, 1)
            pe.wait_ge(tr_lo["mix"], 8)
            run("in")
            pe.wait_ge(gate_lo, 1)
            pe.wait_ge(r_sb, 1)
            for k in range(KT):
                for n, (a, b) in enumerate([(wghi, xthi), (wghi, xtlo), (wglo, xthi)]):
                    last = pe.matmul(bank[7][0:GATES, 0:SEQ], a[:, k, :], b[:, k, :],
                                     start=k == 0 and n == 0, stop=k == KT - 1 and n == 2)
            last.then_inc(gate_mm, 1)
            pe.wait_ge(evac["in"], NG["in"])
            for n in range(len(V_UNITS) // 2):
                if n >= 4:
                    pe.wait_ge(vt_sb, n - 3)
                for a in range(4):
                    u, tt = V_UNITS[2 * n + a // 2], a % 2
                    last = pe.transpose(bank[2 + n % 4][:, a * P:(a + 1) * P], pr[:, u, tt * P:(tt + 1) * P],
                                        ident[:, :])
                last.then_inc(vt_mm, 1)
            pe.wait_ge(gate_sig, 1)
            for tt in range(TT):
                last = pe.transpose(bank[7][:, SEQ + tt * GATES:SEQ + (tt + 1) * GATES],
                                    gatest[:, tt * P:(tt + 1) * P], ident[0:GATES, 0:GATES])
            last.then_inc(gate_tr, 1)

            def score(c):
                q, k, _, _, _, kind, _, _, _ = CALLS[c]
                if c >= 2:
                    pe.wait_ge(s_biased, 2 * (c - 1))
                dst = bank[2 + c % 2]
                if kind == "full":
                    pe.matmul(dst[:, 0:P], pr[:, q, 0:P], pr[:, k, 0:P], start=True, stop=True)
                    last = pe.matmul(dst[:, P:RLEN], pr[:, q, P:SEQ], pr[:, k, :], start=True, stop=True)
                else:
                    pe.matmul(dst[:, 0:NCMP0], pr[:, q, 0:P], kct[:, k, 0:NCMP0], start=True, stop=True)
                    last = pe.matmul(dst[:, NCMP0:NCMP0 + NCMP], pr[:, q, P:SEQ], kct[:, k, :], start=True, stop=True)
                last.then_inc(s_score, 1)

            def transpose_probs(c):
                kind = CALLS[c][5]
                pe.wait_ge(s_diag, 2 * c + 2)
                if c >= 2:
                    pe.wait_ge(s_pts, c - 1)
                dst, pr_, dg = bank[4 + c % 2], pb[c % 3], diag[c % 2]
                if kind == "full":
                    pe.matmul(dst[:, 0:P], pr_[:, 0:P], dg[:, 0, :], start=True, stop=True)
                    pe.matmul(dst[:, P:2 * P], pr_[:, P:2 * P], dg[:, 1, :], start=True, stop=True)
                    last = pe.matmul(dst[:, 2 * P:RLEN], pr_[:, 2 * P:RLEN], dg[:, 1, :], start=True, stop=True)
                else:
                    pe.matmul(dst[0:NCMP0, 0:P], pr_[:, 0:NCMP0], dg[:, 0, :], start=True, stop=True)
                    last = pe.matmul(dst[0:NCMP, P:SEQ], pr_[:, NCMP0:NCMP0 + NCMP], dg[:, 1, :], start=True, stop=True)
                last.then_inc(s_pt, 1)

            def values(c):
                _, _, v, _, h, kind, _, first, final = CALLS[c]
                pe.wait_ge(s_pts, c + 1)
                if kind == "cmp":
                    pe.wait_ge(cmp_sb, 5)
                n = HEAD_ORD[h]
                if first and n >= 2:
                    pe.wait_ge(s_ot, n - 1)
                dst, pt = bank[6 + n % 2], pts[c % 2]
                if kind == "full":
                    pe.matmul(dst[:, 0:SEQ], pr[:, v, 0:P], pt[:, 0:SEQ], start=first, stop=False,
                              skip_group_check=True)
                    last = pe.matmul(dst[:, P:SEQ], pr[:, v, P:SEQ], pt[:, SEQ:RLEN], start=False, stop=final,
                                     skip_group_check=True)
                else:
                    pe.matmul(dst[:, 0:P], vcm[0:NCMP0, v, :], pt[0:NCMP0, 0:P], start=False, stop=False,
                              skip_group_check=True)
                    last = pe.matmul(dst[:, P:SEQ], vcm[0:NCMP, v, :], pt[0:NCMP, P:SEQ], start=False, stop=final,
                                     skip_group_check=True)
                last.then_inc(s_pv, 1)

            pe.wait_ge(vt_sb, len(V_UNITS) // 2)
            pe.wait_ge(gate_sb, 1)
            for s in range(NC_ + 3):
                if s < NC_:
                    if CALLS[s][5] == "cmp":
                        pe.wait_ge(cmp_sb, 3)
                    score(s)
                if 0 <= s - 2 < NC_:
                    transpose_probs(s - 2)
                if 0 <= s - 3 < NC_:
                    values(s - 3)
                if CMP_STEP <= s < CMP_STEP + CMP_PARTS:
                    if s == CMP_STEP:
                        pe.wait_ge(wcmp_in, 32)
                        pe.wait_ge(xcmp_ready, 2 * KV)
                    per = CMP_LEN // CMP_PARTS
                    for l in range((s - CMP_STEP) * per, (s - CMP_STEP + 1) * per):
                        for kv in range(2):
                            last = pe.matmul(bank[kv][0:KV * NCMP, 0:HD],
                                             xcmp[:, kv, l, :, :].rearrange("p g n -> p (g n)"), wcmp[kv][:, l, :],
                                             start=l == 0, stop=l == CMP_LEN - 1, skip_group_check=True)
                    if l == CMP_LEN - 1:
                        last.then_inc(cmp_mm, 1)
                if s == CMP_STEP + CMP_PARTS + 1:
                    pe.wait_ge(cmp_sb, 2)
                    for kv in range(2):
                        last = pe.transpose(bank[0][:, (kv + 1) * P:(kv + 1) * P + KV * NCMP], ksb[:, kv, :],
                                            ident[0:KV * NCMP, 0:KV * NCMP])
                    last.then_inc(cmp_tr, 1)
                if s == CMP_STEP + CMP_PARTS + 3:
                    pe.wait_ge(cmp_sb, 4)
                    for g in range(KV):
                        last = pe.transpose(bank[1][0:NCMP, (g + 1) * P:(g + 2) * P], vct[:, g, :], ident[:, :])
                    last.then_inc(cmp_tr, 1)
            for n, (a, b) in enumerate(GROUPS):
                pe.wait_ge(g_sq, n + 1)
                for h in range(a, b):
                    last = pe.matmul(bank[2 + n][:, 0:SEQ], ones[:, :], osq[:, h, :], start=h == a, stop=h == b - 1)
                last.then_inc(g_sum, 1)
            pe.wait_ge(y_lo, 3)
            pe.wait_ge(cmp_sb, 5)
            run("out")
            transposes("ffn")
            pe.wait_ge(tr_lo["ffn"], 8)
            pe.wait_ge(evac["out"], NG["out"])
            run("wq")
            pe.wait_ge(keys_in, 16)
            for n in range(4):
                if n >= 2:
                    pe.wait_ge(kt_sb, n - 1)
                for a in range(4):
                    last = pe.transpose(bank[2 + n % 2][:, a * P:(a + 1) * P], keys[:, 4 * n + a, :], ident[:, :])
                last.then_inc(kt_mm, 1)
            pe.wait_ge(kt_sb, 4)
            pe.wait_ge(evac["wq"], NG["wq"])
            for n in range(8):
                tt, h0 = n // 4, 2 * (n % 4)
                if n >= 2:
                    pe.wait_ge(sc_sb, n - 1)
                for a in range(4):
                    hc = 2 * h0 + a
                    last = pe.matmul(bank[4 + n % 2][:, a * P:(a + 1) * P], qt[:, hc, tt * P:(tt + 1) * P],
                                     keyst[:, hc, :], start=True, stop=True)
                last.then_inc(sc_mm, 1)
            pe.wait_ge(p_in, 16)
            for k in range(PLE // P):
                for tt in range(TT):
                    last = pe.transpose(bank[6 + k][:, tt * P:(tt + 1) * P], ptile[:, tt, k * P:(k + 1) * P], ident[:, :])
                last.then_inc(pt2_mm, 1)
            pe.wait_ge(pt2_sb, PLE // P)
            pe.wait_ge(pproj_in, 16)
            for n in range(8):
                tt, cb = n // 4, n % 4
                if n >= 2:
                    pe.wait_ge(pp_sb, n - 1)
                for k in range(PLE // P):
                    last = pe.matmul(bank[2 + n % 2][:, :], ptt[:, k, tt * P:(tt + 1) * P],
                                     pproj[:, k, cb * 512:(cb + 1) * 512], start=k == 0, stop=k == PLE // P - 1)
                last.then_inc(pp_mm, 1)

            def transpose_slots(tt):
                pe.wait_ge(coef_ready, (tt + 1) * PEER_H)
                cols = slice(tt * SLOTS, (tt + 1) * SLOTS)
                for a, src in enumerate((slot_idx[:, 0, cols], slot_idx[:, 1, cols], slot_coef[:, cols])):
                    last = pe.transpose(bank[5][:, a * P:(a + 1) * P], src, ident[:, :])
                last.then_inc(tsl_mm[tt], 1)

            def spread_group(tt, i, m, peeled):
                q = HOTS[tt] * i + m
                if tt == 0:
                    pe.wait_ge(hot_ready, (TOKB + 1) * (q + 1))
                else:
                    pair = 2 * i + m // 2
                    if m % 2 == 0:
                        pe.wait_ge(hot1_ready, TOKB * (pair + 1))
                    pe.wait_ge(hot2_ready, (2 * TOKB + 1) * pair + (TOKB, 2 * TOKB + 1)[m % 2])
                if not peeled:
                    pe.wait_ge(spread_sb[tt], q + 1 - HOTS[tt])
                for a in range(TOKB):
                    last = pe.matmul(bank[SPREAD_BANK[m]][:, a * P:(a + 1) * P], hot2[tt][m][:, a, :],
                                     hot1[tt][m][:, a, :], start=True, stop=True)
                last.then_inc(spread_mm[tt], 1)

            for tt in range(TT):
                transpose_slots(tt)
                for m in range(HOTS[tt]):
                    spread_group(tt, 0, m, True)
                with pe.Fori(1, SPREADS // HOTS[tt]) as i:
                    for m in range(HOTS[tt]):
                        spread_group(tt, i, m, False)

            def v_products(i, first=False, final=False):
                for r in range(VRING):
                    c = VRING * i + r
                    pe.wait_ge(clo_ready, c + 1)
                    for b in range(VBLK):
                        pe.wait_ge(vlo_ready, VBLK * c + b + 1)
                        for tt in range(TT):
                            hi, lo = chi[r % 2][:, tt, :], clo[r % 2][:, tt, :]
                            for n, (x1, x2) in enumerate(((hi, vhi[b]), (hi, vlo[b]), (lo, vhi[b]))):
                                last = pe.matmul(bank[tt * VBLK + b][:, :], x1, x2[:, :],
                                                 start=first and r == 0 and n == 0,
                                                 stop=final and r == VRING - 1 and n == 2, skip_group_check=True)
                        last.then_inc(v_mm, 1)

            pe.wait_ge(spread_sb[1], SPREADS)
            v_products(0, first=True)
            with pe.Fori(1, TURNS - 1) as i:
                v_products(i)
            v_products(TURNS - 1, final=True)
            transposes("ple")
            pe.wait_ge(tr_lo["ple"], 8)
            run("gate")


NAMES = ["x", "p", "ln_mix", "w_in", "cmp_wk", "cmp_wv", "cmp_pos", "out_norm", "w_out", "rel_bias", "ln_ffn",
         "peer_wq", "peer_keys", "peer_u", "peer_v", "ln_ple", "ple_gate", "ple_proj", "ln_final"]


def kernel(**inputs):
    import concourse.bacc as bacc
    from concourse.bass_utils import run_bass_kernel_spmd as run

    nc = bacc.Bacc("TRN2", target_bir_lowering=False, num_devices=1)
    arrays, args = {}, []
    for name in NAMES:
        a = np.ascontiguousarray(inputs[name])
        arrays[f"{name}_dram"] = a
        args.append(nc.dram_tensor(f"{name}_dram", a.shape, mybir.dt.from_np(a.dtype), kind="ExternalInput").ap())
    arrays["table_dram"] = bias_table()
    args.append(nc.dram_tensor("table_dram", arrays["table_dram"].shape, mybir.dt.float32, kind="ExternalInput").ap())
    args.append(nc.dram_tensor("out_dram", (1, SEQ, D), mybir.dt.float32, kind="ExternalOutput").ap())
    build(nc, *args)
    r = run(nc, [arrays], core_ids=[0])
    return r.results[0]["out_dram"]
```

```python
import math

import numpy as np

import concourse.bass as bass
from concourse import mybir

SEQ, D, HD = 256, 2048, 128
P = 128
TT = SEQ // P
KT = D // P
A_H, B_H, C_H, KV = 6, 6, 4, 2
NH = A_H + B_H + C_H
GROUP = B_H // KV
GATES = 3 * B_H
CMP_LEN, CMP_STRIDE = 32, 16
NCMP = (SEQ - CMP_LEN) // CMP_STRIDE + 1
NCMP0 = (P - CMP_LEN) // CMP_STRIDE + 1
PEER_H, NKEYS, TOPK = 8, 128, 16
PLE = 256
BUCKETS, MAX_DIST = 32, 1024
EPS = 1e-6
SCALE = HD ** -0.5
NEG = -1e30
TAKEN = -3e38

QA, KA, VA = 0, A_H, 2 * A_H
QB = 3 * A_H
KC, VC = QB + B_H, QB + B_H + KV
KS, VS, KW, VW = VC + KV, VC + 2 * KV, VC + 3 * KV, VC + 4 * KV
QC = VW + KV
KCC, VCC = QC + C_H, QC + 2 * C_H
UNITS = VCC + C_H
GATE_COL = QC * P
V_UNITS = [*range(VA, VA + A_H), *range(VS, VS + KV), *range(VW, VW + KV), *range(VCC, VCC + C_H)]

CHUNK_K, CHUNK_C = 8, 256
RING = 4
GRING = 8
SLOTS = PEER_H * TOPK
QUARTERS = 4
VCOL = D // QUARTERS
VBLK = QUARTERS - 1
VRING = 4
VUNITS = 3
TOKB = 4
RLEN = 384


def bias_table():
    dist = 255 - np.arange(RLEN)
    d = np.maximum(dist, 0)
    exact = BUCKETS // 2
    logd = np.log(np.maximum(d, 1).astype(np.float32) / np.float32(exact))
    large = exact + (logd / np.float32(math.log(MAX_DIST / exact)) * np.float32(BUCKETS - exact)).astype(np.int32)
    bucket = np.where(d < exact, d, np.clip(large, exact, BUCKETS - 1))
    out = np.zeros((BUCKETS + 2, NH + RLEN), np.float32)
    out[BUCKETS, :A_H] = 1.0
    out[BUCKETS + 1, A_H:NH] = 1.0
    out[bucket, NH + np.arange(RLEN)] = 1.0
    count = (dist <= 128).astype(int) + (dist % 4 == 0) + (dist % 16 == 0)
    dilated = np.where((dist >= 0) & (count > 0), np.log(np.maximum(count, 1)), NEG)
    out[BUCKETS, NH:] = dilated
    out[BUCKETS + 1, NH:] = np.where(dist >= 0, 0.0, NEG)
    return out


def calls():
    out = []
    for h in range(A_H):
        out.append((QA + h, KA + h, VA + h, h, h, "full", None, True, True))
    for h in range(C_H):
        out.append((QC + h, KCC + h, VCC + h, A_H + B_H + h, A_H + B_H + h, "full", None, True, True))
    for h in range(B_H):
        g = h // GROUP
        out.append((QB + h, KS + g, VS + g, A_H + h, A_H + h, "full", 3 * h + 1, True, False))
        out.append((QB + h, KW + g, VW + g, A_H + h, A_H + h, "full", 3 * h + 2, False, False))
        out.append((QB + h, g, g, A_H + h, A_H + h, "cmp", 3 * h, False, True))
    return out


class Steps:

    def __init__(self, eng, sem):
        self.eng, self.sem, self.n, self.base = eng, sem, 0, 0

    def did(self, ins):
        ins.then_inc(self.sem, 1)
        self.n += 1

    def wait(self):
        self.eng.wait_ge(self.sem, self.base + self.n)

    def wait_apart(self):
        self.wait()
        self.eng.nop(nofuse=True)

    def enter(self, turn, per_turn):
        self.before, self.per_turn = self.n, per_turn
        self.base, self.n = self.before + turn * per_turn, 0

    def leave(self, turns):
        assert self.n == self.per_turn, (self.n, self.per_turn)
        self.base, self.n = 0, self.before + turns * self.per_turn


def build(nc, x, p, ln_mix, w_in, cmp_wk, cmp_wv, cmp_pos, out_norm, w_out, rel_bias, ln_ffn, peer_wq,
          peer_keys, peer_u, peer_v, ln_ple, ple_gate, ple_proj, ln_final, table, out):
    fp32, f32r, i32, u32 = mybir.dt.float32, mybir.dt.float32r, mybir.dt.int32, mybir.dt.uint32
    ALU, ACT, AX = mybir.AluOpType, mybir.ActivationFunctionType, mybir.AxisListType

    base = -(-nc.sbuf_base // 64) * 64
    size = {fp32: 4, f32r: 4, i32: 4, u32: 4}

    def at(name, offset, shape, dt=fp32):
        return nc.alloc_sbuf_tensor_at(name, shape, dt, offset=base + offset)

    def placer(start):
        cursor = [start]

        def place(name, shape, dt=fp32):
            o = cursor[0]
            cursor[0] += -(-int(np.prod(shape[1:])) * size[dt] // 32) * 32
            return at(name, o, shape, dt)
        return place, cursor

    KB = 1024
    hres = at("hres", 0, [P, TT, D])
    xn = at("xn", 16 * KB, [P, TT, D])
    gain = at("gain", 32 * KB, [P, D])
    bias = at("bias", 16 * KB, [P, NH, RLEN])
    raw = [at(f"raw{r}", (40 + 8 * r) * KB, [P, CHUNK_K, CHUNK_C]) for r in range(RING)]
    whi = [at(f"whi{b}", (72 + 8 * b) * KB, [P, CHUNK_K, CHUNK_C], f32r) for b in range(2)]
    wlo = [at(f"wlo{b}", (88 + 8 * b) * KB, [P, CHUNK_K, CHUNK_C], f32r) for b in range(2)]
    xthi = at("xthi", 104 * KB, [P, KT, SEQ], f32r)
    xtlo = at("xtlo", 120 * KB, [P, KT, SEQ], f32r)
    pr = at("pr", 136 * KB, [P, UNITS, SEQ])

    ot = at("ot", 104 * KB, [P, NH, SEQ])
    o_att = 88 * KB
    sc = [at(f"sc{b}", o_att + b * 1536, [P, RLEN]) for b in range(2)]
    pb = [at(f"pb{b}", o_att + 3072 + b * 1536, [P, RLEN]) for b in range(3)]
    gatest = at("gatest", o_att + 3072, [GATES, SEQ])
    pts = [at(f"pts{b}", o_att + 7680 + b * 1536, [P, RLEN]) for b in range(2)]
    diag = [at(f"diag{b}", o_att + 10752 + b * 1024, [P, TT, P]) for b in range(2)]
    wcmp = [at("wk_cmp", 72 * KB, [P, CMP_LEN, HD]), at("wv_cmp", 120 * KB, [P, CMP_LEN, HD])]
    osq = at("osq", 136 * KB, [P, A_H + C_H, SEQ])
    orms = at("orms", 146 * KB, [P, 3, SEQ])
    ysc = [at("ysc_dilated", 172 * KB, [P, A_H, SEQ]), at("ysc_moba", 178 * KB, [P, C_H, SEQ]),
           at("ysc_nsa", 150 * KB, [P, B_H, SEQ])]
    qt = at("qt", 136 * KB, [P, 2 * PEER_H, SEQ])
    keyst = at("keyst", 152 * KB, [P, 2 * PEER_H, NKEYS])
    scores = at("scores", 160 * KB, [P, TT * PEER_H, 2, NKEYS])
    keys = at("keys", 176 * KB, [P, 2 * PEER_H, HD])
    pproj = at("pproj", 40 * KB, [P, PLE // P, D])
    pp_made = at("pp_made", 56 * KB, [P, TT, D])
    ptile = at("ptile", 32 * KB, [P, TT, PLE])
    ptt = at("ptt", 34 * KB, [P, PLE // P, SEQ])
    spread = at("spread", 32 * KB, [P, TT, NKEYS, P])
    rows = [at(f"rows{r}", (96 + 8 * r) * KB, [P, D]) for r in range(GRING)]
    HOTS = [2, 4]
    o_spread = [190 * KB, 160 * KB]
    tsl = [at("tsl0", 198 * KB, [P, 3, P]), at("tsl1", 201 * KB, [P, 3, P])]
    hot1 = [[at(f"hot1_{t}_{b}", o_spread[t] + 2 * b * KB, [P, TOKB, NKEYS]) for b in range(HOTS[t])]
            for t in range(TT)]
    hot2 = [[at(f"hot2_{t}_{b}", o_spread[t] + 2 * (HOTS[t] + b) * KB, [P, TOKB, NKEYS]) for b in range(HOTS[t])]
            for t in range(TT)]
    vraw = [at(f"vraw{r}", (176 + 6 * r) * KB, [P, VBLK * VCOL]) for r in range(VRING)]
    vhi = [at(f"vhi{b}", (160 + 2 * b) * KB, [P, VCOL], f32r) for b in range(VUNITS)]
    vlo = [at(f"vlo{b}", (166 + 2 * b) * KB, [P, VCOL], f32r) for b in range(VUNITS)]
    chi = [at(f"chi{b}", (172 + b) * KB, [P, TT, P], f32r) for b in range(2)]
    clo = [at(f"clo{b}", (174 + b) * KB, [P, TT, P], f32r) for b in range(2)]
    vrow = [at(f"vrow{r}", (16 + 2 * r) * KB, [P, VCOL]) for r in range(GRING)]
    pp = at("pp", 136 * KB, [P, TT, D])
    sig = [at(f"sig{b}", (152 + 2 * b) * KB, [P, TT * CHUNK_C]) for b in range(2)]

    place, cursor = placer(184 * KB)
    vct = place("vct", [P, KV, NCMP])
    xcmp = place("xcmp", [P, 2, CMP_LEN, KV, NCMP])
    kct = place("kct", [P, KV, NCMP])
    wg = place("wg", [P, KT, GATES])
    wghi = place("wghi", [P, KT, GATES], f32r)
    wglo = place("wglo", [P, KT, GATES], f32r)
    gates = place("gates", [P, TT, GATES])
    ksb = at("ksb", cursor[0], [KV * NCMP, 2, HD])
    rvec = place("rvec", [NH, RLEN])
    tabl = place("tabl", [BUCKETS + 2, NH + RLEN])
    vcm = place("vcm", [P, KV, HD])
    assert cursor[0] <= 200 * KB, cursor[0]
    place, cursor = placer(184 * KB)
    s1 = place("s1", [P, 2, NKEYS])
    s2 = place("s2", [P, 2, NKEYS])
    cand = place("cand", [P, TOPK, TOPK])
    cand2 = place("cand2", [P, TOPK, TOPK])
    pick = place("pick", [P, TOPK, TOPK])
    assert cursor[0] <= 190 * KB

    place, cursor = placer(200 * KB)
    ident = place("ident", [P, P])
    ones = place("ones", [P, P])
    posn = at("posn", 200 * KB + 1024, [CMP_LEN, HD])
    ongn = at("ongn", 200 * KB + 1536, [NH, HD])
    slot_idx = place("slot_idx", [P, 2, TT * SLOTS])
    slot_row = place("slot_row", [P, TT * SLOTS], i32)
    slot_coef = place("slot_coef", [P, TT * SLOTS])
    post = place("post", [P, CMP_LEN])
    ongt = place("ongt", [P, NH])
    valid = place("valid", [P, 1])
    ssq = place("ssq", [P, TT])
    rstd = place("rstd", [P, TT])
    negmax = [place(f"negmax{b}", [P, TT]) for b in range(2)]
    zsum = [place(f"zsum{b}", [P, TT]) for b in range(2)]
    rz = [place(f"rz{b}", [P, TT]) for b in range(2)]
    top = place("top", [P, 2, TOPK])
    topi = place("topi", [P, 2, TOPK], u32)
    topf = place("topf", [P, 2, TOPK])
    best = place("best", [P, TOPK])
    bestj = place("bestj", [P, TOPK], u32)
    bidx = place("bidx", [P, 2, TOPK], u32)
    nbest = place("nbest", [P, 1])
    iota = place("iota", [P, NKEYS])
    expert = [place(f"expert{b}", [P, TOPK], i32) for b in range(2)]
    gsum = [place(f"gsum{b}", [P, 1]) for b in range(2)]
    gexp = [place(f"gexp{b}", [P, TOPK]) for b in range(2)]
    dots = [place(f"dots{b}", [P, TOPK]) for b in range(2)]
    gel = [place(f"gel{b}", [P, TOPK]) for b in range(2)]
    idx4 = place("idx4", [P, TOKB])
    vidx = [place(f"vidx{r}", [P, 1], i32) for r in range(GRING)]
    assert base + cursor[0] <= nc.sbuf_usable_end, (base + cursor[0], nc.sbuf_usable_end)

    SPREAD_BANK = [6, 7, 0, 1]
    bank = [nc.alloc_psum_tensor(f"bank{b}", [P, 512], fp32) for b in range(8)]
    rdram = nc.dram_tensor("bias_by_distance", (NH, P, RLEN), fp32, kind="Internal").ap()

    ppdram = nc.dram_tensor("p_projected", (P, TT, D), fp32, kind="Internal").ap()

    def sem(name):
        return nc.alloc_semaphore(name)

    dve_step, pool_step = sem("dve_step"), sem("pool_step")
    const_ready = sem("const_ready")
    x_in, small_in, keys_in = sem("x_in"), sem("small_in"), sem("keys_in")
    wg_in, wcmp_in, pproj_in = sem("wg_in"), sem("wcmp_in"), sem("pproj_in")
    gain_in = sem("gain_in")
    norms = ["mix", "ffn", "ple", "fin"]
    norm_sq = {n: sem(f"{n}_squared") for n in norms}
    norm_root = {n: sem(f"{n}_root") for n in norms}
    norm_done = {n: sem(f"{n}_normed") for n in norms}
    tr_done = {n: sem(f"{n}_transposed") for n in norms[:3]}
    tr_hi = {n: sem(f"{n}_xthi") for n in norms[:3]}
    tr_lo = {n: sem(f"{n}_xtlo") for n in norms[:3]}
    stages = ["in", "out", "wq", "gate"]
    landed = {s: [sem(f"{s}_landed{r}") for r in range(RING)] for s in stages}
    hi_ready = {s: sem(f"{s}_whi") for s in stages}
    lo_ready = {s: sem(f"{s}_wlo") for s in stages}
    mm_done = {s: sem(f"{s}_products") for s in stages}
    evac = {s: sem(f"{s}_evacuated") for s in stages}
    NG = {"in": UNITS * P // CHUNK_C, "out": D // CHUNK_C, "wq": D // CHUNK_C, "gate": D // CHUNK_C}
    small_tr, small_sb = sem("small_transposed"), sem("small_copied")
    r_mm, r_sb, r_out, bias_in = sem("r_mm"), sem("r_sb"), sem("r_out"), sem("bias_in")
    gate_hi, gate_lo, gate_mm, gate_sig = sem("gate_hi"), sem("gate_lo"), sem("gate_mm"), sem("gate_sig")
    gate_tr, gate_sb, cmp_tr = sem("gates_transposed"), sem("gates_copied"), sem("cmp_values_transposed")
    xcmp_ready, cmp_mm, cmp_sb = sem("xcmp_ready"), sem("cmp_mm"), sem("cmp_sb")
    vt_mm, vt_sb = sem("vt_mm"), sem("vt_sb")
    s_score, s_biased, s_prob, s_diag = sem("scores_ready"), sem("biased"), sem("probs"), sem("diag_ready")
    s_pt, s_pts, s_pv, s_ot = sem("probs_transposed"), sem("probs_t_copied"), sem("pv_done"), sem("head_out")
    g_sq, g_sum, g_root, g_rstd = sem("group_squares"), sem("group_sums"), sem("group_root"), sem("group_rstd")
    y_ready, y_hi, y_lo = sem("y_ready"), sem("y_hi"), sem("y_lo")
    kt_mm, kt_sb, sc_mm, sc_sb = sem("keys_transposed"), sem("keys_copied"), sem("key_scores"), sem("key_scores_copied")
    routed, gate_exp = sem("experts_chosen"), sem("gate_exp")
    fetched = [sem(f"rows_fetched{r}") for r in range(GRING)]
    eaten = sem("rows_used")
    dots_ready, gelu_ready, peer_done = sem("dots_ready"), sem("gelu_ready"), sem("peer_done")
    tsl_mm, tsl_sb = [[sem(f"{n}{t}") for t in range(TT)] for n in ("slots_transposed", "slots_copied")]
    hot_dist, hot_unit = sem("hot_distances"), sem("hot_units")
    hot_ready, hot1_ready = sem("tile0_one_hots"), sem("tile1_even_first_one_hots")
    hot2_ready, idx4_ready = sem("tile1_one_hots"), sem("indices_of_four_tokens")
    spread_mm, spread_sb = [[sem(f"{n}{t}") for t in range(TT)] for n in ("spread_products", "spread_copied")]
    v_landed = [sem(f"v_landed{r}") for r in range(VRING)]
    chi_ready, clo_ready, vhi_ready, vlo_ready = sem("chi_ready"), sem("clo_ready"), sem("vhi_ready"), sem("vlo_ready")
    v_mm = sem("v_products")
    vidx_ready, v_used = sem("vidx_ready"), sem("v_rows_used")
    v_fetched = [sem(f"v_rows_fetched{r}") for r in range(GRING)]
    coef_ready, pp_out, pp_in, p_in = sem("coef_ready"), sem("pp_out"), sem("pp_in"), sem("p_in")
    pt2_mm, pt2_sb, pp_mm, pp_sb = sem("p_transposed"), sem("p_copied"), sem("pp_mm"), sem("pp_sb")
    ple_added, out_sem = sem("ple_added"), sem("out_written")

    CALLS = calls()
    SCORE_ORDER = list(enumerate((0, 1, 4, 5, 2, 3, 6, 7)))
    EARLY_SCORES, LATE_SCORES = SCORE_ORDER[:4], SCORE_ORDER[4:]
    OVER_QUERIES = (136 - 96) // 8
    NC_ = len(CALLS)
    CMP_STEP, CMP_PARTS = 4, 4
    HEAD_ORD = {}
    for c, call in enumerate(CALLS):
        if call[7]:
            HEAD_ORD[call[4]] = len(HEAD_ORD)
    LAST = {c: call[4] for c, call in enumerate(CALLS) if call[8]}
    GROUPS = [(0, A_H), (A_H + B_H, NH), (A_H, A_H + B_H)]
    OUT_HI_STEP = (27, 29)
    NSA_PARTS = [(A_H, A_H + B_H // 2), (A_H + B_H // 2, A_H + B_H)]

    def y_count(n, end):
        return sum(b - a for a, b in GROUPS[:n]) + end - GROUPS[n][0]

    SIDE = A_H + C_H
    SUM_STEP, MEAN_STEP, ROOT_STEP, RECIP_STEP, SCALE_STEP = (13, 15), (14, 16), 17, (18, 19), (20, 23)
    PEER_STEPS = TT * PEER_H
    PAIRS = PEER_STEPS // 2
    HALF = PAIRS // TT
    SPREADS = P // TOKB
    PER_STEP = SPREADS // PEER_H
    TURNS = NKEYS // VRING

    def weights_of(stage):
        return {"in": w_in, "out": w_out, "wq": peer_wq, "gate": ple_gate}[stage]

    block = nc.Block()
    with block:
        @block.sync
        def _(sp):
            for tt in range(TT):
                sp.dma_start(hres[:, tt, :], x[0, tt * P:(tt + 1) * P, :]).then_inc(x_in, 16)
            sp.dma_start(gain[:, :], ln_mix[0:1, :].partition_broadcast(P)).then_inc(gain_in, 16)

            def stream(stage, ngroups, first_group, gap, after=None):
                w = weights_of(stage)
                cols = ngroups * CHUNK_C
                c0 = first_group * CHUNK_C + gap
                view = w[0, :, c0:c0 + cols].rearrange("(h k q) c -> q h k c", q=P, k=CHUNK_K)

                def turn(i, peeled):
                    for r in range(RING):
                        if not peeled:
                            sp.wait_ge(lo_ready[stage], (first_group // 2 + i) * RING + r - RING + 1)
                        elif after:
                            sp.wait_ge(lo_ready[after], 2 * NG[after] - RING + r + 1)
                        col = (2 * i + r // 2) * CHUNK_C
                        sp.dma_start(raw[r][:, :, :], view[:, r % 2, :, bass.ds(col, CHUNK_C)])\
                            .then_inc(landed[stage][r], 16)

                start = 0
                if first_group == 0:
                    turn(0, True)
                    start = 1
                if stage == "gate":
                    sp.wait_ge(pp_out, 16)
                    sp.dma_start(pp[:, :, :], ppdram).then_inc(pp_in, 16)
                with sp.Fori(start, ngroups // 2) as i:
                    turn(i, False)

            sp.dma_start(wg[:, :, :], w_in[0, :, GATE_COL:GATE_COL + GATES].rearrange("(k q) c -> q k c", q=P))\
                .then_inc(wg_in, 16)
            stream("in", QC // 2, 0, 0)
            stream("in", (UNITS - QC) // 2, QC // 2, GATES)
            sp.wait_ge(mm_done["in"], 2 * NG["in"])
            sp.wait_ge(gate_mm, 1)
            for w, sb in ((cmp_wk, wcmp[0]), (cmp_wv, wcmp[1])):
                sp.dma_start(sb[:, :, :], w[0].rearrange("l d e -> d l e")).then_inc(wcmp_in, 16)
            stream("out", NG["out"], 0, 0, after="in")
            sp.wait_ge(s_biased, 2 * NC_)
            sp.dma_start(gain[:, :], ln_ffn[0:1, :].partition_broadcast(P)).then_inc(gain_in, 16)
            sp.wait_ge(y_lo, 4)
            sp.dma_start(keys[:, :, :], peer_keys[0].rearrange("h c k d -> k (h c) d")).then_inc(keys_in, 16)
            stream("wq", NG["wq"], 0, 0, after="out")
            sp.wait_ge(norm_done["ffn"], 4 * TT)
            sp.wait_ge(lo_ready["wq"], 2 * NG["wq"] - 2)
            sp.dma_start(ptile[:, :, :], p[0, 0].rearrange("(t q) c -> q t c", q=P)).then_inc(p_in, 16)
            sp.dma_start(pproj[:, :, :], ple_proj[0].rearrange("(k q) c -> q k c", q=P)).then_inc(pproj_in, 16)
            sp.wait_ge(pp_sb, 8)
            sp.dma_start(ppdram, pp_made[:, :, :]).then_inc(pp_out, 16)
            sp.wait_ge(routed, PEER_STEPS)
            sp.wait_ge(spread_sb[0], SPREADS)
            vview = peer_v[0].rearrange("(c q) d -> q c d", q=P)

            def v_turn(i, peeled):
                for r in range(VRING):
                    if not peeled:
                        sp.wait_ge(vlo_ready, (VRING * i + r - VRING + 1) * VBLK)
                    sp.dma_start(vraw[r][:, :], vview[:, bass.ds(VRING * i + r, 1), 0:VBLK * VCOL]
                                 .rearrange("q o d -> q (o d)")).then_inc(v_landed[r], 16)

            v_turn(0, True)
            with sp.Fori(1, TURNS) as i:
                v_turn(i, False)
            sp.wait_ge(clo_ready, NKEYS)
            sp.dma_start(gain[:, :], ln_ple[0:1, :].partition_broadcast(P)).then_inc(gain_in, 16)
            stream("gate", NG["gate"], 0, 0)
            sp.wait_ge(norm_done["ple"], 4 * TT)
            sp.dma_start(gain[:, :], ln_final[None, :].partition_broadcast(P)).then_inc(gain_in, 16)
            for tt in range(TT):
                for half in range(2):
                    cols = slice(half * D // 2, (half + 1) * D // 2)
                    sp.wait_ge(norm_done["fin"], 4 * tt + 2 * (half + 1))
                    sp.dma_start(out[0, tt * P:(tt + 1) * P, cols], xn[:, tt, cols]).then_inc(out_sem, 16)
            sp.wait_ge(out_sem, 16 * 2 * TT)

        @block.gpsimd
        def _(pool):
            pool.memset(ident[:, :], 0.0).then_inc(pool_step, 1)
            pool.memset(valid[:, :], 1.0).then_inc(pool_step, 1)
            pool.memset(ones[:, :], 1.0).then_inc(const_ready, 1)
            pool.iota(iota[:, :], [[1, NKEYS]], base=0, channel_multiplier=0,
                      allow_small_or_imprecise_dtypes=True).then_inc(const_ready, 1)
            pool.wait_ge(pool_step, 2)
            pool.affine_select(out=ident[:, :], in_=ident[:, :], compare_op=ALU.not_equal, fill=1.0, base=0,
                               pattern=[[-1, P]], channel_multiplier=1).then_inc(const_ready, 1)
            pool.affine_select(out=valid[:, :], in_=valid[:, :], compare_op=ALU.is_ge, fill=0.0,
                               base=-(CMP_LEN - 1), pattern=[[0, 1]], channel_multiplier=1).then_inc(const_ready, 1)
            pool.dma_start(tabl[:, NH:], table[:, NH:]).then_inc(small_in, 16)
            pool.dma_start(tabl[BUCKETS:, 0:NH], table[BUCKETS:, 0:NH]).then_inc(small_in, 16)
            pool.dma_start(tabl[0:BUCKETS, 0:NH], rel_bias).then_inc(small_in, 16)
            pool.dma_start(posn[:, :], cmp_pos[0]).then_inc(small_in, 16)
            pool.dma_start(ongn[:, :], out_norm[0].rearrange("(h d) -> h d", d=HD)).then_inc(small_in, 16)
            def split_first_lo(stage):
                pool.wait_ge(hi_ready[stage], 1)
                pool.tensor_tensor(wlo[0][:, :, :], raw[0][:, :, :], whi[0][:, :, :].bitcast(fp32), ALU.subtract)\
                    .then_inc(lo_ready[stage], 1)

            split_first_lo("in")
            pool.wait_ge(r_sb, 1)
            pool.dma_start(rdram, rvec[:, None, :].broadcast_to([NH, P, RLEN])).then_inc(r_out, 16)
            pool.wait_ge(r_out, 16)
            pool.wait_ge(tr_lo["mix"], 8)
            pool.wait_ge(tr_hi["mix"], 8)
            shift, heads = [RLEN - 1, P], [P * RLEN, NH]
            tile1 = bass.AP(tensor=rdram.tensor, offset=P - 1, ap=[shift, heads, [1, SEQ]])
            tile0 = bass.AP(tensor=rdram.tensor, offset=SEQ - 1, ap=[shift, heads, [1, P]])
            pool.dma_start(bias[:, :, P:RLEN], tile1).then_inc(bias_in, 16)
            pool.dma_start(bias[:, :, 0:P], tile0).then_inc(bias_in, 16)

            pool.wait_ge(evac["in"], VC // 2 + 1)
            pool.wait_ge(small_sb, 2)
            for kv, unit in ((0, KC), (1, VC)):
                for g in range(KV):
                    a = pr[:, unit + g, :]
                    win = bass.AP(tensor=a.tensor, offset=a.offset, ap=[a.ap[0], [1, CMP_LEN], [CMP_STRIDE, NCMP]])
                    pool.tensor_tensor(xcmp[:, kv, :, g, :], win, post[:, :, None].broadcast_to([P, CMP_LEN, NCMP]),
                                       ALU.add).then_inc(xcmp_ready, 1)

            def fetch(pairs, peeled):
                for b in range(2):
                    pool.wait_ge(routed, pairs * 2 + b + 1)
                    for k in range(TOPK):
                        slot = k % GRING
                        if peeled and b == 0 and k == OVER_QUERIES:
                            pool.wait_ge(sc_mm, 8)
                        if not (peeled and b == 0 and k < GRING):
                            pool.wait_ge(eaten, (pairs * 2 + b) * TOPK + k - GRING + 1)
                        pool.nop(nofuse=True)
                        pool.indirect_dma_start(rows[slot][:, :], None, peer_u[0],
                                                bass.IndirectOffsetOnAxis(ap=expert[b][:, k:k + 1], axis=0))\
                            .then_inc(fetched[slot], 16)

            split_first_lo("wq")
            pool.wait_ge(mm_done["wq"], 2 * NG["wq"])
            fetch(0, True)
            with pool.Fori(1, PAIRS) as i:
                fetch(i, False)

            quarters = peer_v[0].rearrange("e (f c) -> (e f) c", f=QUARTERS)

            def v_fetch(i, peeled):
                for r in range(GRING):
                    if not peeled:
                        pool.wait_ge(v_used, GRING * i + r - GRING + 1)
                    pool.tensor_copy(vidx[r][:, :], slot_row[:, bass.ds(GRING * i + r, 1)]).then_inc(vidx_ready, 1)
                    pool.wait_ge(vidx_ready, GRING * i + r + 1)
                    pool.nop(nofuse=True)
                    pool.indirect_dma_start(vrow[r][:, :], None, quarters,
                                            bass.IndirectOffsetOnAxis(ap=vidx[r][:, :], axis=0))\
                        .then_inc(v_fetched[r], 16)

            pool.wait_ge(eaten, PEER_STEPS * TOPK)

            def even_first_hots(i, m, peeled):
                n = 2 * i + m // 2
                if not peeled:
                    pool.wait_ge(spread_mm[1], 4 * i + m - 3)
                if not (peeled and m == 0):
                    pool.wait_ge(hot1_ready, TOKB * n)
                pool.tensor_copy(idx4[:, :], tsl[1][:, 0, bass.ds((4 * i + m) * TOKB, TOKB)]).then_inc(idx4_ready, 1)
                pool.wait_ge(idx4_ready, n + 1)
                pool.nop(nofuse=True)
                for a in range(TOKB):
                    pool.tensor_scalar(hot1[1][m][:, a, :], iota[:, :], idx4[:, a:a + 1], None,
                                       ALU.is_equal).then_inc(hot1_ready, 1)

            pool.wait_ge(tsl_sb[1], 1)
            for m in (0, 2):
                even_first_hots(0, m, True)
            with pool.Fori(1, SPREADS // 4) as i:
                for m in (0, 2):
                    even_first_hots(i, m, False)
            v_fetch(0, True)
            with pool.Fori(1, TURNS) as i:
                v_fetch(i, False)
            split_first_lo("gate")

        @block.scalar
        def _(act):
            def norm_sums(name):
                act.activation(xn[:, 0, :], hres[:, 0, :], ACT.Square, accum_out=ssq[:, 0:1]).then_inc(norm_sq[name], 1)
                act.wait_ge(norm_root[name], 1)
                act.activation(rstd[:, :], ssq[:, :], ACT.Sqrt).then_inc(norm_root[name], 1)

            def take_hi(name):
                for b in range(8):
                    tt, kb = b // 4, b % 4
                    act.wait_ge(tr_done[name], b + 1)
                    act.copy(xthi[:, 4 * kb:4 * kb + 4, tt * P:(tt + 1) * P],
                             bank[2 + b % 4][:, :].rearrange("p (a t) -> p a t", a=4)).then_inc(tr_hi[name], 1)

            def split_hi(stage, turn, r, peeled):
                act.wait_ge(landed[stage][r], 16 * (turn + 1))
                if not (peeled and r < 2):
                    act.wait_ge(mm_done[stage], RING * turn + r - 1)
                act.copy(whi[r % 2][:, :, :], raw[r][:, :, :]).then_inc(hi_ready[stage], 1)

            def run(stage, take, presplit=0, beside_first=None, beside=None, after_splits=None):
                def turn(i, peeled, last=False):
                    if not peeled or presplit < 1:
                        split_hi(stage, i, 0, peeled)
                    if not peeled and take:
                        take(2 * i - 1, 1)
                    if not peeled or presplit < 2:
                        split_hi(stage, i, 1, peeled)
                    if peeled and beside_first:
                        beside_first()
                    if last and beside:
                        beside()
                    split_hi(stage, i, 2, peeled)
                    if take:
                        take(2 * i, 0)
                    split_hi(stage, i, 3, peeled)

                turns = NG[stage] // 2
                turn(0, True)
                with act.Fori(1, turns - 1) as i:
                    turn(i, False)
                turn(turns - 1, False, last=True)
                if after_splits:
                    after_splits()
                if take:
                    take(2 * turns - 1, 1)

            def copy_to(dst, stage):
                def take(group, parity):
                    act.wait_ge(mm_done[stage], 2 * group + 2)
                    act.copy(dst[:, bass.ds(2 * group, 2), :],
                             bank[parity][:, :].rearrange("p (u t) -> p u t", u=2)).then_inc(evac[stage], 1)
                return take

            act.wait_ge(x_in, 32)
            norm_sums("mix")
            split_hi("in", 0, 0, True)
            take_hi("mix")
            def gate_weights_hi():
                act.wait_ge(wg_in, 16)
                act.copy(wghi[:, :, :], wg[:, :, :]).then_inc(gate_hi, 1)

            run("in", copy_to(pr, "in"), presplit=1, beside_first=gate_weights_hi)
            act.wait_ge(gate_mm, 1)
            act.activation(gatest[:, :], bank[7][0:GATES, 0:SEQ], ACT.Sigmoid).then_inc(gate_sig, 1)

            def exps(c):
                w = RLEN if CALLS[c][5] == "full" else NCMP0 + NCMP
                w0 = P if CALLS[c][5] == "full" else NCMP0
                act.wait_ge(s_biased, 2 * c + 2)
                if c >= 3:
                    act.wait_ge(s_pt, c - 2)
                for tt, cols in ((0, slice(0, w0)), (1, slice(w0, w))):
                    act.activation(pb[c % 3][:, cols], sc[c % 2][:, cols], ACT.Exp, bias=negmax[c % 2][:, tt:tt + 1],
                                   accum_out=zsum[c % 2][:, tt:tt + 1]).then_inc(s_prob, 1)

            def copy_pt(c):
                act.wait_ge(s_pt, c + 1)
                if c >= 2:
                    act.wait_ge(s_pv, c - 1)
                rows_, w = (P, RLEN) if CALLS[c][5] == "full" else (NCMP, SEQ)
                act.copy(pts[c % 2][0:rows_, 0:w], bank[4 + c % 2][0:rows_, 0:w]).then_inc(s_pts, 1)

            def head_out(c):
                h = LAST[c]
                act.wait_ge(s_pv, c + 1)
                act.copy(ot[:, h, :], bank[6 + HEAD_ORD[h] % 2][:, 0:SEQ]).then_inc(s_ot, 1)
                n = HEAD_ORD[h]
                act.wait_ge(s_ot, n + 1)
                if n >= SIDE:
                    act.wait_ge(g_sum, 1)
                act.activation(osq[:, n % SIDE, :], ot[:, h, :], ACT.Square).then_inc(g_sq, 1)

            def y_halves(n, a, b):
                g0 = GROUPS[n][0]
                act.wait_ge(y_ready, y_count(n, b))
                act.copy(xthi[:, a:b, :], ysc[n][:, a - g0:b - g0, :]).then_inc(y_hi, 1)

            for s in range(NC_ + 4):
                if s < NC_:
                    exps(s)
                if 0 <= s - 2 < NC_:
                    copy_pt(s - 2)
                if s - 4 in LAST:
                    head_out(s - 4)
                if s in OUT_HI_STEP:
                    act.wait_ge(cmp_mm, 1)
                    split_hi("out", 0, OUT_HI_STEP.index(s), True)
                if s == ROOT_STEP:
                    act.wait_ge(g_root, 2)
                    act.activation(orms[:, 0:2, :], orms[:, 0:2, :], ACT.Sqrt).then_inc(g_rstd, 1)
                for n in range(2):
                    if s == SCALE_STEP[n] + 3:
                        y_halves(n, *GROUPS[n])
            act.wait_ge(g_root, 3)
            act.activation(orms[:, 2, :], orms[:, 2, :], ACT.Sqrt).then_inc(g_rstd, 1)
            for a, b in NSA_PARTS:
                y_halves(2, a, b)
            run("out", None, presplit=2)
            act.wait_ge(mm_done["out"], 2 * NG["out"] - 1)
            split_hi("wq", 0, 0, True)
            act.wait_ge(evac["out"], NG["out"])
            norm_sums("ffn")
            for n in range(4):
                act.wait_ge(kt_mm, n + 1)
                act.copy(keyst[:, 4 * n:4 * n + 4, :], bank[6 + n % 2][:, :].rearrange("p (a k) -> p a k", a=4))\
                    .then_inc(kt_sb, 1)
            take_hi("ffn")
            def route_exp(turn, b, peeled):
                s = 2 * turn + b
                act.wait_ge(routed, s + 1)
                act.activation(gexp[b][:, :], best[:, :], ACT.Exp, bias=nbest[:, :], accum_out=gsum[b][:, :])\
                    .then_inc(gate_exp, 1)

            def take_scores(order):
                for j, n in order:
                    act.wait_ge(sc_mm, j + 1)
                    act.copy(scores[:, 2 * n:2 * n + 2, :, :],
                             bank[4 + j % 4][:, :].rearrange("p (s c k) -> p s c k", s=2, c=2)).then_inc(sc_sb, 1)

            run("wq", copy_to(qt, "wq"), presplit=1, beside=lambda: take_scores(EARLY_SCORES),
                after_splits=lambda: route_exp(0, 0, True))
            take_scores(LATE_SCORES)

            def gelu(turn, b):
                act.wait_ge(dots_ready, 2 * turn + b + 1)
                act.activation(gel[b][:, :], dots[b][:, :], ACT.Gelu).then_inc(gelu_ready, 1)

            for k in range(PLE // P):
                act.wait_ge(pt2_mm, k + 1)
                act.copy(ptt[:, k, :], bank[6 + k][:, 0:SEQ]).then_inc(pt2_sb, 1)
            for n in range(8):
                act.wait_ge(pp_mm, n + 1)
                tt, cb = n // 4, n % 4
                act.copy(pp_made[:, tt, cb * 512:(cb + 1) * 512], bank[2 + n % 2][:, :]).then_inc(pp_sb, 1)

            def take_spread(tt, q, m):
                act.wait_ge(spread_mm[tt], q + 1)
                act.copy(spread[:, tt, :, bass.ds(TOKB * q, TOKB)].rearrange("p i t -> p t i"),
                         bank[SPREAD_BANK[m % HOTS[tt]]][:, :].rearrange("p (t i) -> p t i", t=TOKB)).then_inc(spread_sb[tt], 1)

            def tile0_hots(q, m, peeled):
                if not (peeled and m < 2):
                    act.wait_ge(spread_mm[0], q - 1)
                h = [hot1[0][m % 2], hot2[0][m % 2]]
                for c in range(2):
                    for a in range(TOKB):
                        act.activation(h[c][:, a, :], iota[:, :], ACT.Abs, scale=-1.0,
                                       bias=tsl[0][:, c, bass.ds(TOKB * q + a, 1)]).then_inc(hot_dist, 1)
                act.wait_ge(hot_dist, 2 * TOKB * (q + 1))
                act.activation(h[1][:, :, :], h[1][:, :, :], ACT.Relu, scale=-1.0, bias=ones[:, 0:1])\
                    .then_inc(hot_unit, 1)
                act.activation(h[0][:, :, :], h[0][:, :, :], ACT.Relu, scale=-1.0, bias=ones[:, 0:1])\
                    .then_inc(hot_ready, 1)
                act.wait_ge(hot_unit, q + 1)
                for a in range(TOKB):
                    act.activation(h[1][:, a, :], h[1][:, a, :], ACT.Copy,
                                   scale=tsl[0][:, 2, bass.ds(TOKB * q + a, 1)]).then_inc(hot_ready, 1)

            def peer(i, spreading, last, first=False):
                for b in range(2):
                    if b == 0 or not last:
                        route_exp(i + b, 1 - b, False)
                    if spreading:
                        q = (2 * (i - HALF) + b) * PER_STEP
                        for m in range(PER_STEP):
                            tile0_hots(q + m, m, first and b == 0)
                            if m >= 1:
                                take_spread(0, q + m - 1, m - 1)
                        take_spread(0, q + PER_STEP - 1, PER_STEP - 1)
                    gelu(i, b)

            with act.Fori(0, HALF) as i:
                peer(i, False, False)
            act.wait_ge(tsl_mm[0], 1)
            act.copy(tsl[0][:, :, :], bank[5][:, 0:3 * P].rearrange("p (a t) -> p a t", a=3)).then_inc(tsl_sb[0], 1)
            act.wait_ge(pp_out, 16)
            act.wait_ge(tsl_sb[0], 1)
            peer(HALF, True, False, first=True)
            with act.Fori(HALF + 1, PAIRS - 1) as i:
                peer(i, True, False)
            peer(PAIRS - 1, True, True)
            act.wait_ge(tsl_mm[1], 1)
            act.copy(tsl[1][:, :, :], bank[5][:, 0:3 * P].rearrange("p (a t) -> p a t", a=3)).then_inc(tsl_sb[1], 1)
            with act.Fori(0, SPREADS // 4) as i:
                for m in range(4):
                    take_spread(1, 4 * i + m, m)

            act.wait_ge(spread_sb[1], SPREADS)
            def v_halves(i, peeled):
                for r in range(VRING):
                    c = VRING * i + r
                    if not (peeled and r < 2):
                        act.wait_ge(v_mm, VBLK * (c - 1))
                    act.copy(chi[r % 2][:, :, :], spread[:, :, bass.ds(c, 1), :].rearrange("p a o t -> p a (o t)"))\
                        .then_inc(chi_ready, 1)
                    act.wait_ge(v_landed[r], 16 * (i + 1))
                    for b in range(VBLK):
                        if not (peeled and r == 0):
                            act.wait_ge(v_mm, VBLK * c + b - VUNITS + 1)
                        act.copy(vhi[b][:, :], vraw[r][:, b * VCOL:(b + 1) * VCOL]).then_inc(vhi_ready, 1)

            v_halves(0, True)
            with act.Fori(1, TURNS) as i:
                v_halves(i, False)

            act.wait_ge(peer_done, VBLK)
            norm_sums("ple")
            split_hi("gate", 0, 0, True)
            take_hi("ple")

            def sigmoid_out(group, parity):
                act.wait_ge(mm_done["gate"], 2 * group + 2)
                if not (isinstance(group, int) and group == 0):
                    act.wait_ge(ple_added, group)
                act.activation(sig[parity][:, :], bank[parity][:, :], ACT.Sigmoid).then_inc(evac["gate"], 1)

            run("gate", sigmoid_out, presplit=1)
            act.wait_ge(ple_added, NG["gate"])
            norm_sums("fin")

        @block.vector
        def _(dve):
            st = Steps(dve, dve_step)

            def norm_scale(name, turn):
                dve.scalar_tensor_tensor(out=xn[:, 1, :], in0=hres[:, 1, :], scalar=1.0, in1=hres[:, 1, :],
                                         op0=ALU.mult, op1=ALU.mult, accum_out=ssq[:, 1:2]).then_inc(norm_sq[name], 1)
                dve.wait_ge(norm_sq[name], TT)
                dve.tensor_scalar(ssq[:, :], ssq[:, :], 1.0 / D, EPS, ALU.mult, ALU.add)\
                    .then_inc(norm_root[name], 1)
                dve.wait_ge(norm_root[name], 2)
                st.did(dve.reciprocal(rstd[:, :], rstd[:, :]))
                dve.wait_ge(gain_in, 16 * (turn + 1))
                st.wait()

            def norm_piece(name, b):
                tt, cols = b // 4, slice(b % 4 * 512, (b % 4 + 1) * 512)
                dve.scalar_tensor_tensor(out=xn[:, tt, cols], in0=hres[:, tt, cols], scalar=rstd[:, tt:tt + 1],
                                         in1=gain[:, cols], op0=ALU.mult, op1=ALU.mult).then_inc(norm_done[name], 1)

            def take_lo(name, b):
                tt, kb = b // 4, b % 4
                dve.wait_ge(tr_hi[name], b + 1)
                dst = (slice(None), slice(4 * kb, 4 * kb + 4), slice(tt * P, (tt + 1) * P))
                dve.tensor_tensor(xtlo[dst], bank[2 + b % 4][:, :].rearrange("p (a t) -> p a t", a=4),
                                  xthi[dst].bitcast(fp32), ALU.subtract).then_inc(tr_lo[name], 1)

            def norm_and_split(name, turn):
                norm_scale(name, turn)
                for b in range(4):
                    norm_piece(name, b)
                for b in range(4):
                    norm_piece(name, 4 + b)
                    take_lo(name, b)
                for b in range(4, 8):
                    take_lo(name, b)

            def run(stage, take, first_split=False, beside_first=None, beside=None):
                def split_lo(i, r):
                    dve.wait_ge(hi_ready[stage], RING * i + r + 1)
                    dve.tensor_tensor(wlo[r % 2][:, :, :], raw[r][:, :, :], whi[r % 2][:, :, :].bitcast(fp32),
                                      ALU.subtract).then_inc(lo_ready[stage], 1)

                def turn(i, peeled, last=False):
                    if not (peeled and first_split):
                        split_lo(i, 0)
                    if not peeled and take:
                        take(2 * i - 1, 1)
                    if peeled and first_split:
                        dve.wait_ge(lo_ready[stage], 1)
                    split_lo(i, 1)
                    if last and beside:
                        beside()
                    if peeled and beside_first:
                        beside_first()
                    split_lo(i, 2)
                    if take:
                        take(2 * i, 0)
                    split_lo(i, 3)

                turns = NG[stage] // 2
                turn(0, True)
                with dve.Fori(1, turns - 1) as i:
                    turn(i, False)
                turn(turns - 1, False, last=True)
                if take:
                    take(2 * turns - 1, 1)

            dve.wait_ge(x_in, 32)
            norm_and_split("mix", 0)
            def small_copies():
                dve.wait_ge(small_tr, 2)
                dve.tensor_copy(post[:, :], bank[6][:, 0:CMP_LEN]).then_inc(small_sb, 1)
                dve.tensor_copy(ongt[:, :], bank[6][:, CMP_LEN:CMP_LEN + NH]).then_inc(small_sb, 1)
                dve.wait_ge(r_mm, 1)
                dve.tensor_copy(rvec[:, :], bank[7][0:NH, 0:RLEN]).then_inc(r_sb, 1)
                dve.wait_ge(gate_hi, 1)
                dve.tensor_tensor(wglo[:, :, :], wg[:, :, :], wghi[:, :, :].bitcast(fp32), ALU.subtract)\
                    .then_inc(gate_lo, 1)

            run("in", None, first_split=True, beside_first=small_copies)
            for n in range(len(V_UNITS) // 2):
                dve.wait_ge(vt_mm, n + 1)
                u = V_UNITS[2 * n]
                dve.tensor_copy(pr[:, u:u + 2, :], bank[2 + n % 4][:, :].rearrange("p (u t) -> p u t", u=2))\
                    .then_inc(vt_sb, 1)
            dve.wait_ge(gate_tr, 1)
            dve.tensor_copy(gates[:, :, :], bank[7][:, SEQ:SEQ + TT * GATES].rearrange("p (t g) -> p t g", t=TT))\
                .then_inc(gate_sb, 1)

            def biased(c):
                _, _, _, bh, _, kind, _, _, _ = CALLS[c]
                dve.wait_ge(s_score, c + 1)
                if c >= 2:
                    dve.wait_ge(s_prob, 2 * (c - 1))
                if kind == "full":
                    w, w0 = RLEN, P
                    spans = [(slice(0, RLEN), bias[:, bh, :])]
                else:
                    w, w0 = NCMP0 + NCMP, NCMP0
                    spans = [(slice(0, w0), bias[:, bh, CMP_LEN - 1:P:CMP_STRIDE]),
                             (slice(w0, w), bias[:, bh, P + CMP_LEN - 1:RLEN:CMP_STRIDE])]
                for cols, b in spans:
                    st.did(dve.scalar_tensor_tensor(out=sc[c % 2][:, cols], in0=bank[2 + c % 2][:, cols], scalar=SCALE,
                                                    in1=b, op0=ALU.mult, op1=ALU.add))
                st.wait()
                for tt, cols in ((0, slice(0, w0)), (1, slice(w0, w))):
                    dve.tensor_reduce(negmax[c % 2][:, tt:tt + 1], sc[c % 2][:, cols], AX.X, ALU.max, negate=True)\
                        .then_inc(s_biased, 1)

            def scaled_identity(c):
                _, _, _, _, _, kind, gate, _, _ = CALLS[c]
                dve.wait_ge(s_prob, 2 * c + 2)
                r = rz[c % 2]
                st.did(dve.reciprocal(r[:, :], zsum[c % 2][:, :]))
                st.wait()
                if gate is not None:
                    st.did(dve.tensor_tensor(r[:, :], r[:, :], gates[:, :, gate], ALU.mult))
                    st.wait()
                if kind == "cmp":
                    st.did(dve.tensor_tensor(r[:, 0:1], r[:, 0:1], valid[:, :], ALU.mult))
                    st.wait()
                if c >= 2:
                    dve.wait_ge(s_pt, c - 1)
                for tt in range(TT):
                    dve.tensor_scalar(diag[c % 2][:, tt, :], ident[:, :], r[:, tt:tt + 1], None, ALU.mult)\
                        .then_inc(s_diag, 1)

            def group_mean(n):
                a, b = GROUPS[n]
                dve.wait_ge(g_sum, n + 1)
                dve.tensor_scalar(orms[:, n, :], bank[n % 2][:, 0:SEQ], 1.0 / ((b - a) * HD), EPS, ALU.mult, ALU.add)\
                    .then_inc(g_root, 1)

            def group_reciprocal(n):
                dve.wait_ge(g_rstd, 1 if n < 2 else 2)
                st.did(dve.reciprocal(orms[:, n, :], orms[:, n, :]))
                st.wait()

            def scale_heads(n, first, end):
                for h in range(first, end):
                    dve.scalar_tensor_tensor(out=ysc[n][:, h - GROUPS[n][0], :], in0=ot[:, h, :],
                                             scalar=ongt[:, h:h + 1], in1=orms[:, n, :], op0=ALU.mult, op1=ALU.mult)\
                        .then_inc(y_ready, 1)

            def y_lo_half(part, n, a, b):
                g0 = GROUPS[n][0]
                dve.wait_ge(y_hi, part + 1)
                dve.tensor_tensor(xtlo[:, a:b, :], ysc[n][:, a - g0:b - g0, :], xthi[:, a:b, :].bitcast(fp32),
                                  ALU.subtract).then_inc(y_lo, 1)

            dve.wait_ge(bias_in, 32)
            dve.wait_ge(const_ready, 4)
            dve.wait_ge(gate_sb, 1)
            for s in range(NC_ + 1):
                if s < NC_:
                    biased(s)
                if s >= 1:
                    scaled_identity(s - 1)
                if s == CMP_STEP + CMP_PARTS:
                    dve.wait_ge(cmp_mm, 1)
                    dve.tensor_copy(ksb[:, 0, :], bank[0][0:KV * NCMP, 0:HD]).then_inc(cmp_sb, 1)
                    dve.tensor_copy(ksb[:, 1, :], bank[1][0:KV * NCMP, 0:HD]).then_inc(cmp_sb, 1)
                if s == CMP_STEP + CMP_PARTS + 2:
                    dve.wait_ge(cmp_tr, 1)
                    for kv, dst in enumerate((kct, vct)):
                        dve.tensor_copy(dst[:, :, :], bank[0][:, (kv + 1) * P:(kv + 1) * P + KV * NCMP]
                                        .rearrange("p (g n) -> p g n", g=KV)).then_inc(cmp_sb, 1)
                if s == CMP_STEP + CMP_PARTS + 4:
                    dve.wait_ge(cmp_tr, 2)
                    dve.tensor_copy(vcm[0:NCMP, :, :],
                                    bank[1][0:NCMP, P:P + KV * HD].rearrange("p (g d) -> p g d", g=KV)).then_inc(cmp_sb, 1)
                for n in range(2):
                    if s == MEAN_STEP[n]:
                        group_mean(n)
                    if s == RECIP_STEP[n]:
                        group_reciprocal(n)
                    a, b = GROUPS[n]
                    half = (a + b) // 2
                    if s == SCALE_STEP[n]:
                        scale_heads(n, a, half)
                    if s == SCALE_STEP[n] + 1:
                        scale_heads(n, half, b)
                    if s == SCALE_STEP[n] + 4:
                        y_lo_half(n, n, a, b)
            group_mean(2)
            dve.wait_ge(hi_ready["out"], 1)
            dve.tensor_tensor(wlo[0][:, :, :], raw[0][:, :, :], whi[0][:, :, :].bitcast(fp32), ALU.subtract)\
                .then_inc(lo_ready["out"], 1)
            group_reciprocal(2)
            for a, b in NSA_PARTS:
                scale_heads(2, a, b)
            for m, (a, b) in enumerate(NSA_PARTS):
                y_lo_half(2 + m, 2, a, b)

            def add_mixer(group, parity):
                dve.wait_ge(mm_done["out"], 2 * group + 2)
                cols = bass.ds(group * CHUNK_C, CHUNK_C)
                dve.tensor_tensor(hres[:, :, cols], hres[:, :, cols],
                                  bank[parity][:, :].rearrange("p (t c) -> p t c", t=TT), ALU.add)\
                    .then_inc(evac["out"], 1)

            run("out", add_mixer, first_split=True)
            dve.wait_ge(evac["out"], NG["out"])
            norm_and_split("ffn", 1)

            def route(s, b, peeled):
                if not peeled:
                    dve.wait_ge(gate_exp, s)
                st.did(dve.tensor_copy(s1[:, :, :], scores[:, bass.ds(s, 1), :, :].rearrange("p o c k -> p (o c) k")))
                st.wait_apart()
                for c in range(2):
                    st.did(dve.max(top[:, c, 0:8], s1[:, c, :]))
                st.wait_apart()
                for c in range(2):
                    st.did(dve.max_index(topi[:, c, 0:8], top[:, c, 0:8], s1[:, c, :]))
                    st.did(dve.match_replace(s2[:, c, :], top[:, c, 0:8], s1[:, c, :], TAKEN))
                st.wait_apart()
                for c in range(2):
                    st.did(dve.max(top[:, c, 8:16], s2[:, c, :]))
                st.wait_apart()
                for c in range(2):
                    st.did(dve.max_index(topi[:, c, 8:16], top[:, c, 8:16], s2[:, c, :]))
                st.did(dve.tensor_tensor(cand[:, :, :], top[:, 0, :, None].broadcast_to([P, TOPK, TOPK]),
                                         top[:, 1, None, :].broadcast_to([P, TOPK, TOPK]), ALU.add))
                st.wait()
                st.did(dve.tensor_copy(topf[:, :, :], topi[:, :, :]))
                c1 = cand[:, :, :].rearrange("p a b -> p (a b)")
                c2 = cand2[:, :, :].rearrange("p a b -> p (a b)")
                st.did(dve.max(best[:, 0:8], c1))
                st.wait_apart()
                st.did(dve.max_index(bestj[:, 0:8], best[:, 0:8], c1))
                st.did(dve.match_replace(c2, best[:, 0:8], c1, TAKEN))
                st.did(dve.tensor_scalar(nbest[:, :], best[:, 0:1], -1.0, None, ALU.mult))
                st.wait_apart()
                st.did(dve.max(best[:, 8:16], c2))
                st.wait_apart()
                st.did(dve.max_index(bestj[:, 8:16], best[:, 8:16], c2))
                st.wait()
                st.did(dve.tensor_scalar(bidx[:, 0, :], bestj[:, :], 4, None, ALU.logical_shift_right))
                st.did(dve.tensor_scalar(bidx[:, 1, :], bestj[:, :], TOPK - 1, None, ALU.bitwise_and))
                st.wait()
                slots = bass.ds(s * TOPK, TOPK)
                for c in range(2):
                    st.did(dve.tensor_tensor(pick[:, :, :], bidx[:, c, :, None].broadcast_to([P, TOPK, TOPK]),
                                             iota[:, None, 0:TOPK].broadcast_to([P, TOPK, TOPK]), ALU.is_equal))
                    st.wait()
                    st.did(dve.tensor_tensor(pick[:, :, :], pick[:, :, :],
                                             topf[:, c, None, :].broadcast_to([P, TOPK, TOPK]), ALU.mult))
                    st.wait()
                    st.did(dve.tensor_reduce(slot_idx[:, c, slots], pick[:, :, :], AX.X, ALU.add))
                    st.wait()
                dve.scalar_tensor_tensor(out=expert[b][:, :], in0=slot_idx[:, 0, slots], scalar=float(NKEYS),
                                         in1=slot_idx[:, 1, slots], op0=ALU.mult, op1=ALU.add).then_inc(routed, 1)
                dve.wait_ge(routed, s + 1)
                st.did(dve.tensor_scalar(slot_row[:, slots], expert[b][:, :], float(QUARTERS), float(QUARTERS - 1),
                                         ALU.mult, ALU.add))

            ROUTE_STEPS = 1 + 2 + 4 + 2 + 3 + 2 + 3 + 1 + 1 + 2 + 6 + 1

            def tile1_hots(i, m, peeled):
                q = 4 * i + m
                if not peeled:
                    dve.wait_ge(spread_mm[1], q - 3)
                if m % 2:
                    dve.tensor_tensor(hot1[1][m][:, :, :], iota[:, None, :].broadcast_to([P, TOKB, NKEYS]),
                                      tsl[1][:, 0, bass.ds(TOKB * q, TOKB)][:, :, None]
                                      .broadcast_to([P, TOKB, NKEYS]), ALU.is_equal).then_inc(hot2_ready, 1)
                for a in range(TOKB):
                    t = TOKB * q + a
                    dve.tensor_scalar(hot2[1][m][:, a, :], iota[:, :], tsl[1][:, 1, bass.ds(t, 1)],
                                      tsl[1][:, 2, bass.ds(t, 1)], ALU.is_equal, ALU.mult).then_inc(hot2_ready, 1)

            def use_rows(turn, b, tt):
                s = 2 * turn + b
                for k in range(TOPK):
                    dve.wait_ge(fetched[k % GRING], (s * (TOPK // GRING) + k // GRING + 1) * 16)
                    r = rows[k % GRING]
                    dve.scalar_tensor_tensor(out=r[:, :], in0=r[:, :], scalar=1.0, in1=xn[:, tt, :], op0=ALU.mult,
                                             op1=ALU.mult, accum_out=dots[b][:, k:k + 1]).then_inc(eaten, 1)
                dve.wait_ge(eaten, (s + 1) * TOPK)
                dve.wait_ge(gate_exp, s + 1)
                dve.reciprocal(gsum[b][:, :], gsum[b][:, :]).then_inc(dots_ready, 1)
                dve.wait_ge(gelu_ready, s + 1)
                dve.scalar_tensor_tensor(out=slot_coef[:, bass.ds(s * TOPK, TOPK)], in0=gel[b][:, :],
                                         scalar=gsum[b][:, :], in1=gexp[b][:, :], op0=ALU.mult, op1=ALU.mult)\
                    .then_inc(coef_ready, 1)

            def peer_pair(i, tt, last=False, first=False):
                for b in range(2):
                    if first and b == 1:
                        dve.wait_ge(sc_sb, 8)
                    if b == 0 or not last:
                        route(2 * i + 1 + b, 1 - b, False)
                    use_rows(i, b, tt)

            def first_route():
                dve.wait_ge(sc_sb, 1)
                route(0, 0, True)

            run("wq", None, first_split=True, beside=first_route)
            peer_pair(0, 0, first=True)
            with dve.Fori(1, HALF) as i:
                st.enter(i - 1, 2 * ROUTE_STEPS)
                peer_pair(i, 0)
            st.leave(HALF - 1)
            with dve.Fori(HALF, PAIRS - 1) as i:
                st.enter(i - HALF, 2 * ROUTE_STEPS)
                peer_pair(i, 1)
            st.leave(PAIRS - 1 - HALF)
            peer_pair(PAIRS - 1, 1, last=True)
            dve.wait_ge(tsl_sb[1], 1)
            for m in range(4):
                tile1_hots(0, m, True)
            with dve.Fori(1, SPREADS // 4) as i:
                for m in range(4):
                    tile1_hots(i, m, False)

            def v_turn(i, tt, peeled):
                for r in range(VRING):
                    c = VRING * i + r
                    dve.wait_ge(chi_ready, c + 1)
                    dve.tensor_tensor(clo[r % 2][:, :, :], spread[:, :, bass.ds(c, 1), :].rearrange("p a o t -> p a (o t)"),
                                      chi[r % 2][:, :, :].bitcast(fp32), ALU.subtract).then_inc(clo_ready, 1)
                    for b in range(VBLK):
                        dve.wait_ge(vhi_ready, VBLK * c + b + 1)
                        dve.tensor_tensor(vlo[b][:, :], vraw[r][:, b * VCOL:(b + 1) * VCOL],
                                          vhi[b][:, :].bitcast(fp32), ALU.subtract).then_inc(vlo_ready, 1)
                    for n in (2 * r, 2 * r + 1):
                        dve.wait_ge(v_fetched[n], 16 * (i + 1))
                        if not (peeled and n == 0):
                            dve.wait_ge(v_used, GRING * i + n)
                        cols = hres[:, tt, VBLK * VCOL:D]
                        dve.scalar_tensor_tensor(out=cols, in0=vrow[n][:, :], scalar=slot_coef[:, bass.ds(GRING * i + n, 1)],
                                                 in1=cols, op0=ALU.mult, op1=ALU.add).then_inc(v_used, 1)

            v_turn(0, 0, True)
            with dve.Fori(1, TURNS // TT) as i:
                v_turn(i, 0, False)
            with dve.Fori(TURNS // TT, TURNS) as i:
                v_turn(i, 1, False)
            dve.wait_ge(v_used, TT * SLOTS)
            dve.wait_ge(v_mm, NKEYS * VBLK)
            for tt in range(TT):
                for b in range(VBLK):
                    cols = hres[:, tt, b * VCOL:(b + 1) * VCOL]
                    dve.tensor_tensor(cols, cols, bank[tt * VBLK + b][:, :], ALU.add).then_inc(peer_done, 1)
            dve.wait_ge(peer_done, TT * VBLK)

            norm_and_split("ple", 2)

            def add_ple(group, parity):
                dve.wait_ge(evac["gate"], group + 1)
                cols = bass.ds(group * CHUNK_C, CHUNK_C)
                g = sig[parity][:, :].rearrange("p (t c) -> p t c", t=TT)
                st.did(dve.tensor_tensor(g, g, pp[:, :, cols], ALU.mult))
                st.wait()
                dve.tensor_tensor(hres[:, :, cols], hres[:, :, cols], g, ALU.add).then_inc(ple_added, 1)

            def run_gate():
                stage = "gate"

                def split_lo(i, r):
                    dve.wait_ge(hi_ready[stage], RING * i + r + 1)
                    dve.tensor_tensor(wlo[r % 2][:, :, :], raw[r][:, :, :], whi[r % 2][:, :, :].bitcast(fp32),
                                      ALU.subtract).then_inc(lo_ready[stage], 1)

                dve.wait_ge(lo_ready[stage], 1)
                split_lo(0, 1)
                split_lo(0, 2)
                add_ple(0, 0)
                split_lo(0, 3)
                with dve.Fori(1, NG[stage] // 2) as i:
                    st.enter(i - 1, 2)
                    split_lo(i, 0)
                    add_ple(2 * i - 1, 1)
                    split_lo(i, 1)
                    split_lo(i, 2)
                    add_ple(2 * i, 0)
                    split_lo(i, 3)
                st.leave(NG[stage] // 2 - 1)
                add_ple(NG[stage] - 1, 1)

            dve.wait_ge(pp_in, 16)
            run_gate()
            dve.wait_ge(ple_added, NG["gate"])
            norm_scale("fin", 3)
            for b in range(8):
                norm_piece("fin", b)

        @block.tensor
        def _(pe):
            def transposes(name):
                for b in range(8):
                    tt, kb = b // 4, b % 4
                    pe.wait_ge(norm_done[name], b + 1)
                    if b >= 4:
                        pe.wait_ge(tr_lo[name], b - 3)
                    for a in range(4):
                        k = 4 * kb + a
                        last = pe.transpose(bank[2 + b % 4][:, a * P:(a + 1) * P], xn[:, tt, k * P:(k + 1) * P],
                                            ident[:, :])
                    last.then_inc(tr_done[name], 1)

            def chunk(stage, i, r, peeled):
                feature_major = stage in ("in", "wq")
                acc = bank[r // 2]
                pe.wait_ge(lo_ready[stage], RING * i + r + 1)
                if r % 2 == 0 and not peeled:
                    pe.wait_ge(evac[stage], 2 * i + r // 2 - 1)
                for k in range(CHUNK_K):
                    kk = (r % 2) * CHUNK_K + k
                    for u in range(2):
                        cols = slice(u * P, (u + 1) * P)
                        start = r % 2 == 0 and k == 0 and u == 0
                        stop = r % 2 == 1 and k == CHUNK_K - 1
                        hi, lo = whi[r % 2], wlo[r % 2]
                        dst = acc[:, u * SEQ:(u + 1) * SEQ]
                        if feature_major:
                            parts = [(hi[:, k, cols], xthi[:, kk, :]), (hi[:, k, cols], xtlo[:, kk, :]),
                                     (lo[:, k, cols], xthi[:, kk, :])]
                        else:
                            parts = [(xthi[:, kk, cols], hi[:, k, :]), (xthi[:, kk, cols], lo[:, k, :]),
                                     (xtlo[:, kk, cols], hi[:, k, :])]
                        for n, (a, b) in enumerate(parts):
                            last = pe.matmul(dst, a, b, start=start and n == 0, stop=stop and n == 2,
                                             skip_group_check=True)
                last.then_inc(mm_done[stage], 1)

            def run(stage, before_last=None):
                for r in range(RING):
                    chunk(stage, 0, r, True)
                with pe.Fori(1, NG[stage] // 2 - 1) as i:
                    for r in range(RING):
                        chunk(stage, i, r, False)
                if before_last:
                    before_last()
                for r in range(RING):
                    chunk(stage, NG[stage] // 2 - 1, r, False)

            pe.wait_ge(const_ready, 4)
            transposes("mix")
            pe.wait_ge(small_in, 80)
            pe.transpose(bank[6][:, 0:CMP_LEN], posn[:, :], ident[0:CMP_LEN, 0:CMP_LEN]).then_inc(small_tr, 1)
            pe.transpose(bank[6][:, CMP_LEN:CMP_LEN + NH], ongn[:, :], ident[0:NH, 0:NH]).then_inc(small_tr, 1)
            pe.matmul(bank[7][0:NH, 0:RLEN], tabl[:, 0:NH], tabl[:, NH:], start=True, stop=True).then_inc(r_mm, 1)
            pe.wait_ge(tr_lo["mix"], 8)
            run("in")
            pe.wait_ge(gate_lo, 1)
            pe.wait_ge(r_sb, 1)
            for k in range(KT):
                for n, (a, b) in enumerate([(wghi, xthi), (wghi, xtlo), (wglo, xthi)]):
                    last = pe.matmul(bank[7][0:GATES, 0:SEQ], a[:, k, :], b[:, k, :],
                                     start=k == 0 and n == 0, stop=k == KT - 1 and n == 2)
            last.then_inc(gate_mm, 1)
            pe.wait_ge(evac["in"], NG["in"])
            for n in range(len(V_UNITS) // 2):
                if n >= 4:
                    pe.wait_ge(vt_sb, n - 3)
                for a in range(4):
                    u, tt = V_UNITS[2 * n + a // 2], a % 2
                    last = pe.transpose(bank[2 + n % 4][:, a * P:(a + 1) * P], pr[:, u, tt * P:(tt + 1) * P],
                                        ident[:, :])
                last.then_inc(vt_mm, 1)
            pe.wait_ge(gate_sig, 1)
            for tt in range(TT):
                last = pe.transpose(bank[7][:, SEQ + tt * GATES:SEQ + (tt + 1) * GATES],
                                    gatest[:, tt * P:(tt + 1) * P], ident[0:GATES, 0:GATES])
            last.then_inc(gate_tr, 1)

            def add_squares(n, h):
                a, b = GROUPS[n]
                pe.wait_ge(g_sq, HEAD_ORD[h] + 1)
                if n == 2 and h == a:
                    pe.wait_ge(g_root, 1)
                last = pe.matmul(bank[n % 2][:, 0:SEQ], ones[:, :], osq[:, HEAD_ORD[h] % SIDE, :], start=h == a,
                                 stop=h == b - 1)
                if h == b - 1:
                    last.then_inc(g_sum, 1)

            def score(c):
                q, k, _, _, _, kind, _, _, _ = CALLS[c]
                if c >= 2:
                    pe.wait_ge(s_biased, 2 * (c - 1))
                dst = bank[2 + c % 2]
                if kind == "full":
                    pe.matmul(dst[:, 0:P], pr[:, q, 0:P], pr[:, k, 0:P], start=True, stop=True)
                    last = pe.matmul(dst[:, P:RLEN], pr[:, q, P:SEQ], pr[:, k, :], start=True, stop=True)
                else:
                    pe.matmul(dst[:, 0:NCMP0], pr[:, q, 0:P], kct[:, k, 0:NCMP0], start=True, stop=True)
                    last = pe.matmul(dst[:, NCMP0:NCMP0 + NCMP], pr[:, q, P:SEQ], kct[:, k, :], start=True, stop=True)
                last.then_inc(s_score, 1)

            def transpose_probs(c):
                kind = CALLS[c][5]
                pe.wait_ge(s_diag, 2 * c + 2)
                if c >= 2:
                    pe.wait_ge(s_pts, c - 1)
                dst, pr_, dg = bank[4 + c % 2], pb[c % 3], diag[c % 2]
                if kind == "full":
                    pe.matmul(dst[:, 0:P], pr_[:, 0:P], dg[:, 0, :], start=True, stop=True)
                    pe.matmul(dst[:, P:2 * P], pr_[:, P:2 * P], dg[:, 1, :], start=True, stop=True)
                    last = pe.matmul(dst[:, 2 * P:RLEN], pr_[:, 2 * P:RLEN], dg[:, 1, :], start=True, stop=True)
                else:
                    pe.matmul(dst[0:NCMP0, 0:P], pr_[:, 0:NCMP0], dg[:, 0, :], start=True, stop=True)
                    last = pe.matmul(dst[0:NCMP, P:SEQ], pr_[:, NCMP0:NCMP0 + NCMP], dg[:, 1, :], start=True, stop=True)
                last.then_inc(s_pt, 1)

            def values(c):
                _, _, v, _, h, kind, _, first, final = CALLS[c]
                pe.wait_ge(s_pts, c + 1)
                if kind == "cmp":
                    pe.wait_ge(cmp_sb, 5)
                n = HEAD_ORD[h]
                if first and n >= 2:
                    pe.wait_ge(s_ot, n - 1)
                dst, pt = bank[6 + n % 2], pts[c % 2]
                if kind == "full":
                    pe.matmul(dst[:, 0:SEQ], pr[:, v, 0:P], pt[:, 0:SEQ], start=first, stop=False,
                              skip_group_check=True)
                    last = pe.matmul(dst[:, P:SEQ], pr[:, v, P:SEQ], pt[:, SEQ:RLEN], start=False, stop=final,
                                     skip_group_check=True)
                else:
                    pe.matmul(dst[:, 0:P], vcm[0:NCMP0, v, :], pt[0:NCMP0, 0:P], start=False, stop=False,
                              skip_group_check=True)
                    last = pe.matmul(dst[:, P:SEQ], vcm[0:NCMP, v, :], pt[0:NCMP, P:SEQ], start=False, stop=final,
                                     skip_group_check=True)
                last.then_inc(s_pv, 1)

            pe.wait_ge(vt_sb, len(V_UNITS) // 2)
            pe.wait_ge(gate_sb, 1)
            for s in range(NC_ + 3):
                if s < NC_:
                    if CALLS[s][5] == "cmp":
                        pe.wait_ge(cmp_sb, 3)
                    score(s)
                if 0 <= s - 2 < NC_:
                    transpose_probs(s - 2)
                if 0 <= s - 3 < NC_:
                    values(s - 3)
                if CMP_STEP <= s < CMP_STEP + CMP_PARTS:
                    if s == CMP_STEP:
                        pe.wait_ge(wcmp_in, 32)
                        pe.wait_ge(xcmp_ready, 2 * KV)
                    per = CMP_LEN // CMP_PARTS
                    for l in range((s - CMP_STEP) * per, (s - CMP_STEP + 1) * per):
                        for kv in range(2):
                            last = pe.matmul(bank[kv][0:KV * NCMP, 0:HD],
                                             xcmp[:, kv, l, :, :].rearrange("p g n -> p (g n)"), wcmp[kv][:, l, :],
                                             start=l == 0, stop=l == CMP_LEN - 1, skip_group_check=True)
                    if l == CMP_LEN - 1:
                        last.then_inc(cmp_mm, 1)
                if s == CMP_STEP + CMP_PARTS + 1:
                    pe.wait_ge(cmp_sb, 2)
                    for kv in range(2):
                        last = pe.transpose(bank[0][:, (kv + 1) * P:(kv + 1) * P + KV * NCMP], ksb[:, kv, :],
                                            ident[0:KV * NCMP, 0:KV * NCMP])
                    last.then_inc(cmp_tr, 1)
                if s == CMP_STEP + CMP_PARTS + 3:
                    pe.wait_ge(cmp_sb, 4)
                    for g in range(KV):
                        last = pe.transpose(bank[1][0:NCMP, (g + 1) * P:(g + 2) * P], vct[:, g, :], ident[:, :])
                    last.then_inc(cmp_tr, 1)
                for n in range(2):
                    if s == SUM_STEP[n]:
                        pe.wait_ge(cmp_sb, 5)
                        for h in range(*GROUPS[n]):
                            add_squares(n, h)
                if s >= 1 and s - 5 in LAST and HEAD_ORD[LAST[s - 5]] >= SIDE:
                    add_squares(2, LAST[s - 5])
            add_squares(2, LAST[NC_ - 1])
            pe.wait_ge(y_lo, 4)
            pe.wait_ge(cmp_sb, 5)
            run("out")
            pe.wait_ge(keys_in, 16)
            for n in range(4):
                if n >= 2:
                    pe.wait_ge(kt_sb, n - 1)
                for a in range(4):
                    last = pe.transpose(bank[6 + n % 2][:, a * P:(a + 1) * P], keys[:, 4 * n + a, :], ident[:, :])
                last.then_inc(kt_mm, 1)
            transposes("ffn")
            pe.wait_ge(tr_lo["ffn"], 8)
            pe.wait_ge(evac["out"], NG["out"])
            def key_scores(order):
                for j, n in order:
                    tt, h0 = n // 4, 2 * (n % 4)
                    if j >= 4:
                        pe.wait_ge(sc_sb, j - 3)
                    for a in range(4):
                        hc = 2 * h0 + a
                        last = pe.matmul(bank[4 + j % 4][:, a * P:(a + 1) * P], qt[:, hc, tt * P:(tt + 1) * P],
                                         keyst[:, hc, :], start=True, stop=True)
                    last.then_inc(sc_mm, 1)

            def early_scores():
                pe.wait_ge(kt_sb, 4)
                pe.wait_ge(evac["wq"], 4)
                key_scores(EARLY_SCORES)

            run("wq", before_last=early_scores)
            pe.wait_ge(evac["wq"], NG["wq"])
            key_scores(LATE_SCORES)
            pe.wait_ge(sc_sb, 8)
            pe.wait_ge(p_in, 16)
            for k in range(PLE // P):
                for tt in range(TT):
                    last = pe.transpose(bank[6 + k][:, tt * P:(tt + 1) * P], ptile[:, tt, k * P:(k + 1) * P], ident[:, :])
                last.then_inc(pt2_mm, 1)
            pe.wait_ge(pt2_sb, PLE // P)
            pe.wait_ge(pproj_in, 16)
            for n in range(8):
                tt, cb = n // 4, n % 4
                if n >= 2:
                    pe.wait_ge(pp_sb, n - 1)
                for k in range(PLE // P):
                    last = pe.matmul(bank[2 + n % 2][:, :], ptt[:, k, tt * P:(tt + 1) * P],
                                     pproj[:, k, cb * 512:(cb + 1) * 512], start=k == 0, stop=k == PLE // P - 1)
                last.then_inc(pp_mm, 1)

            def transpose_slots(tt):
                pe.wait_ge(coef_ready, (tt + 1) * PEER_H)
                cols = slice(tt * SLOTS, (tt + 1) * SLOTS)
                for a, src in enumerate((slot_idx[:, 0, cols], slot_idx[:, 1, cols], slot_coef[:, cols])):
                    last = pe.transpose(bank[5][:, a * P:(a + 1) * P], src, ident[:, :])
                last.then_inc(tsl_mm[tt], 1)

            def spread_group(tt, i, m, peeled):
                q = HOTS[tt] * i + m
                if tt == 0:
                    pe.wait_ge(hot_ready, (TOKB + 1) * (q + 1))
                else:
                    pair = 2 * i + m // 2
                    if m % 2 == 0:
                        pe.wait_ge(hot1_ready, TOKB * (pair + 1))
                    pe.wait_ge(hot2_ready, (2 * TOKB + 1) * pair + (TOKB, 2 * TOKB + 1)[m % 2])
                if not peeled:
                    pe.wait_ge(spread_sb[tt], q + 1 - HOTS[tt])
                for a in range(TOKB):
                    last = pe.matmul(bank[SPREAD_BANK[m]][:, a * P:(a + 1) * P], hot2[tt][m][:, a, :],
                                     hot1[tt][m][:, a, :], start=True, stop=True)
                last.then_inc(spread_mm[tt], 1)

            for tt in range(TT):
                transpose_slots(tt)
                for m in range(HOTS[tt]):
                    spread_group(tt, 0, m, True)
                with pe.Fori(1, SPREADS // HOTS[tt]) as i:
                    for m in range(HOTS[tt]):
                        spread_group(tt, i, m, False)

            def v_products(i, first=False, final=False):
                for r in range(VRING):
                    c = VRING * i + r
                    pe.wait_ge(clo_ready, c + 1)
                    for b in range(VBLK):
                        pe.wait_ge(vlo_ready, VBLK * c + b + 1)
                        for tt in range(TT):
                            hi, lo = chi[r % 2][:, tt, :], clo[r % 2][:, tt, :]
                            for n, (x1, x2) in enumerate(((hi, vhi[b]), (hi, vlo[b]), (lo, vhi[b]))):
                                last = pe.matmul(bank[tt * VBLK + b][:, :], x1, x2[:, :],
                                                 start=first and r == 0 and n == 0,
                                                 stop=final and r == VRING - 1 and n == 2, skip_group_check=True)
                        last.then_inc(v_mm, 1)

            pe.wait_ge(spread_sb[1], SPREADS)
            v_products(0, first=True)
            with pe.Fori(1, TURNS - 1) as i:
                v_products(i)
            v_products(TURNS - 1, final=True)
            transposes("ple")
            pe.wait_ge(tr_lo["ple"], 8)
            run("gate")


NAMES = ["x", "p", "ln_mix", "w_in", "cmp_wk", "cmp_wv", "cmp_pos", "out_norm", "w_out", "rel_bias", "ln_ffn",
         "peer_wq", "peer_keys", "peer_u", "peer_v", "ln_ple", "ple_gate", "ple_proj", "ln_final"]


def kernel(**inputs):
    import concourse.bacc as bacc
    from concourse.bass_utils import run_bass_kernel_spmd as run

    nc = bacc.Bacc("TRN2", target_bir_lowering=False, num_devices=1)
    arrays, args = {}, []
    for name in NAMES:
        a = np.ascontiguousarray(inputs[name])
        arrays[f"{name}_dram"] = a
        args.append(nc.dram_tensor(f"{name}_dram", a.shape, mybir.dt.from_np(a.dtype), kind="ExternalInput").ap())
    arrays["table_dram"] = bias_table()
    args.append(nc.dram_tensor("table_dram", arrays["table_dram"].shape, mybir.dt.float32, kind="ExternalInput").ap())
    args.append(nc.dram_tensor("out_dram", (1, SEQ, D), mybir.dt.float32, kind="ExternalOutput").ap())
    build(nc, *args)
    r = run(nc, [arrays], core_ids=[0])
    return r.results[0]["out_dram"]
```
